# Optimizing a Trainium2 kernel written in Bass

```python
import jax, jax.numpy as jnp
from jax import lax
import numpy as np

D_MODEL = 1024
BATCH = 1
SEQ = 512
DEPTH = 2
DEC_BATCH = 8
DEC_SEQ = 4
PAST_LEN = 4096
PAGE_SIZE = 128

MIX_WIDTH = D_MODEL
H_GLA = 4
DV_GLA = (MIX_WIDTH // 2) // H_GLA
DK_GLA = DV_GLA // 2
GATE_RANK = 16
GATE_TEMP = 16.0
H_RET = 4
DK_RET = (MIX_WIDTH // 2) // H_RET
DV_RET = DK_RET
D_FF = ((8 * D_MODEL // 3 + 127) // 128) * 128
CHUNK = 64
ROPE_BASE = 10000.0
EPS = 1e-6
PROJ_SIZES = (H_GLA * DK_GLA, H_GLA * DK_GLA, H_GLA * DV_GLA, H_GLA * DV_GLA, GATE_RANK,
              H_RET * DK_RET, H_RET * DK_RET, H_RET * DV_RET, H_RET * DV_RET)
PROJ_COLS = sum(PROJ_SIZES)

kernel_name = "hymba_gla_retnet_macaron_step"

def rmsnorm(x, g):
    xf = x.astype(jnp.float32)
    y = xf * lax.rsqrt(jnp.mean(xf * xf, axis=-1, keepdims=True) + EPS)
    return (y * g.astype(jnp.float32)).astype(x.dtype)

def swiglu(x, w_gu, w_down):
    gate, up = jnp.split(x @ w_gu, 2, axis=-1)
    return (jax.nn.silu(gate) * up) @ w_down

def head_rmsnorm(o, g, dtype):
    B, T, H, dv = o.shape
    y = o * lax.rsqrt(jnp.mean(o * o, axis=-1, keepdims=True) + EPS)
    return (y.reshape(B, T, H * dv) * g.astype(jnp.float32)).astype(dtype)

def rotary(x, pos):
    half = x.shape[-1] // 2
    inv_freq = ROPE_BASE ** (-jnp.arange(half, dtype=jnp.float32) / half)
    ang = pos[:, None] * inv_freq[None, :]
    cos = jnp.cos(ang)[None, :, None, :]
    sin = jnp.sin(ang)[None, :, None, :]
    x1, x2 = x[..., :half], x[..., half:]
    return jnp.concatenate([x1 * cos - x2 * sin, x1 * sin + x2 * cos], axis=-1)

def to_chunks(x):
    B, T, H, d = x.shape
    n = -(-T // CHUNK)
    x = jnp.pad(x, ((0, 0), (0, n * CHUNK - T), (0, 0), (0, 0)))
    return x.reshape(B, n, CHUNK, H, d).transpose(1, 0, 3, 2, 4)

def from_chunks(o, T):
    n, B, H, C, d = o.shape
    return o.transpose(1, 0, 3, 2, 4).reshape(B, n * C, H, d)[:, :T]

def causal_mask():
    return jnp.tril(jnp.ones((CHUNK, CHUNK), dtype=bool))

def gla_chunk(S, inp):
    q, k, v, lg = inp
    b = jnp.cumsum(lg, axis=2)
    o_inter = jnp.einsum('bhtk,bhkv->bhtv', q * jnp.exp(b), S)
    diff = b[:, :, :, None, :] - b[:, :, None, :, :]
    decay = jnp.exp(jnp.where(causal_mask()[:, :, None], diff, -jnp.inf))
    A = jnp.einsum('bhtk,bhsk,bhtsk->bhts', q, k, decay)
    o = o_inter + jnp.einsum('bhts,bhsv->bhtv', A, v)
    b_last = b[:, :, -1:, :]
    S_new = jnp.exp(b_last[:, :, 0, :])[..., None] * S + jnp.einsum('bhsk,bhsv->bhkv', k * jnp.exp(b_last - b), v)
    return S_new, o

def ret_chunk(S, inp):
    q, k, v, lg = inp
    b = jnp.cumsum(lg[..., 0], axis=2)
    o_inter = jnp.exp(b)[..., None] * jnp.einsum('bhtk,bhkv->bhtv', q, S)
    D = jnp.exp(jnp.where(causal_mask(), b[:, :, :, None] - b[:, :, None, :], -jnp.inf))
    A = jnp.einsum('bhtk,bhsk->bhts', q, k) * D
    o = o_inter + jnp.einsum('bhts,bhsv->bhtv', A, v)
    b_last = b[:, :, -1:]
    S_new = jnp.exp(b_last[:, :, 0])[..., None, None] * S + jnp.einsum('bhsk,bhsv->bhkv', k * jnp.exp(b_last - b)[..., None], v)
    return S_new, o

def chunked_scan(step, S0, q, k, v, lg):
    T = q.shape[1]
    xs = tuple(to_chunks(a.astype(jnp.float32)) for a in (q, k, v, lg))
    S, o = lax.scan(step, S0.astype(jnp.float32), xs)
    return from_chunks(o, T), S

def mixer(h, pos, w_in, w_a2, b_a, gn_gla, gn_ret, w_out, s_gla, s_ret):
    B, T, _ = h.shape
    proj = h @ w_in
    offs, acc = [], 0
    for s in PROJ_SIZES[:-1]:
        acc += s
        offs.append(acc)
    q_a, k_a, v_a, g_a, a_lo, q_r, k_r, v_r, g_r = jnp.split(proj, offs, axis=-1)
    qa = q_a.reshape(B, T, H_GLA, DK_GLA) * (DK_GLA ** -0.5)
    ka = k_a.reshape(B, T, H_GLA, DK_GLA)
    va = v_a.reshape(B, T, H_GLA, DV_GLA)
    lg_a = jax.nn.log_sigmoid((a_lo @ w_a2 + b_a).astype(jnp.float32)).reshape(B, T, H_GLA, DK_GLA) / GATE_TEMP
    o_a, S_a = chunked_scan(gla_chunk, s_gla, qa, ka, va, lg_a)
    o_a = head_rmsnorm(o_a, gn_gla, h.dtype) * jax.nn.silu(g_a)
    qr = rotary(q_r.reshape(B, T, H_RET, DK_RET).astype(jnp.float32), pos)
    kr = rotary(k_r.reshape(B, T, H_RET, DK_RET).astype(jnp.float32), pos) * (DK_RET ** -0.5)
    vr = v_r.reshape(B, T, H_RET, DV_RET)
    log_gamma = jnp.log1p(-jnp.exp2(-5.0 - jnp.arange(H_RET, dtype=jnp.float32)))
    lg_r = jnp.broadcast_to(log_gamma[None, None, :, None], (B, T, H_RET, 1))
    o_r, S_r = chunked_scan(ret_chunk, s_ret, qr, kr, vr, lg_r)
    o_r = head_rmsnorm(o_r, gn_ret, h.dtype) * jax.nn.silu(g_r)
    out = jnp.concatenate([o_a, o_r], axis=-1) @ w_out
    return out, S_a.astype(s_gla.dtype), S_r.astype(s_ret.dtype)

def trunk(x, pos, s_gla, s_ret, norm_g, w1_gu, w1_down, w2_gu, w2_down,
          w_in, w_a2, b_a, gn_gla, gn_ret, w_out):
    new_gla, new_ret = [], []
    for l in range(DEPTH):
        n = norm_g[l]
        x = x + 0.5 * rmsnorm(swiglu(rmsnorm(x, n[0]), w1_gu[l], w1_down[l]), n[1])
        m, S_a, S_r = mixer(rmsnorm(x, n[2]), pos, w_in[l], w_a2[l], b_a[l], gn_gla[l], gn_ret[l], w_out[l],
                            s_gla[l], s_ret[l])
        x = x + rmsnorm(m, n[3])
        x = x + 0.5 * rmsnorm(swiglu(rmsnorm(x, n[4]), w2_gu[l], w2_down[l]), n[5])
        new_gla.append(S_a)
        new_ret.append(S_r)
    return x, jnp.stack(new_gla), jnp.stack(new_ret)

def setup_inputs(seed: int = 0) -> dict:
    key = jax.random.key(seed)
    ks = jax.random.split(key, 16)
    f = jnp.float32
    nrm = lambda k, shape, s: jax.random.normal(k, shape, f) * s
    return {
        "x_prompt": nrm(ks[0], (BATCH, SEQ, D_MODEL), 1.0),
        "x_sample": nrm(ks[1], (DEC_BATCH, DEC_SEQ, D_MODEL), 1.0),
        "state_gla": nrm(ks[2], (DEPTH, DEC_BATCH, H_GLA, DK_GLA, DV_GLA), 2.0),
        "state_ret": nrm(ks[3], (DEPTH, DEC_BATCH, H_RET, DK_RET, DV_RET), 2.0),
        "norm_g": 1.0 + nrm(ks[4], (DEPTH, 6, D_MODEL), 0.05),
        "w1_gu": nrm(ks[5], (DEPTH, D_MODEL, 2 * D_FF), D_MODEL ** -0.5),
        "w1_down": nrm(ks[6], (DEPTH, D_FF, D_MODEL), D_FF ** -0.5),
        "w2_gu": nrm(ks[7], (DEPTH, D_MODEL, 2 * D_FF), D_MODEL ** -0.5),
        "w2_down": nrm(ks[8], (DEPTH, D_FF, D_MODEL), D_FF ** -0.5),
        "w_in": nrm(ks[9], (DEPTH, D_MODEL, PROJ_COLS), D_MODEL ** -0.5),
        "w_a2": nrm(ks[10], (DEPTH, GATE_RANK, H_GLA * DK_GLA), GATE_RANK ** -0.5),
        "b_a": nrm(ks[11], (DEPTH, H_GLA * DK_GLA), 0.1),
        "gn_gla": 1.0 + nrm(ks[12], (DEPTH, H_GLA * DV_GLA), 0.05),
        "gn_ret": 1.0 + nrm(ks[13], (DEPTH, H_RET * DV_RET), 0.05),
        "w_out": nrm(ks[14], (DEPTH, MIX_WIDTH, D_MODEL), MIX_WIDTH ** -0.5),
    }

def reference(x_prompt, x_sample, state_gla, state_ret, norm_g, w1_gu, w1_down, w2_gu, w2_down,
              w_in, w_a2, b_a, gn_gla, gn_ret, w_out):
    params = (norm_g, w1_gu, w1_down, w2_gu, w2_down, w_in, w_a2, b_a, gn_gla, gn_ret, w_out)
    B, T, _ = x_prompt.shape
    zero_gla = jnp.zeros((DEPTH, B, H_GLA, DK_GLA, DV_GLA), x_prompt.dtype)
    zero_ret = jnp.zeros((DEPTH, B, H_RET, DK_RET, DV_RET), x_prompt.dtype)
    pos_p = jnp.arange(T, dtype=jnp.float32)
    y_prompt, gla_p, ret_p = trunk(x_prompt, pos_p, zero_gla, zero_ret, *params)
    Ts = x_sample.shape[1]
    pos_s = PAST_LEN + jnp.arange(Ts, dtype=jnp.float32)
    y_sample, gla_s, ret_s = trunk(x_sample, pos_s, state_gla, state_ret, *params)
    return (y_prompt, y_sample, gla_p, ret_p, gla_s, ret_s)


_drawn_inputs = setup_inputs


def setup_inputs(seed=0):
    import zlib

    import numpy as np

    out = dict(_drawn_inputs(seed))
    spreads = {}
    factors = {}
    for name, (base, spread) in spreads.items():
        noise = np.random.default_rng([zlib.crc32(name.encode()), seed]).standard_normal(out[name].shape)
        drawn = base * np.exp(spread * noise) if base else spread * noise
        out[name] = __import__('jax').numpy.asarray(drawn.astype(out[name].dtype))
    for name, factor in factors.items():
        out[name] = (out[name] * factor).astype(out[name].dtype)
    return out
```

```python
from contextlib import ExitStack

import concourse.bass as bass
from concourse import mybir

F32 = mybir.dt.float32
F32R = mybir.dt.float32r
U8 = mybir.dt.uint8
ALU = mybir.AluOpType
ACT = mybir.ActivationFunctionType
AX = mybir.AxisListType

P = 128
EPS = 1e-6
GATE_TEMP = 16.0
SPLIT_SLOTS = 2
UNITS = 4
UNIT_KT = 8
CH = 128
LEVELS = (64, 32, 16, 8, 4, 2, 1)


class Signal:

    def __init__(self, sem, per_layer):
        self.sem, self.per = sem, per_layer

    def at(self, l, i):
        return l * self.per + (i + 1)


def const_layout(HR, T, TS, NS, NV):
    cols, at = {}, 0
    for name, n in (("ident", P), ("ones", P), ("cos", T), ("sin", T), ("decay_mask", HR * CH),
                    ("q_decay", HR * CH), ("k_decay", HR), ("k_decay_s", HR), ("decay_mask_s", HR * TS),
                    ("scan_keep", T), ("batch_mask", NS), ("eps", 1)):
        cols[name] = (at, at + n)
        at += n
    return cols, at


def trunk_kernel(nc, x_prompt, x_sample, state_gla, state_ret, norm_g, w1_gu, w1_down, w2_gu, w2_down,
                 w_in, w_a2, b_a, gn_gla, gn_ret, w_out, consts, masks,
                 y_prompt, y_sample, gla_p, ret_p, gla_s, ret_s, gammas):
    DEPTH, NS, HG, DKG, DV = state_gla.shape
    HR, DKR = state_ret.shape[2:4]
    TP, D = x_prompt.shape[1:]
    DS = x_sample.shape[1]
    TS = NS * DS
    T = TP + TS
    HALF = T // 2
    KD = D // P
    FF = w1_down.shape[1]
    KF = FF // P
    GR = w_a2.shape[1]
    NCH = TP // CH
    HA = HG + HR
    QT = HG * DKG // P
    NN = norm_g.shape[1]
    DOWN_KT = [(KF + UNITS - 1 - u) // UNITS for u in range(UNITS)]
    ALO_KT = [KD // UNITS] * UNITS
    FULL_KT = [KD] * UNITS
    cc, _ = const_layout(HR, T, TS, NS, 0)
    V_GLA = DEPTH * NN * KD
    V_RET = V_GLA + DEPTH * HG
    V_BA = V_RET + DEPTH * HR
    NV = V_BA + DEPTH * QT

    GLA_V = 2 * HG * DKG
    GLA_G = GLA_V + HG * DV
    A_LO = GLA_G + HG * DV
    RET_Q = A_LO + GR
    RET_K = RET_Q + HR * DKR
    RET_V = RET_K + HR * DKR
    RET_G = RET_V + HR * DV
    IN_GROUPS = (("qk_a", 0), ("v_a", GLA_V), ("q_r", RET_Q), ("k_r", RET_K), ("v_r", RET_V),
                 ("g_a", GLA_G), ("g_r", RET_G))
    NIN = 1 + UNITS * len(IN_GROUPS)
    UP_GROUPS, DOWN_GROUPS, OUT_GROUPS = KF // 2, KD, KD // UNITS
    UP = (0, UP_GROUPS + DOWN_GROUPS + 1 + len(IN_GROUPS) + OUT_GROUPS)
    DOWN = (UP[0] + UP_GROUPS, UP[1] + UP_GROUPS)
    WIN = DOWN[0] + DOWN_GROUPS
    WOUT = WIN + 1 + len(IN_GROUPS)
    GROUPS = DOWN[1] + DOWN_GROUPS
    NL = len(LEVELS)
    SCAN_SLOT = 5
    STEPS = ["q", "k"] + list(range(NL))
    DIFF_SLOT = {6 + 2 * j: s for j, s in enumerate(STEPS)}
    PROD_SLOT = {8 + 2 * j: s for j, s in enumerate(STEPS)}
    SCORE_SLOT = {13 + 2 * n: n for n in range(NL)}
    TAKE_SLOT = {14 + 2 * n: n for n in range(NL)}
    SCORE_SLOT.update({26: NL, 27: NL + 1})
    TAKE_SLOT.update({27: NL, 28: NL + 1})
    ROT0 = 1 + 2 * UNITS

    with ExitStack() as ctx:
        def sb(name, shape, dt=F32):
            return ctx.enter_context(nc.sbuf_tensor(name, shape, dt))

        def sem(name):
            return ctx.enter_context(nc.semaphore(name))

        def sig(name, per_layer):
            return Signal(sem(name), per_layer)

        def overlay(*tensors):
            out = []
            with ExitStack() as place:
                for name, shape, dt in tensors:
                    out.append(place.enter_context(nc.sbuf_tensor(name, shape, dt)))
            return out

        x = sb("x", [P, KD, T])
        raw = sb("raw", [P, UNITS, UNIT_KT, P])
        w_hi = sb("w_hi", [P, SPLIT_SLOTS, UNIT_KT, P], F32R)
        w_lo = sb("w_lo", [P, SPLIT_SLOTS, UNIT_KT, P], F32R)
        cst = sb("cst", [P, consts.shape[1]])
        msk = sb("msk", [P, masks.shape[1]], U8)
        rstd_pre = sb("rstd_pre", [P, T])
        acc = sb("acc", [P, T])
        sq = sb("sq", [P, 2, T])
        tmp = sb("tmp", [P, 2, T])
        vecs = sb("vecs", [P, NV])
        half_gain = sb("half_gain", [P, DEPTH * NN * KD])
        chunk_decay = sb("chunk_decay", [P, QT, NCH + NS])
        rms = sb("rms", [P, 2, HA])

        xs_hi, xs_lo = overlay(("xs_hi", [P, KD, T], F32R), ("xs_lo", [P, KD, T], F32R))
        y, = overlay(("y", [P, KD, T], F32))
        v_tok, k_tok, a_ret, q_ret_dec, s_gla, s_ret, o_tok = overlay(
            ("v_tok", [P, HA, P], F32),
            ("k_tok", [P, HR * P + QT * P], F32),
            ("a_ret", [P, HR, CH], F32),
            ("q_ret_dec", [P, HR, CH], F32),
            ("s_gla", [P, 2, QT, DV], F32), ("s_ret", [P, 2, HR, DV], F32),
            ("o_tok", [P, HA, P], F32))
        ret_state, gla_state, v_by_batch, k_tok_s, q_ret_dec_s = overlay(
            ("ret_state", [P, HR, NS, DV], F32), ("gla_state", [P, QT, NS, DV], F32),
            ("v_by_batch", [TS, NS, DV], F32), ("k_tok_s", [TS, HR * P + QT * P], F32),
            ("q_ret_dec_s", [P, HR, TS], F32))
        sb("xs_place", [P, 2 * KD * T])

        h_hi, h_lo = overlay(("h_hi", [P, KF, T], F32R), ("h_lo", [P, KF, T], F32R))
        x_tok, vec_rows, mask_rows = overlay(("x_tok", [P, NCH + 1, D], F32), ("vec_rows", [P, P], F32),
                                             ("mask_rows", [P, masks.shape[1]], F32))
        y_tok, = overlay(("y_tok", [P, NCH + 1, D], F32))
        y_out, = overlay(("y_out", [P, KD, T], F32))
        (qk_a, q_dec, k_dec, v_t, g_t, q_r, k_r, b_cum, e_buf, k_lvl, q_lvl, a_gla, a_gla_s, a_ret_s,
         w_a2_sb) = overlay(
            ("qk_a", [P, 2 * QT, T], F32),
            ("q_dec", [P, QT, T], F32),
            ("k_dec", [P, QT, T], F32),
            ("v_t", [P, HA, T], F32),
            ("g_t", [P, HA, T], F32),
            ("q_r", [P, HR, T], F32), ("k_r", [P, HR, T], F32),
            ("b_cum", [P, QT, T], F32), ("e_buf", [P, QT, T], F32),
            ("k_lvl", [P, QT, T], F32), ("q_lvl", [P, QT, HALF], F32),
            ("a_gla", [P, 2, NCH, 2, CH], F32),
            ("a_gla_s", [TS, 2, 2, TS], F32), ("a_ret_s", [TS, HR, TS], F32),
            ("w_a2_sb", [GR, QT * P], F32))
        sb("h_place", [P, 2 * KF * T])
        v_tok_s = k_lvl[0:TS, :, :].rearrange("p q t -> p (q t)")[:, 0:HA * P].rearrange("p (h v) -> p h v", h=HA)

        ps = ctx.enter_context(nc.psum_tensor("ps", [P, 8, 512], F32))

        def pair(i):
            return ps[:, 2 * i:2 * i + 2, 0:HALF]

        def halves(ap):
            return ap.rearrange("p (a t) -> p a t", a=2)

        def c(name, parts=P):
            a, b = cc[name]
            return cst[0:parts, a:b]

        ident, ones, eps = c("ident"), c("ones"), c("eps")
        cos, sin = c("cos"), c("sin")

        def gain(l, n, k):
            return vecs[:, bass.ds(l * (NN * KD) + (n * KD + k), 1)]

        def post_gain(l, q, k):
            table = vecs if q == 1 else half_gain
            return table[:, bass.ds(l * (NN * KD) + ((2 * q + 1) * KD + k), 1)]

        loaded, vec_turned, vec_ready = sem("loaded"), sem("vec_turned"), sem("vec_ready")
        raw_ready = [sem(f"raw_ready{i}") for i in range(UNITS)]
        units_issued = sem("units_issued")
        hi_split = sem("hi_split")
        split_ready = [sem(f"split_ready{i}") for i in range(SPLIT_SLOTS)]
        split_used = [sem(f"split_used{i}") for i in range(SPLIT_SLOTS)]
        x_turned, x_copied = sem("x_turned"), sem("x_copied")
        w_a2_loaded = sem("w_a2_loaded")
        xh_ready, xs_ready = sig("xh_ready", 3 * KD), sig("xs_ready", 3 * KD)
        xsq_ready, xsq_used = sig("xsq_ready", 3 * KD), sig("xsq_used", 3 * KD)
        pre_log, pre_ready = sig("pre_log", 3), sig("pre_ready", 3)
        y_read = sig("y_read", 3 * KD)
        acc_step = sig("acc_step", 3 * (KD - 1))
        post_sum, post_log, post_ready = sig("post_sum", 3), sig("post_log", 3), sig("post_ready", 3)
        y_scaled, x_ready = sig("y_scaled", 3 * KD), sig("x_ready", 3 * KD)
        gate_scaled, up_scaled = sig("gate_scaled", 2 * KF), sig("up_scaled", 2 * KF)
        gate_silu, h_prod = sig("gate_silu", 2 * KF), sig("h_prod", 2 * KF)
        hh_ready, h_ready = sig("hh_ready", 2 * KF), sig("h_ready", 2 * KF)
        in_read = sig("in_read", NIN)
        z_ready, z_abs, z_min = sig("z_ready", 1), sig("z_abs", 1), sig("z_min", 1)
        z_exp, z_ln, log_gate, b_ready = sig("z_exp", 1), sig("z_ln", 1), sig("log_gate", 1), sig("b_ready", 1)
        swapped, rot_parts, rotated = sig("swapped", 2 * HR), sig("rot_parts", 2 * HR), sig("rotated", 2 * HR)
        silu_done, gates_ready = sig("silu_done", 2), sig("gates_ready", 1)
        diff_ready, exp_ready, prod_ready = sig("diff_ready", NL + 1), sig("exp_ready", NL + 2), sig("prod_ready", NL + 2)
        scores_ready, scores_taken, a_zeroed = sig("scores_ready", NL + 2), sig("scores_taken", NL + 2), sig("a_zeroed", 1)
        NSTEP = NCH + 1
        turned, v_tok_ready, k_tok_ready = sig("turned", NSTEP), sig("v_tok_ready", NSTEP), sig("k_tok_ready", NSTEP)
        qd_ready = sig("qd_ready", NCH)
        ret_scores, a_ret_ready = sig("ret_scores", NSTEP), sig("a_ret_ready", NSTEP)
        state_delta, state_ready = sig("state_delta", NCH), sig("state_ready", NCH)
        o_ready, o_sq, o_ms = sig("o_ready", NSTEP), sig("o_sq", NSTEP), sig("o_ms", NSTEP)
        o_root, o_rms, o_normed = sig("o_root", NSTEP), sig("o_rms", NSTEP), sig("o_normed", NSTEP)
        o_turned, o_gated = sig("o_turned", NCH), sig("o_gated", NSTEP)
        v_masked, s_delta, s_updated = sig("v_masked", HA), sig("s_delta", HA), sig("s_updated", HA)
        states_stored, states_loaded = sem("states_stored"), sem("states_loaded")
        oh_ready, ol_ready = sig("oh_ready", HA), sig("ol_ready", HA)
        y_turned, y_copied, stored = sem("y_turned"), sem("y_copied"), sem("stored")

        block = ctx.enter_context(nc.Block())

        def out_slot(h):
            return (h % 2, h // 2) if h < HG else ((h - HG) // 2, 2 + (h - HG) % 2)

        def wait(eng, signal, l, i):
            eng.wait_ge(signal.sem, signal.at(l, i))

        def wait_unit(eng, g, u):
            eng.wait_ge(split_used[u % SPLIT_SLOTS], 2 * g + (u // SPLIT_SLOTS + 2))

        def wait_in_tile(eng, l, t):
            j, u = ((t - 1) // UNITS + 1, (t - 1) % UNITS) if t else (0, UNITS - 1)
            wait_unit(eng, l * GROUPS + (WIN + j), u)

        def ahead_of_wait(eng):
            eng.wait_ge(loaded, LOADS)

        X0 = KD + 1
        STATE_DMAS = (2 + QT + HR) * 16
        STATE_LOADS = (QT + HR) * 16
        LOADS = 8 * 16

        @block.sync
        def _(sp):
            sp.dma_start(cst[:, :], consts).then_inc(loaded, 16)
            sp.dma_start(mask_rows[:, :], masks).then_inc(loaded, 16)
            sp.dma_start(x_tok[:, 0:NCH, :], x_prompt[0].rearrange("(c p) d -> p c d", p=P)).then_inc(loaded, 16)
            sp.dma_start(x_tok[0:TS, NCH, :], x_sample.rearrange("b t d -> (b t) d")).then_inc(loaded, 16)
            for row, v in ((0, norm_g.rearrange("l n (k p) -> (l n k) p", p=P)),
                           (V_GLA, gn_gla.rearrange("l (k p) -> (l k) p", p=P)),
                           (V_RET, gn_ret.rearrange("l (k p) -> (l k) p", p=P)),
                           (V_BA, b_a.rearrange("l (k p) -> (l k) p", p=P))):
                sp.dma_start(vec_rows[row:row + v.shape[0], :], v).then_inc(loaded, 16)

            def unit(g, u, rows, kt):
                sp.wait_ge(split_ready[u % SPLIT_SLOTS], 2 * g + (u // SPLIT_SLOTS + 1))
                sp.sem_inc(units_issued, 1)
                sp.dma_start(raw[:, u, 0:kt, :], rows.rearrange("(k p) m -> p k m", p=P)).then_inc(raw_ready[u], 16)

            def k_parts(g, w, l, cols, kts):
                k0 = 0
                for u in range(UNITS):
                    unit(g, u, w[l, k0 * P:(k0 + kts[u]) * P, cols], kts[u])
                    k0 += kts[u]

            def ffn(l, f, w_gu, w_down):
                with sp.Fori(0, UP_GROUPS) as i:
                    for u in range(UNITS):
                        unit(l * GROUPS + UP[f] + i, u, w_gu[l, :, bass.ds(i * (2 * P) + (u // 2 * P + u % 2 * FF), P)], KD)
                with sp.Fori(0, DOWN_GROUPS) as m:
                    k_parts(l * GROUPS + DOWN[f] + m, w_down, l, bass.ds(m * P, P), DOWN_KT)

            with sp.Fori(0, DEPTH) as l:
                ffn(l, 0, w1_gu, w1_down)
                k_parts(l * GROUPS + WIN, w_in, l, slice(A_LO, A_LO + P), ALO_KT)
                for j, (_, col) in enumerate(IN_GROUPS):
                    for u in range(UNITS):
                        unit(l * GROUPS + (WIN + 1 + j), u, w_in[l, :, col + u * P:col + (u + 1) * P], KD)
                with sp.Fori(0, OUT_GROUPS) as j:
                    for u in range(UNITS):
                        unit(l * GROUPS + WOUT + j, u, w_out[l, :, bass.ds(j * (UNITS * P) + u * P, P)], KD)
                ffn(l, 1, w2_gu, w2_down)

        @block.gpsimd
        def _(pool):
            for s in range(SPLIT_SLOTS):
                pool.sem_inc(split_ready[s], 2)
            pool.wait_ge(loaded, LOADS)

            def group(g, kts):
                for u in range(UNITS):
                    s, kt = u % SPLIT_SLOTS, kts[u]
                    pool.wait_ge(raw_ready[u], g * 16 + 16)
                    pool.wait_ge(split_used[s], 2 * g + (u // SPLIT_SLOTS + 1))
                    pool.tensor_tensor(w_hi[:, s, 0:kt, :], raw[:, u, 0:kt, :],
                                       ones.rearrange("p (k m) -> p k m", k=1).broadcast_to([P, kt, P]),
                                       ALU.mult).then_inc(hi_split, 1)
                    pool.wait_ge(hi_split, g * UNITS + (u + 1))
                    pool.tensor_tensor(w_lo[:, s, 0:kt, :], raw[:, u, 0:kt, :], w_hi[:, s, 0:kt, :].bitcast(F32),
                                       ALU.subtract).then_inc(split_ready[s], 1)

            with pool.Fori(0, DEPTH) as l:
                for f in range(2):
                    with pool.Fori(0, UP_GROUPS) as i:
                        group(l * GROUPS + UP[f] + i, FULL_KT)
                    with pool.Fori(0, DOWN_GROUPS) as i:
                        group(l * GROUPS + DOWN[f] + i, DOWN_KT)
                    if f == 0:
                        group(l * GROUPS + WIN, ALO_KT)
                        with pool.Fori(0, len(IN_GROUPS) + OUT_GROUPS) as i:
                            group(l * GROUPS + (WIN + 1) + i, FULL_KT)

        @block.tensor
        def _(pe):
            for s in range(SPLIT_SLOTS):
                pe.sem_inc(split_used[s], 1)

            def unit(g, u, kt, hi, lo, k0, bank, first, last, before_k=None, after_k=None):
                s = u % SPLIT_SLOTS
                pe.wait_ge(split_ready[s], 2 * g + (u // SPLIT_SLOTS + 3))
                for k in range(kt):
                    if before_k:
                        before_k(k0 + k)
                    for n, (w, v) in enumerate(((w_hi, hi), (w_hi, lo), (w_lo, hi))):
                        for a in range(2):
                            mm = pe.matmul(ps[:, bank + a, 0:HALF], w[:, s, k, :], v[:, k0 + k, a * HALF:(a + 1) * HALF],
                                           start=(first and k == 0 and n == 0), stop=(last and k == kt - 1 and n == 2))
                    if k == kt - 1:
                        mm.then_inc(split_used[s], 1)
                    if after_k:
                        after_k(k0 + k)

            def stats(l, q):
                def add(k):
                    wait(pe, xsq_ready, l, q * KD + k)
                    for a in range(2):
                        mm = pe.matmul(ps[:, 6 + a, 0:HALF], ones, tmp[:, k % 2, a * HALF:(a + 1) * HALF],
                                       start=(k == 0), stop=(k == KD - 1))
                    mm.then_inc(xsq_used.sem, 1)
                return add

            def x_split(l, q):
                return lambda k: wait(pe, xs_ready, l, q * KD + k)

            def up_chunk(l, f, g, par, first=False):
                for j in range(2):
                    peeled = first and j == 0
                    unit(g, 2 * par + j, KD, xs_hi, xs_lo, 0, 4 * par + 2 * j, True, True,
                         before_k=x_split(l, 2 * f) if peeled else None, after_k=stats(l, 2 * f) if peeled else None)

            def ffn(l, f):
                g0 = l * GROUPS + UP[f]
                up_chunk(l, f, g0, 0, first=True)
                wait(pe, pre_log, l, 2 * f)
                up_chunk(l, f, g0, 1)
                with pe.Fori(1, UP_GROUPS) as i:
                    for par in range(2):
                        pe.wait_ge(up_scaled.sem, l * up_scaled.per + i * 2 + (f * KF + par - 1))
                        up_chunk(l, f, g0 + i, par)
                wait(pe, up_scaled, l, f * KF + KF - 2)

                def down_tile(m, par, before_k=None):
                    k0 = 0
                    for u in range(UNITS):
                        unit(l * GROUPS + DOWN[f] + m, u, DOWN_KT[u], h_hi, h_lo, k0, 2 * par, u == 0, u == UNITS - 1,
                             before_k=before_k)
                        k0 += DOWN_KT[u]

                down_tile(0, 0, before_k=lambda k: wait(pe, h_ready, l, f * KF + k))
                down_tile(1, 1)
                with pe.Fori(1, DOWN_GROUPS // 2) as i:
                    for par in range(2):
                        pe.wait_ge(y_read.sem, l * y_read.per + i * 2 + (2 * f * KD + par - 1))
                        down_tile(i * 2 + par, par)
                post_stats(l, 2 * f)

            def post_stats(l, q):
                wait(pe, acc_step, l, q * (KD - 1) + KD - 2)
                for a in range(2):
                    mm = pe.matmul(ps[:, 4 + a, 0:HALF], ones, acc[:, a * HALF:(a + 1) * HALF], start=True, stop=True)
                mm.then_inc(post_sum.sem, 1)

            def in_tile(l, t):
                j, u = (t - 1) // UNITS, (t - 1) % UNITS
                if t >= 2:
                    wait(pe, in_read, l, t - 2)
                unit(l * GROUPS + (WIN + 1 + j), u, KD, xs_hi, xs_lo, 0, 2 * (t % 2), True, True)

            def gate_logits(l):
                wait(pe, in_read, l, 0)
                pe.wait_ge(w_a2_loaded, l * 16 + 16)
                wait(pe, pre_log, l, 1)
                for q in range(QT):
                    for a in range(2):
                        mm = pe.matmul(ps[:, 4 + 2 * q + a, 0:HALF], w_a2_sb[:, q * P:(q + 1) * P],
                                       tmp[0:GR, 0, a * HALF:(a + 1) * HALF], start=True, stop=True)
                mm.then_inc(z_ready.sem, 1)

            def level_scores(l, n):
                m = LEVELS[n]
                wait(pe, prod_ready, l, 2 + n)
                if n == 0:
                    wait(pe, z_min, l, 0)
                if n >= 2:
                    wait(pe, scores_taken, l, n - 1 if LEVELS[n - 1] < DS else n - 2)
                for p in range(2):
                    for c_ in range(NCH):
                        for hh in range(2):
                            at = (c_ * 2 + hh) * (CH // 2)
                            mm = pe.matmul(ps[:, 4 + 2 * (n % 2) + p, at:at + CH // 2],
                                           k_lvl[p * DKG:(p + 1) * DKG, hh, c_ * CH:(c_ + 1) * CH],
                                           q_lvl[p * DKG:(p + 1) * DKG, hh, c_ * CH // 2:(c_ + 1) * CH // 2],
                                           start=True, stop=True)
                if m < DS:
                    ahead_of_wait(pe)
                    wait(pe, scores_taken, l, n - 1)
                    for p in range(2):
                        for hh in range(2):
                            mm = pe.matmul(ps[0:TS, 4 + 2 * ((n + 1) % 2) + p, hh * TS:hh * TS + TS // 2],
                                           k_lvl[p * DKG:(p + 1) * DKG, hh, TP:T],
                                           q_lvl[p * DKG:(p + 1) * DKG, hh, TP // 2:HALF], start=True, stop=True)
                mm.then_inc(scores_ready.sem, 1)

            def diagonal_scores(l, sample):
                ahead_of_wait(pe)
                wait(pe, scores_taken, l, NL if sample else NL - 1)
                for p in range(2):
                    for c_ in ([NCH] if sample else range(NCH)):
                        n = TS if sample else CH
                        for hh in range(2):
                            at = (c_ % 2 * 2 + hh) * CH
                            mm = pe.matmul(ps[0:n, 4 + 2 * p + (0 if sample else c_ // 2), at:at + n],
                                           qk_a[p * DKG:(p + 1) * DKG, QT + hh, c_ * CH:c_ * CH + n],
                                           qk_a[p * DKG:(p + 1) * DKG, hh, c_ * CH:c_ * CH + n], start=True, stop=True)
                mm.then_inc(scores_ready.sem, 1)

            def turn(l, c_, n):
                t0 = c_ * CH
                if c_ == 0:
                    wait(pe, in_read, l, NIN - 1)
                    wait(pe, rotated, l, 2 * HR - 1)
                else:
                    wait(pe, v_tok_ready, l, c_ - 1)
                    wait(pe, k_tok_ready, l, c_ - 1)
                    wait(pe, state_ready, l, c_ - 1)
                for h in range(HA):
                    pe.transpose(ps[0:n, h // 4, h % 4 * P:(h % 4 + 1) * P], v_t[:, h, t0:t0 + n], ident)
                for h in range(HR):
                    pe.transpose(ps[0:n, 2, h * P:(h + 1) * P], k_r[:, h, t0:t0 + n], ident)
                for q in range(QT):
                    mm = pe.transpose(ps[0:n, 3, q * P:(q + 1) * P], k_dec[:, q, t0:t0 + n], ident)
                mm.then_inc(turned.sem, 1)

            def out_turn(l, c_):
                wait(pe, o_normed, l, c_)
                wait(pe, state_ready, l, c_)
                for h in range(HA):
                    a, i = out_slot(h)
                    mm = pe.transpose(ps[:, 4 + h // 4, h % 4 * P:(h % 4 + 1) * P], o_tok[:, 4 * a + i, :], ident)
                mm.then_inc(o_turned.sem, 1)

            def retention_scores(l, c_, n):
                t0 = c_ * CH
                if c_ == 0:
                    wait(pe, scores_taken, l, NL + 1)
                else:
                    wait(pe, o_gated, l, c_ - 1)
                for h in range(HR):
                    mm = pe.matmul(ps[0:n, 4, h * n:(h + 1) * n], k_r[:, h, t0:t0 + n], q_r[:, h, t0:t0 + n],
                                   start=True, stop=True)
                mm.then_inc(ret_scores.sem, 1)

            def chunk(l, c_):
                t0 = c_ * CH
                turn(l, c_, CH)
                if c_:
                    out_turn(l, c_ - 1)
                retention_scores(l, c_, CH)
                wait(pe, v_tok_ready, l, c_)
                wait(pe, k_tok_ready, l, c_)
                for h in range(HR):
                    pe.matmul(ps[:, 5, h * DV:(h + 1) * DV], k_tok[:, h * P:(h + 1) * P], v_tok[:, HG + h, :],
                              start=True, stop=True)
                for h in range(HG):
                    q, p = h // 2, h % 2
                    at = (HR + q) * P + p * DKG
                    mm = pe.matmul(ps[p * DKG:(p + 1) * DKG, 3, (QT + q) * DV:(QT + q + 1) * DV],
                                   k_tok[:, at:at + DKG], v_tok[:, h, :], start=True, stop=True)
                mm.then_inc(state_delta.sem, 1)
                wait(pe, a_ret_ready, l, c_)
                if c_ == 0:
                    wait(pe, scores_taken, l, NL + 1)
                else:
                    wait(pe, o_normed, l, c_ - 1)
                    wait(pe, state_ready, l, c_ - 1)
                    wait(pe, qd_ready, l, c_ - 1)
                for h in range(HG):
                    q, p = h // 2, h % 2
                    a, i = out_slot(h)
                    o = ps[:, 6 + a, i * DV:(i + 1) * DV]
                    pe.matmul(o, a_gla[:, p, c_, q, :], v_tok[:, h, :], start=True, stop=(c_ == 0))
                    if c_:
                        pe.matmul(o, q_dec[p * DKG:(p + 1) * DKG, q, t0:t0 + CH],
                                  s_gla[p * DKG:(p + 1) * DKG, (c_ - 1) % 2, q, :], start=False, stop=True)
                for h in range(HR):
                    a, i = out_slot(HG + h)
                    o = ps[:, 6 + a, i * DV:(i + 1) * DV]
                    mm = pe.matmul(o, a_ret[:, h, :], v_tok[:, HG + h, :], start=True, stop=(c_ == 0))
                    if c_:
                        mm = pe.matmul(o, q_ret_dec[:, h, :], s_ret[:, (c_ - 1) % 2, h, :], start=False, stop=True)
                mm.then_inc(o_ready.sem, 1)

            def sample(l):
                turn(l, NCH, TS)
                out_turn(l, NCH - 1)
                retention_scores(l, NCH, TS)
                wait(pe, v_tok_ready, l, NCH)
                wait(pe, k_tok_ready, l, NCH)
                wait(pe, a_ret_ready, l, NCH)
                wait(pe, qd_ready, l, NCH - 1)
                pe.wait_ge(states_loaded, l * STATE_LOADS + STATE_LOADS)
                for h in range(HA):
                    q, p = h // 2, h % 2
                    bank, at = 6 + out_slot(h)[0], out_slot(h)[1] * TS
                    scores = a_gla_s[:, p, q, :] if h < HG else a_ret_s[:, h - HG, :]
                    pe.matmul(ps[:, bank, at:at + TS], v_tok_s[:, h, :], scores, start=True, stop=False,
                              skip_group_check=True)
                    for b in range(NS):
                        o = ps[:, bank, at + b * DS:at + (b + 1) * DS]
                        if h < HG:
                            state = gla_state[p * DKG:(p + 1) * DKG, q, b, :]
                            queries = q_dec[p * DKG:(p + 1) * DKG, q, TP + b * DS:TP + (b + 1) * DS]
                        else:
                            state = ret_state[:, h - HG, b, :]
                            queries = q_ret_dec_s[:, h - HG, b * DS:(b + 1) * DS]
                        mm = pe.matmul(o, state, queries, start=False, stop=(b == NS - 1), skip_group_check=True)
                mm.then_inc(o_ready.sem, 1)
                wait(pe, o_sq, l, NCH)
                wait(pe, a_ret_ready, l, NCH)
                pe.matmul(ps[:, 4, 0:HA * TS], ones, sq[:, 0, 0:HA * TS], start=True, stop=True).then_inc(o_ms.sem, 1)
                for h in range(HA):
                    wait(pe, v_masked, l, h)
                    if h >= 2:
                        wait(pe, s_updated, l, h - 2)
                    if h < HG:
                        q, p = h // 2, h % 2
                        keys, r0, r1 = k_tok_s[:, HR * P + h * DKG:HR * P + (h + 1) * DKG], p * DKG, (p + 1) * DKG
                    else:
                        keys, r0, r1 = k_tok_s[:, (h - HG) * P:(h - HG + 1) * P], 0, P
                    for a in range(2):
                        mm = pe.matmul(ps[r0:r1, 2 * (h % 2) + a, :], keys,
                                       v_by_batch[:, a * NS // 2:(a + 1) * NS // 2, :], start=True, stop=True)
                    mm.then_inc(s_delta.sem, 1)

            def out_projection(l):
                for m in range(KD):
                    if m >= 2:
                        wait(pe, y_read, l, KD + m - 2)
                    else:
                        wait(pe, s_updated, l, HA - 1)
                    unit(l * GROUPS + (WOUT + m // UNITS), m % UNITS, KD, xs_hi, xs_lo, 0, 2 * (m % 2), True, True,
                         before_k=(lambda k: wait(pe, ol_ready, l, k)) if m == 0 else None)
                post_stats(l, 1)

            pe.wait_ge(loaded, LOADS)
            pe.transpose(ps[:, 5, 0:NV], vec_rows[0:NV, :], ident[0:NV, 0:NV]).then_inc(vec_turned, 1)
            for d in range(KD):
                mm = pe.transpose(ps[:, 4, d * TS:(d + 1) * TS], x_tok[0:TS, NCH, d * P:(d + 1) * P], ident[0:TS, 0:TS])
            mm.then_inc(x_turned, 1)
            for d in range(KD):
                if d >= 4:
                    pe.wait_ge(x_copied, d - 2)
                for c_ in range(NCH):
                    mm = pe.transpose(ps[:, d % 4, c_ * P:(c_ + 1) * P], x_tok[:, c_, d * P:(d + 1) * P], ident)
                mm.then_inc(x_turned, 1)

            with pe.Fori(0, DEPTH) as l:
                ffn(l, 0)
                k0 = 0
                for u in range(UNITS):
                    unit(l * GROUPS + WIN, u, ALO_KT[u], xs_hi, xs_lo, k0, 0, u == 0, u == UNITS - 1,
                         before_k=x_split(l, 1), after_k=stats(l, 1))
                    k0 += ALO_KT[u]
                for t in range(1, NIN):
                    in_tile(l, t)
                    if t == UNITS:
                        gate_logits(l)
                    if t in SCORE_SLOT:
                        n = SCORE_SLOT[t]
                        if n < NL:
                            level_scores(l, n)
                        else:
                            diagonal_scores(l, sample=(n > NL))
                for c_ in range(NCH):
                    chunk(l, c_)
                sample(l)
                out_projection(l)
                ffn(l, 1)

            for c_ in range(NCH + 1):
                n = P if c_ < NCH else TS
                for a in range(2):
                    i = 2 * c_ + a
                    if i == 0:
                        pe.wait_ge(x_ready.sem, X0 + DEPTH * x_ready.per)
                    if i >= 4:
                        pe.wait_ge(y_copied, i - 3)
                    for d in range(4):
                        mm = pe.transpose(ps[0:n, i % 4, d * P:(d + 1) * P], x[:, 4 * a + d, c_ * P:c_ * P + n], ident)
                    mm.then_inc(y_turned, 1)

        @block.scalar
        def _(act):
            def pre_tile(l, q, k, done):
                act.wait_ge(x_ready.sem, done)
                act.activation(xs_hi[:, k, :], x[:, k, :], ACT.Copy, scale=gain(l, 2 * q, k)).then_inc(xh_ready.sem, 1)
                if k >= 2:
                    wait(act, xsq_used, l, q * KD + k - 2)
                act.activation(tmp[:, k % 2, :], x[:, k, :], ACT.Square).then_inc(xsq_ready.sem, 1)

            def inverse_root(l, q, dst, bank_pair, log_sig, ready_sig):
                act.activation(halves(dst), pair(bank_pair), ACT.Ln, bias=eps, scale=1.0 / D).then_inc(log_sig.sem, 1)
                wait(act, log_sig, l, q)
                act.activation(dst, dst, ACT.Exp, scale=-0.5).then_inc(ready_sig.sem, 1)

            def pre_norm(l, q):
                for k in range(KD):
                    pre_tile(l, q, k, l * x_ready.per + (X0 if q == 0 else X0 + (q - 1) * KD + k + 1))
                wait(act, xsq_used, l, q * KD + KD - 1)
                inverse_root(l, q, rstd_pre[:, :], 3, pre_log, pre_ready)

            def up(l, f):
                with act.Fori(0, KF) as c_:
                    at = l * gate_scaled.per + c_ + (f * KF + 1)
                    act.wait_ge(gate_scaled.sem, at)
                    act.activation(tmp[:, 0, :], tmp[:, 0, :], ACT.Silu).then_inc(gate_silu.sem, 1)
                    act.wait_ge(h_prod.sem, at)
                    act.activation(h_hi[:, bass.ds(c_, 1), :], tmp[:, 0:1, :], ACT.Copy).then_inc(hh_ready.sem, 1)

            def post_norm(l, q, g0, last_unit):
                for m in range(KD):
                    wait_unit(act, *last_unit(g0, m))
                    if m >= 2:
                        wait(act, acc_step, l, q * (KD - 1) + max(m - 2, 1) - 1)
                    act.activation(halves((y_out if q == 1 else y)[:, m, :]), pair(m % 2), ACT.Copy)
                    act.activation(halves(sq[:, m % 2, :]), pair(m % 2), ACT.Square).then_inc(y_read.sem, 1)
                wait(act, post_sum, l, q)
                inverse_root(l, q, acc[:, :], 2, post_log, post_ready)

            down_unit = lambda g0, m: (g0 + m, UNITS - 1)
            out_unit = lambda g0, m: (g0 + m // UNITS, m % UNITS)

            def swap_halves(l, t):
                n = t - ROT0
                src, hd = (q_r if n < HR else k_r)[:, n % HR, :], DKR // 2
                wait(act, in_read, l, t)
                if n:
                    wait(act, rotated, l, n - 1)
                act.activation(tmp[0:hd, 1, :], src[hd:2 * hd, :], ACT.Copy)
                act.activation(tmp[hd:2 * hd, 1, :], src[0:hd, :], ACT.Copy).then_inc(swapped.sem, 1)

            act.wait_ge(vec_turned, 1)
            act.activation(vecs[:, :], ps[:, 5, 0:NV], ACT.Copy).then_inc(vec_ready, 1)
            act.wait_ge(vec_ready, 1)
            act.activation(half_gain[:, :], vecs[:, 0:DEPTH * NN * KD], ACT.Copy, scale=0.5).then_inc(vec_ready, 1)
            with act.Fori(0, DEPTH) as l:
                pre_norm(l, 0)
                up(l, 0)
                post_norm(l, 0, l * GROUPS + DOWN[0], down_unit)
                act.dma_start(w_a2_sb[:, :], w_a2[l]).then_inc(w_a2_loaded, 16)
                pre_norm(l, 1)
                wait(act, z_ready, l, 0)
                for q in range(QT):
                    o = act.activation(halves(e_buf[:, q, :]), pair(2 + q), ACT.Abs,
                                       bias=vecs[:, bass.ds(l * QT + (V_BA + q), 1)])
                o.then_inc(z_abs.sem, 1)
                wait(act, z_abs, l, 0)
                act.activation(e_buf[:, :, :], e_buf[:, :, :], ACT.Exp, scale=-1.0).then_inc(z_exp.sem, 1)
                wait(act, z_exp, l, 0)
                act.activation(e_buf[:, :, :], e_buf[:, :, :], ACT.Ln, bias=ones[:, 0:1]).then_inc(z_ln.sem, 1)
                for t in range(SCAN_SLOT, NIN):
                    if ROT0 <= t < ROT0 + 2 * HR:
                        swap_halves(l, t)
                    if t in DIFF_SLOT:
                        s = DIFF_SLOT[t]
                        if s == "q":
                            wait(act, b_ready, l, 0)
                            act.activation(e_buf[:, :, :], b_cum[:, :, :], ACT.Exp, scale=1.0 / GATE_TEMP)\
                                .then_inc(exp_ready.sem, 1)
                        else:
                            n = 0 if s == "k" else 1 + s
                            wait(act, diff_ready, l, n)
                            act.activation(e_buf[:, :, :], e_buf[:, :, :], ACT.Exp, scale=1.0 / GATE_TEMP)\
                                .then_inc(exp_ready.sem, 1)
                wait(act, in_read, l, NIN - 1)
                for i in range(2):
                    act.activation(g_t[:, i * HG:(i + 1) * HG, :], g_t[:, i * HG:(i + 1) * HG, :], ACT.Silu)\
                        .then_inc(silu_done.sem, 1)
                for c_ in range(NCH + 1):
                    n = CH if c_ < NCH else TS
                    if c_ == NCH:
                        wait(act, state_ready, l, NCH - 1)
                        last = (NCH - 1) % 2
                        act.dma_start(gla_p[l, 0].rearrange("(q p) k v -> (p k) q v", p=2), s_gla[:, last, :, :])\
                            .then_inc(states_stored, 16)
                        act.dma_start(ret_p[l, 0].rearrange("h k v -> k h v"), s_ret[:, last, :, :])\
                            .then_inc(states_stored, 16)
                        wait(act, o_normed, l, NCH - 1)
                        wait(act, o_turned, l, NCH - 1)
                        act.wait_ge(states_stored, l * STATE_DMAS + 32)
                        for q in range(QT):
                            act.dma_start(gla_state[:, q, :, :], state_gla[l, :, 2 * q:2 * q + 2]
                                          .rearrange("b p k v -> (p k) b v")).then_inc(states_loaded, 16)
                        for h in range(HR):
                            act.dma_start(ret_state[:, h, :, :], state_ret[l, :, h].rearrange("b k v -> k b v"))\
                                .then_inc(states_loaded, 16)
                    wait(act, turned, l, c_)
                    if c_:
                        wait(act, o_ready, l, c_ - 1)
                    vt, kt = (v_tok, k_tok) if c_ < NCH else (v_tok_s, k_tok_s)
                    for i in range(2):
                        act.activation(vt[0:n, 4 * i:4 * i + 4, :],
                                       ps[0:n, i, :].rearrange("p (h v) -> p h v", v=DV), ACT.Copy)
                    act.activation(kt[0:n, HR * P:(HR + QT) * P], ps[0:n, 3, 0:QT * P], ACT.Copy)\
                        .then_inc(v_tok_ready.sem, 1)
                    wait(act, o_ready, l, c_)
                    if c_ < NCH:
                        w = sq[:, :, 0:4 * DV]
                        act.activation(w, ps[:, 6:8, :], ACT.Square).then_inc(o_sq.sem, 1)
                        wait(act, o_ms, l, c_)
                        act.activation(rms[:, 1, :], rms[:, 0, :], ACT.Sqrt, bias=eps, scale=1.0 / DV)\
                            .then_inc(o_root.sem, 1)
                    else:
                        act.activation(sq[:, 0, 0:HA * TS].rearrange("p (a t) -> p a t", a=2), ps[:, 6:8, 0:HG * TS],
                                       ACT.Square).then_inc(o_sq.sem, 1)
                        wait(act, o_ms, l, c_)
                        act.activation(sq[:, 1, 0:HA * TS], ps[:, 4, 0:HA * TS], ACT.Sqrt, bias=eps, scale=1.0 / DV)\
                            .then_inc(o_root.sem, 1)
                wait(act, s_updated, l, HG - 1)
                for q in range(QT):
                    act.dma_start(gla_s[l, :, 2 * q:2 * q + 2].rearrange("b p k v -> (p k) b v"), gla_state[:, q, :, :])\
                        .then_inc(states_stored, 16)
                for h in range(HR):
                    wait(act, s_updated, l, HG + h)
                    act.dma_start(ret_s[l, :, h].rearrange("b k v -> k b v"), ret_state[:, h, :, :])\
                        .then_inc(states_stored, 16)
                wait(act, o_gated, l, NCH)
                act.wait_ge(states_stored, l * STATE_DMAS + STATE_DMAS)
                for h in range(HA):
                    act.activation(xs_hi[:, h, :], v_t[:, h, :], ACT.Copy).then_inc(oh_ready.sem, 1)
                post_norm(l, 1, l * GROUPS + WOUT, out_unit)
                pre_norm(l, 2)
                up(l, 1)
                post_norm(l, 2, l * GROUPS + DOWN[1], down_unit)

            for i in range(2 * (NCH + 1)):
                c_, a = i // 2, i % 2
                n = P if c_ < NCH else TS
                act.wait_ge(y_turned, i + 1)
                act.activation(y_tok[0:n, c_, a * 512:(a + 1) * 512], ps[0:n, i % 4, :], ACT.Copy).then_inc(y_copied, 1)
                if a:
                    act.wait_ge(y_copied, i + 1)
                    act.dma_start(y_prompt[0, c_ * P:(c_ + 1) * P, :] if c_ < NCH else
                                  y_sample.rearrange("b t d -> (b t) d"), y_tok[0:n, c_, :]).then_inc(stored, 16)
            act.wait_ge(stored, 16 * (NCH + 1))
            act.wait_ge(states_stored, DEPTH * STATE_DMAS)

        @block.vector
        def _(dve):
            def pre_low(l, q, k):
                wait(dve, xh_ready, l, q * KD + k)
                dve.scalar_tensor_tensor(out=xs_lo[:, k, :], in0=x[:, k, :], scalar=gain(l, 2 * q, k),
                                         in1=xs_hi[:, k, :].bitcast(F32), op0=ALU.mult, op1=ALU.subtract)\
                   .then_inc(xs_ready.sem, 1)

            def up(l, f):
                with dve.Fori(0, UP_GROUPS) as i:
                    for par in range(2):
                        at = l * gate_scaled.per + i * 2 + (f * KF + par + 1)
                        wait(dve, pre_ready, l, 2 * f)
                        wait_unit(dve, l * GROUPS + UP[f] + i, 2 * par + 1)
                        dve.tensor_tensor(halves(tmp[:, 0, :]), pair(2 * par), halves(rstd_pre[:, :]), ALU.mult)\
                           .then_inc(gate_scaled.sem, 1)
                        dve.tensor_tensor(halves(tmp[:, 1, :]), pair(2 * par + 1), halves(rstd_pre[:, :]), ALU.mult)\
                           .then_inc(up_scaled.sem, 1)
                        dve.wait_ge(gate_silu.sem, at)
                        dve.wait_ge(up_scaled.sem, at)
                        dve.tensor_tensor(tmp[:, 0, :], tmp[:, 0, :], tmp[:, 1, :], ALU.mult).then_inc(h_prod.sem, 1)
                        dve.wait_ge(hh_ready.sem, at)
                        tile = bass.ds(i * 2 + par, 1)
                        dve.tensor_tensor(h_lo[:, tile, :], tmp[:, 0:1, :], h_hi[:, tile, :].bitcast(F32), ALU.subtract)\
                           .then_inc(h_ready.sem, 1)
                        dve.wait_ge(h_ready.sem, at)

            def add_squares(l, q):
                for m in range(1, KD):
                    wait(dve, y_read, l, q * KD + m)
                    if m > 1:
                        wait(dve, acc_step, l, q * (KD - 1) + m - 2)
                    dve.tensor_tensor(acc[:, :], sq[:, 0, :] if m == 1 else acc[:, :], sq[:, m % 2, :], ALU.add)\
                       .then_inc(acc_step.sem, 1)

            def residual(l, q, pre=None):
                add_squares(l, q)
                wait(dve, post_ready, l, q)
                for k in range(KD):
                    yk = (y_out if q == 1 else y)[:, k, :]
                    dve.tensor_tensor(yk, yk, acc[:, :], ALU.mult).then_inc(y_scaled.sem, 1)
                    if pre is not None and k:
                        pre_low(l, pre, k - 1)
                    wait(dve, y_scaled, l, q * KD + k)
                    dve.scalar_tensor_tensor(out=x[:, k, :], in0=yk, scalar=post_gain(l, q, k), in1=x[:, k, :],
                                             op0=ALU.mult, op1=ALU.add).then_inc(x_ready.sem, 1)
                if pre is not None:
                    pre_low(l, pre, KD - 1)

            def take_tile(l, t):
                wait_in_tile(dve, l, t)
                out, src, r, scale = None, pair(t % 2), halves(rstd_pre[:, :]), None
                if t == 0:
                    dve.tensor_tensor(halves(tmp[0:GR, 0, :]), src[0:GR], r[0:GR], ALU.mult).then_inc(in_read.sem, 1)
                    return
                kind, i = IN_GROUPS[(t - 1) // UNITS][0], (t - 1) % UNITS
                out = {"qk_a": qk_a, "v_a": v_t, "q_r": q_r, "k_r": k_r, "v_r": v_t, "g_a": g_t, "g_r": g_t}[kind]
                i += {"v_r": HG, "g_r": HG}.get(kind, 0)
                scale = DKG ** -0.5 if kind == "qk_a" and i < QT else 1.0
                dve.scalar_tensor_tensor(out=halves(out[:, i, :]), in0=src, scalar=scale, in1=r, op0=ALU.mult,
                                         op1=ALU.mult).then_inc(in_read.sem, 1)

            def rotate(l, n):
                buf, scale = (q_r, 1.0) if n < HR else (k_r, DKR ** -0.5)
                wait(dve, swapped, l, n)
                dve.scalar_tensor_tensor(out=tmp[:, 1, :], in0=tmp[:, 1, :], scalar=scale, in1=sin, op0=ALU.mult,
                                         op1=ALU.mult)
                dve.scalar_tensor_tensor(out=buf[:, n % HR, :], in0=buf[:, n % HR, :], scalar=scale, in1=cos,
                                         op0=ALU.mult, op1=ALU.mult).then_inc(rot_parts.sem, 1)
                wait(dve, rot_parts, l, n)
                dve.tensor_tensor(buf[:, n % HR, :], buf[:, n % HR, :], tmp[:, 1, :], ALU.add).then_inc(rotated.sem, 1)

            def by_block(buf, w, m):
                return buf[:, :, 0:w].rearrange("p q (n h m) -> p q n h m", h=2, m=m)

            def exponents(l, s):
                if s == "q":
                    return
                wait(dve, prod_ready, l, STEPS.index(s) - 1)
                if s == "k":
                    for t0, w, m in ((0, TP, CH), (TP, TS, DS)):
                        b = b_cum[:, :, t0:t0 + w].rearrange("p q (n m) -> p q n m", m=m)
                        e = e_buf[:, :, t0:t0 + w].rearrange("p q (n m) -> p q n m", m=m)
                        o = dve.tensor_tensor(e, b[:, :, :, m - 1:m].broadcast_to([P, QT, w // m, m]), b, ALU.subtract)
                    o.then_inc(diff_ready.sem, 1)
                    return
                m = LEVELS[s]
                w = T if m < DS else TP
                b, e = by_block(b_cum, w, m), by_block(e_buf, w, m)
                ref = b[:, :, :, 0, m - 1:m].broadcast_to([P, QT, w // (2 * m), m])
                dve.tensor_tensor(e[:, :, :, 0, :], ref, b[:, :, :, 0, :], ALU.subtract)
                dve.tensor_tensor(e[:, :, :, 1, :], b[:, :, :, 1, :], ref, ALU.subtract).then_inc(diff_ready.sem, 1)

            def products(l, s):
                queries, keys = qk_a[:, 0:QT, :], qk_a[:, QT:2 * QT, :]
                j = STEPS.index(s)
                wait(dve, exp_ready, l, j)
                if s == "q":
                    dve.tensor_copy(chunk_decay[:, :, 0:NCH], e_buf[:, :, CH - 1:TP:CH])
                    dve.tensor_copy(chunk_decay[:, :, NCH:NCH + NS], e_buf[:, :, TP + DS - 1:T:DS])
                    dve.tensor_tensor(q_dec[:, :, :], queries, e_buf[:, :, :], ALU.mult).then_inc(prod_ready.sem, 1)
                elif s == "k":
                    dve.tensor_tensor(k_dec[:, :, :], keys, e_buf[:, :, :], ALU.mult).then_inc(prod_ready.sem, 1)
                else:
                    m = LEVELS[s]
                    w = T if m < DS else TP
                    if s:
                        wait(dve, scores_ready, l, s - 1)
                    dve.tensor_tensor(k_lvl[:, :, 0:w], keys[:, :, 0:w], e_buf[:, :, 0:w], ALU.mult)
                    dve.tensor_tensor(q_lvl[:, :, 0:w // 2].rearrange("p q (n m) -> p q n m", m=m),
                                      by_block(queries, w, m)[:, :, :, 1, :], by_block(e_buf, w, m)[:, :, :, 1, :],
                                      ALU.mult).then_inc(prod_ready.sem, 1)

            def take_scores(l, n):
                ahead_of_wait(dve)
                wait(dve, scores_ready, l, n)
                if n == 0:
                    wait(dve, a_zeroed, l, 0)
                for p in range(2):
                    if n < NL:
                        m = LEVELS[n]
                        mask = msk[:, n * (CH // 2):(n + 1) * (CH // 2)]
                        nb = CH // (2 * m)
                        for i in range(NCH):
                            o = dve.copy_predicated(
                                a_gla[:, p, i].rearrange("p x (n h m) -> p x n h m", h=2, m=m)[:, :, :, 1, :],
                                mask.rearrange("p (x n m) -> p x n m", x=1, m=m).broadcast_to([P, 2, nb, m]),
                                ps[:, 4 + 2 * (n % 2) + p, i * CH:(i + 1) * CH].rearrange("p (x n m) -> p x n m", x=2, m=m))
                        if m < DS:
                            nb = TS // (2 * m)
                            o = dve.copy_predicated(
                                a_gla_s[:, p].rearrange("p x (n h m) -> p x n h m", h=2, m=m)[:, :, :, 1, :],
                                mask[0:TS, 0:TS // 2].rearrange("p (x n m) -> p x n m", x=1, m=m)
                                .broadcast_to([TS, 2, nb, m]),
                                ps[0:TS, 4 + 2 * ((n + 1) % 2) + p, 0:2 * TS]
                                .rearrange("p (x t) -> p x t", x=2)[:, :, 0:TS // 2]
                                .rearrange("p x (n m) -> p x n m", m=m))
                    elif n == NL:
                        mask = msk[:, NL * (CH // 2):NL * (CH // 2) + CH].rearrange("p (x t) -> p x t", x=1)
                        o = dve.copy_predicated(a_gla[:, p].rearrange("p c x t -> p (c x) t"),
                                                mask.broadcast_to([P, 2 * NCH, CH]),
                                                ps[:, 4 + 2 * p:6 + 2 * p, :].rearrange("p a (x t) -> p (a x) t", t=CH))
                    else:
                        mask = msk[0:TS, NL * (CH // 2):NL * (CH // 2) + TS].rearrange("p (x t) -> p x t", x=1)
                        o = dve.copy_predicated(a_gla_s[:, p], mask.broadcast_to([TS, 2, TS]),
                                                ps[0:TS, 4 + 2 * p, 0:2 * CH].rearrange("p (x t) -> p x t", t=CH)[:, :, 0:TS])
                o.then_inc(scores_taken.sem, 1)

            def chunk_buffers(l, c_):
                sample = c_ == NCH
                n, t0 = (TS, TP) if sample else (CH, c_ * CH)
                wait(dve, turned, l, c_)
                if c_:
                    wait(dve, o_ready, l, c_ - 1)
                if sample:
                    dve.wait_ge(states_loaded, l * STATE_LOADS + STATE_LOADS)
                kt, decay = (k_tok_s, c("k_decay_s", TS)) if sample else (k_tok, c("k_decay"))
                for h in range(HR):
                    o = dve.tensor_scalar(kt[0:n, h * P:(h + 1) * P], ps[0:n, 2, h * P:(h + 1) * P], decay[:, h:h + 1],
                                          None, ALU.mult)
                o.then_inc(k_tok_ready.sem, 1)
                if c_:
                    q_decay = c("q_decay").rearrange("p (h t) -> p h t", h=HR)
                    if sample:
                        for h in range(HR):
                            o = dve.tensor_tensor(q_ret_dec_s[:, h, :].rearrange("p (b t) -> p b t", t=DS),
                                                  q_r[:, h, TP:T].rearrange("p (b t) -> p b t", t=DS),
                                                  q_decay[:, h:h + 1, 0:DS].broadcast_to([P, NS, DS]), ALU.mult)
                    else:
                        o = dve.tensor_tensor(q_ret_dec[:, :, :], q_r[:, :, t0:t0 + CH], q_decay, ALU.mult)
                    o.then_inc(qd_ready.sem, 1)
                wait(dve, ret_scores, l, c_)
                if sample:
                    dve.tensor_tensor(a_ret_s.rearrange("p h t -> p (h t)"), ps[0:TS, 4, 0:HR * TS],
                                      c("decay_mask_s", TS), ALU.mult).then_inc(a_ret_ready.sem, 1)
                else:
                    dve.tensor_tensor(a_ret.rearrange("p h t -> p (h t)"), ps[:, 4, :], c("decay_mask"), ALU.mult)\
                       .then_inc(a_ret_ready.sem, 1)

            def update_states(l, c_):
                wait(dve, state_delta, l, c_)
                new, old = c_ % 2, (c_ - 1) % 2
                if c_ >= 1:
                    wait(dve, o_ready, l, c_ - 1)
                    wait(dve, state_ready, l, c_ - 1)
                for q in range(QT):
                    delta = ps[:, 3, (QT + q) * DV:(QT + q + 1) * DV]
                    if c_ == 0:
                        dve.tensor_copy(s_gla[:, new, q, :], delta)
                    else:
                        dve.scalar_tensor_tensor(out=s_gla[:, new, q, :], in0=s_gla[:, old, q, :],
                                                 scalar=chunk_decay[:, q, c_:c_ + 1], in1=delta, op0=ALU.mult, op1=ALU.add)
                for h in range(HR):
                    delta = ps[:, 5, h * DV:(h + 1) * DV]
                    if c_ == 0:
                        o = dve.tensor_copy(s_ret[:, new, h, :], delta)
                    else:
                        o = dve.scalar_tensor_tensor(out=s_ret[:, new, h, :], in0=s_ret[:, old, h, :],
                                                     scalar=gammas[h] ** CH, in1=delta, op0=ALU.mult, op1=ALU.add)
                o.then_inc(state_ready.sem, 1)

            def norm_outputs(l, c_):
                wait(dve, o_sq, l, c_)
                if c_:
                    wait(dve, o_normed, l, c_ - 1)
                dve.tensor_reduce(rms[:, 0, :], sq[:, :, 0:4 * DV].rearrange("p a (h v) -> p a h v", v=DV), AX.X,
                                  ALU.add).then_inc(o_ms.sem, 1)
                wait(dve, o_root, l, c_)
                dve.reciprocal(rms[:, 0, :], rms[:, 1, :]).then_inc(o_rms.sem, 1)
                wait(dve, o_rms, l, c_)
                for a in range(2):
                    o = dve.tensor_tensor(o_tok[:, 4 * a:4 * a + 4, :], ps[:, 6 + a, :].rearrange("p (h v) -> p h v", v=DV),
                                          rms[:, 0, 4 * a:4 * a + 4].rearrange("p (h v) -> p h v", v=1)
                                          .broadcast_to([P, 4, DV]), ALU.mult)
                o.then_inc(o_normed.sem, 1)

            def gate_outputs(l, c_):
                wait(dve, o_turned, l, c_)
                if c_ == 0:
                    wait(dve, gates_ready, l, 0)
                for a in range(2):
                    o = dve.tensor_tensor(v_t[:, 4 * a:4 * a + 4, c_ * CH:(c_ + 1) * CH],
                                          ps[:, 4 + a, :].rearrange("p (h t) -> p h t", t=CH),
                                          g_t[:, 4 * a:4 * a + 4, c_ * CH:(c_ + 1) * CH], ALU.mult)
                o.then_inc(o_gated.sem, 1)

            def head_gains(l):
                for i in range(2):
                    wait(dve, silu_done, l, i)
                    for h in range(HG):
                        v = bass.ds(l * HG + ((V_GLA if i == 0 else V_RET) + h), 1)
                        o = dve.tensor_scalar(g_t[:, i * HG + h, :], g_t[:, i * HG + h, :], vecs[:, v], None, ALU.mult)
                o.then_inc(gates_ready.sem, 1)

            def sample_outputs(l):
                wait(dve, o_root, l, NCH)
                dve.reciprocal(sq[:, 0, 0:HA * TS], sq[:, 1, 0:HA * TS]).then_inc(o_rms.sem, 1)
                wait(dve, o_rms, l, NCH)
                r = sq[:, 0, 0:HA * TS].rearrange("p (h t) -> p h t", t=TS)
                for a in range(2):
                    o = dve.tensor_tensor(tmp[:, 0, a * HG * TS:(a + 1) * HG * TS].rearrange("p (h t) -> p h t", t=TS),
                                          ps[:, 6 + a, 0:HG * TS].rearrange("p (h t) -> p h t", t=TS),
                                          r[:, a * HG:(a + 1) * HG, :], ALU.mult)
                o.then_inc(o_normed.sem, 1)
                wait(dve, o_normed, l, NCH)
                normed = tmp[:, 0, 0:HA * TS].rearrange("p (h t) -> p h t", t=TS)
                for i, heads in enumerate((slice(0, HG, 2), slice(HG, HG + 2), slice(1, HG, 2), slice(HG + 2, HA))):
                    o = dve.tensor_tensor(v_t[:, heads, TP:T], normed[:, 2 * i:2 * i + 2, :], g_t[:, heads, TP:T], ALU.mult)
                o.then_inc(o_gated.sem, 1)

            def mask_values(l, h):
                if h == 0:
                    wait(dve, v_tok_ready, l, NCH)
                else:
                    wait(dve, s_delta, l, h - 1)
                dve.tensor_tensor(v_by_batch[:, :, :], v_tok_s[:, h:h + 1, :].broadcast_to([TS, NS, DV]),
                                  c("batch_mask", TS).rearrange("p (b x) -> p b x", x=1).broadcast_to([TS, NS, DV]),
                                  ALU.mult).then_inc(v_masked.sem, 1)

            def update_sample_state(l, h):
                wait(dve, s_delta, l, h)
                if h == 0:
                    wait(dve, o_ready, l, NCH)
                delta = ps[:, 2 * (h % 2):2 * (h % 2) + 2, :]
                if h < HG:
                    q, p = h // 2, h % 2
                    for b in range(NS):
                        rows = slice(p * DKG, (p + 1) * DKG)
                        o = dve.scalar_tensor_tensor(out=gla_state[rows, q, b, :], in0=gla_state[rows, q, b, :],
                                                     scalar=chunk_decay[rows, q, NCH + b:NCH + b + 1],
                                                     in1=delta[rows, b // 4, b % 4 * DV:(b % 4 + 1) * DV],
                                                     op0=ALU.mult, op1=ALU.add)
                else:
                    s = ret_state[:, h - HG, :, :].rearrange("p (a b) v -> p a (b v)", a=2)
                    o = dve.scalar_tensor_tensor(out=s, in0=s, scalar=gammas[h - HG] ** DS, in1=delta, op0=ALU.mult,
                                                 op1=ALU.add)
                o.then_inc(s_updated.sem, 1)

            dve.wait_ge(loaded, LOADS)
            dve.tensor_copy(msk[:, :], mask_rows[:, :])
            dve.wait_ge(x_turned, 1)
            dve.tensor_copy(x[:, :, TP:T], ps[:, 4, 0:KD * TS].rearrange("p (d t) -> p d t", t=TS)).then_inc(x_copied, 1)
            for d in range(KD):
                dve.wait_ge(x_turned, d + 2)
                dve.tensor_copy(x[:, d, 0:TP], ps[:, d % 4, :]).then_inc(x_copied, 1)
            dve.wait_ge(x_copied, X0)
            dve.sem_inc(x_ready.sem, X0)
            with dve.Fori(0, DEPTH) as l:
                for k in range(KD):
                    pre_low(l, 0, k)
                up(l, 0)
                residual(l, 0, pre=1)
                for t in range(NIN):
                    if t == 0:
                        wait(dve, pre_ready, l, 1)
                    take_tile(l, t)
                    if t == UNITS:
                        wait(dve, z_abs, l, 0)
                        for q in range(QT):
                            o = dve.tensor_scalar(halves(k_lvl[:, q, :]), pair(2 + q), vecs[:, bass.ds(l * QT + (V_BA + q), 1)], 0.0,
                                                  ALU.add, ALU.min)
                        o.then_inc(z_min.sem, 1)
                        dve.memset(a_gla.rearrange("p a c x t -> p (a c x t)"), 0.0)
                        dve.memset(a_gla_s.rearrange("p a x t -> p (a x t)"), 0.0).then_inc(a_zeroed.sem, 1)
                    if t == SCAN_SLOT:
                        wait(dve, z_ln, l, 0)
                        wait(dve, z_min, l, 0)
                        dve.tensor_tensor(k_lvl[:, :, :], k_lvl[:, :, :], e_buf[:, :, :], ALU.subtract)\
                           .then_inc(log_gate.sem, 1)
                        wait(dve, log_gate, l, 0)
                        for q in range(QT):
                            o = dve.tensor_tensor_scan(b_cum[:, q, :], c("scan_keep"), k_lvl[:, q, :], 0.0, ALU.mult, ALU.add)
                        o.then_inc(b_ready.sem, 1)
                    if ROT0 < t <= ROT0 + 2 * HR:
                        rotate(l, t - 1 - ROT0)
                    if t in TAKE_SLOT:
                        take_scores(l, TAKE_SLOT[t])
                    if t in PROD_SLOT:
                        products(l, PROD_SLOT[t])
                    if t in DIFF_SLOT:
                        exponents(l, DIFF_SLOT[t])
                for c_ in range(NCH):
                    chunk_buffers(l, c_)
                    update_states(l, c_)
                    if c_ == 0:
                        head_gains(l)
                    norm_outputs(l, c_)
                    gate_outputs(l, c_)
                chunk_buffers(l, NCH)
                mask_values(l, 0)
                sample_outputs(l)
                for h in range(HA):
                    if h + 1 < HA:
                        mask_values(l, h + 1)
                    update_sample_state(l, h)
                for h in range(HA):
                    wait(dve, oh_ready, l, h)
                    dve.tensor_tensor(xs_lo[:, h, :], v_t[:, h, :], xs_hi[:, h, :].bitcast(F32), ALU.subtract)\
                       .then_inc(ol_ready.sem, 1)
                residual(l, 1, pre=2)
                up(l, 1)
                residual(l, 2)


_INS = ["x_prompt", "x_sample", "state_gla", "state_ret", "norm_g", "w1_gu", "w1_down", "w2_gu", "w2_down",
        "w_in", "w_a2", "b_a", "gn_gla", "gn_ret", "w_out"]
PAST_LEN = 4096
ROPE_BASE = 10000.0


def _tables(np, HR, DKR, TP, NS, DS):
    TS = NS * DS
    T = TP + TS
    cols, n = const_layout(HR, T, TS, NS, 0)
    tab = np.zeros((P, n), np.float32)

    def put(name, a):
        lo, hi = cols[name]
        tab[0:a.shape[0], lo:hi] = a.reshape(a.shape[0], hi - lo)

    put("ident", np.eye(P))
    put("ones", np.ones((P, P)))
    half = DKR // 2
    freq = np.float32(ROPE_BASE) ** (-np.arange(half, dtype=np.float32) / np.float32(half))
    pos = np.concatenate([np.arange(TP), np.tile(PAST_LEN + np.arange(DS), NS)]).astype(np.float32)
    ang = (freq[:, None] * pos[None, :]).astype(np.float32).astype(np.float64)
    put("cos", np.concatenate([np.cos(ang), np.cos(ang)]))
    put("sin", np.concatenate([-np.sin(ang), np.sin(ang)]))
    gam = 1.0 - 2.0 ** (-5.0 - np.arange(HR))
    i = np.arange(CH)
    d = i[None, :] - i[:, None]
    put("decay_mask", np.stack([np.where(d >= 0, g ** np.maximum(d, 0), 0.0) for g in gam], 1))
    put("q_decay", np.broadcast_to(np.stack([g ** (i + 1) for g in gam])[None], (P, HR, CH)))
    put("k_decay", np.stack([g ** (CH - 1 - i) for g in gam], 1))
    j = np.arange(TS)
    put("k_decay_s", np.stack([g ** (DS - 1 - j % DS) for g in gam], 1))
    d = j[None, :] - j[:, None]
    same = j[None, :] // DS == j[:, None] // DS
    put("decay_mask_s", np.stack([np.where(same & (d >= 0), g ** np.maximum(d, 0), 0.0) for g in gam], 1))
    keep = np.ones((P, T))
    keep[:, 0:TP:CH] = 0.0
    keep[:, TP::DS] = 0.0
    put("scan_keep", keep)
    put("batch_mask", (j[:, None] // DS == np.arange(NS)[None, :]).astype(np.float32))
    put("eps", np.full((P, 1), EPS))
    parts = []
    t = np.arange(CH // 2)
    for m in LEVELS:
        parts.append((i[:, None] // (2 * m) == t[None, :] // m) & (i[:, None] % (2 * m) < m))
    parts.append(np.eye(CH, dtype=bool))
    return tab, np.concatenate(parts, 1).astype(np.float32), [float(g) for g in gam]


def kernel(**inputs):
    import numpy as _np
    import concourse.bacc as _bacc
    from concourse import mybir as _mybir
    from concourse.bass_utils import run_bass_kernel_spmd as _run

    nc = _bacc.Bacc("TRN2", target_bir_lowering=False, num_devices=1)
    arrays, args = {}, []
    given = {name: _np.ascontiguousarray(inputs[name]) for name in _INS}
    DEPTH, NS, HG, DKG, DV = given["state_gla"].shape
    HR, DKR = given["state_ret"].shape[2:4]
    B, TP, D = given["x_prompt"].shape
    DS = given["x_sample"].shape[1]
    given["consts"], given["masks"], gammas = _tables(_np, HR, DKR, TP, NS, DS)
    for name, a in given.items():
        arrays[f"in_{name}_dram"] = a
        args.append(nc.dram_tensor(f"in_{name}_dram", a.shape, _mybir.dt.from_np(a.dtype), kind="ExternalInput").ap())
    outs = [(B, TP, D), (NS, DS, D), (DEPTH, B, HG, DKG, DV), (DEPTH, B, HR, DKR, DV),
            (DEPTH, NS, HG, DKG, DV), (DEPTH, NS, HR, DKR, DV)]
    for i, shape in enumerate(outs):
        args.append(nc.dram_tensor(f"out_{i}_dram", shape, F32, kind="ExternalOutput").ap())
    trunk_kernel(nc, *args, gammas)
    r = _run(nc, [arrays], core_ids=[0])
    return tuple(r.results[0][f"out_{i}_dram"] for i in range(len(outs)))
```

```python
from contextlib import ExitStack

import concourse.bass as bass
from concourse import mybir

F32 = mybir.dt.float32
F32R = mybir.dt.float32r
U8 = mybir.dt.uint8
ALU = mybir.AluOpType
ACT = mybir.ActivationFunctionType
AX = mybir.AxisListType

P = 128
EPS = 1e-6
GATE_TEMP = 16.0
SPLIT_SLOTS = 2
UNITS = 4
UNIT_KT = 8
CH = 128
LEVELS = (64, 32, 16, 8, 4, 2, 1)


class Signal:

    def __init__(self, sem, per_layer):
        self.sem, self.per = sem, per_layer

    def at(self, l, i):
        return l * self.per + (i + 1)


def const_layout(HR, T, TS, NS, NV):
    cols, at = {}, 0
    for name, n in (("ident", P), ("ones", P), ("cos", T), ("sin", T), ("decay_mask", HR * CH),
                    ("q_decay", HR * CH), ("k_decay", HR), ("k_decay_s", HR), ("decay_mask_s", HR * TS),
                    ("scan_keep", T), ("batch_mask", NS), ("eps", 1)):
        cols[name] = (at, at + n)
        at += n
    return cols, at


def trunk_kernel(nc, x_prompt, x_sample, state_gla, state_ret, norm_g, w1_gu, w1_down, w2_gu, w2_down,
                 w_in, w_a2, b_a, gn_gla, gn_ret, w_out, consts, masks,
                 y_prompt, y_sample, gla_p, ret_p, gla_s, ret_s, gammas):
    DEPTH, NS, HG, DKG, DV = state_gla.shape
    HR, DKR = state_ret.shape[2:4]
    TP, D = x_prompt.shape[1:]
    DS = x_sample.shape[1]
    TS = NS * DS
    T = TP + TS
    HALF = T // 2
    KD = D // P
    FF = w1_down.shape[1]
    KF = FF // P
    GR = w_a2.shape[1]
    NCH = TP // CH
    HA = HG + HR
    QT = HG * DKG // P
    NN = norm_g.shape[1]
    DOWN_KT = [(KF + UNITS - 1 - u) // UNITS for u in range(UNITS)]
    ALO_KT = [KD // UNITS] * UNITS
    FULL_KT = [KD] * UNITS
    cc, _ = const_layout(HR, T, TS, NS, 0)
    V_GLA = DEPTH * NN * KD
    V_RET = V_GLA + DEPTH * HG
    V_BA = V_RET + DEPTH * HR
    NV = V_BA + DEPTH * QT

    GLA_V = 2 * HG * DKG
    GLA_G = GLA_V + HG * DV
    A_LO = GLA_G + HG * DV
    RET_Q = A_LO + GR
    RET_K = RET_Q + HR * DKR
    RET_V = RET_K + HR * DKR
    RET_G = RET_V + HR * DV
    IN_GROUPS = (("qk_a", 0), ("q_r", RET_Q), ("k_r", RET_K), ("v_a", GLA_V), ("v_r", RET_V),
                 ("g_a", GLA_G), ("g_r", RET_G))
    NIN = 1 + UNITS * len(IN_GROUPS)
    UP_GROUPS, DOWN_GROUPS, OUT_GROUPS = KF // 2, KD, KD // UNITS
    UP = (0, UP_GROUPS + DOWN_GROUPS + 1 + len(IN_GROUPS) + OUT_GROUPS)
    DOWN = (UP[0] + UP_GROUPS, UP[1] + UP_GROUPS)
    WIN = DOWN[0] + DOWN_GROUPS
    WOUT = WIN + 1 + len(IN_GROUPS)
    GROUPS = DOWN[1] + DOWN_GROUPS
    NL = len(LEVELS)
    SCAN_SLOT = 5
    STEPS = ["q", "k"] + list(range(NL))
    STEP_SLOTS = [6, 8, 10, 12, 14, 15, 16, 17, 18, 19]
    DIFF_SLOT = dict(zip(STEP_SLOTS, STEPS))
    PROD_SLOT = dict(zip(STEP_SLOTS[1:], STEPS))
    SCORE_SLOT = {t + 1: s for t, s in PROD_SLOT.items() if s not in ("q", "k")}
    SCORE_SLOT.update({21: NL, 22: NL + 1})
    TAKE_SLOT = {t + 1: n for t, n in SCORE_SLOT.items()}
    ROT0 = 1 + UNITS
    V_LAST = 5 * UNITS
    G0 = V_LAST + 1
    S = NCH
    IN_SLOT_STEPS = {24: ("turn", 0), 25: ("scores", 0), 26: ("out", 0), 27: ("turn", 1), 28: ("scores", 1)}
    TAIL_STEPS = (("back", 0), ("out", 1), ("turn", 2), ("scores", 2), ("back", 1), ("turn", 3), ("out", 2),
                  ("scores", 3), ("back", 2), ("turn", S), ("out", 3), ("scores", S), ("out", S), ("back", 3),
                  ("back", S))
    assert NCH == 4
    BANK0 = (4, 4, 0, 4, 0)
    BACK_BANKS = ((2, 3), (5, 7), (1, 3), (5, 7), (1, 3))
    UPDATE_ORDER = tuple(range(HG, HA)) + tuple(range(HG))

    with ExitStack() as ctx:
        def sb(name, shape, dt=F32):
            return ctx.enter_context(nc.sbuf_tensor(name, shape, dt))

        def sem(name):
            return ctx.enter_context(nc.semaphore(name))

        def sig(name, per_layer):
            return Signal(sem(name), per_layer)

        def overlay(*tensors):
            out = []
            with ExitStack() as place:
                for name, shape, dt in tensors:
                    out.append(place.enter_context(nc.sbuf_tensor(name, shape, dt)))
            return out

        x = sb("x", [P, KD, T])
        raw = sb("raw", [P, UNITS, UNIT_KT, P])
        w_hi = sb("w_hi", [P, SPLIT_SLOTS, UNIT_KT, P], F32R)
        w_lo = sb("w_lo", [P, SPLIT_SLOTS, UNIT_KT, P], F32R)
        cst = sb("cst", [P, consts.shape[1]])
        msk = sb("msk", [P, masks.shape[1]], U8)
        rstd_pre = sb("rstd_pre", [P, T])
        acc = sb("acc", [P, T])
        sq = sb("sq", [P, 2, T])
        tmp = sb("tmp", [P, 2, T])
        vecs = sb("vecs", [P, NV])
        half_gain = sb("half_gain", [P, DEPTH * NN * KD])
        chunk_decay = sb("chunk_decay", [P, QT, NCH + NS])
        rms = sb("rms", [P, 2, HA])

        xs_hi, xs_lo = overlay(("xs_hi", [P, KD, T], F32R), ("xs_lo", [P, KD, T], F32R))
        y, = overlay(("y", [P, KD, T], F32))
        ret_state, gla_state, v_tok_s, k_tok_s = overlay(
            ("ret_state", [P, HR, NS, DV], F32), ("gla_state", [P, QT, NS, DV], F32),
            ("v_tok_s", [TS, HA, P], F32), ("k_tok_s", [TS, HR * P + QT * P], F32))
        sb("xs_place", [P, 2 * KD * T])

        h_hi, h_lo = overlay(("h_hi", [P, KF, T], F32R), ("h_lo", [P, KF, T], F32R))
        x_tok, vec_rows, mask_rows = overlay(("x_tok", [P, NCH + 1, D], F32), ("vec_rows", [P, P], F32),
                                             ("mask_rows", [P, masks.shape[1]], F32))
        y_tok, = overlay(("y_tok", [P, NCH + 1, D], F32))
        (qk_a, b_cum, e_buf, k_lvl, q_lvl, q_dec, k_dec, v_t, g_t, q_r, k_r, a_gla, a_gla_s, a_ret_s,
         w_a2_sb) = overlay(
            ("qk_a", [P, 2 * QT, T], F32), ("b_cum", [P, QT, T], F32), ("e_buf", [P, QT, T], F32),
            ("k_lvl", [P, QT, T], F32), ("q_lvl", [P, QT, HALF], F32),
            ("q_dec", [P, QT, T], F32),
            ("k_dec", [P, QT, T], F32),
            ("v_t", [P, HA, T], F32),
            ("g_t", [P, HA, T], F32),
            ("q_r", [P, HR, T], F32), ("k_r", [P, HR, T], F32),
            ("a_gla", [P, 2, NCH, 2, CH], F32),
            ("a_gla_s", [TS, 2, 2, TS], F32), ("a_ret_s", [TS, HR, TS], F32),
            ("w_a2_sb", [GR, QT * P], F32))
        v_tok, k_tok, a_ret, s_gla, s_ret, o_tok = overlay(
            ("v_tok", [P, 2, HA, P], F32),
            ("k_tok", [P, HR * P + QT * P], F32),
            ("a_ret", [P, HR, CH], F32),
            ("s_gla", [P, 2, QT, DV], F32), ("s_ret", [P, 2, HR, DV], F32),
            ("o_tok", [P, HA, P], F32))
        _, y_out, o_lo, o_hi = overlay(("ahead_of_v_t", [P, 7 * QT * T + QT * HALF], F32), ("y_out", [P, KD, T], F32),
                                       ("o_lo", [P, HA, T], F32R), ("o_hi", [P, HA, T], F32R))
        assert KD == HA == 2 * HR
        sb("h_place", [P, 2 * KF * T])
        QW = NS * TS
        q_gla_s = acc[:, 0:QT * QW].rearrange("p (q t) -> p q t", t=QW)
        q_ret_s = v_tok[:, 0].rearrange("p h v -> p (h v)")[:, 0:HR * QW].rearrange("p (h t) -> p h t", t=QW)

        def v_by_batch(i):
            return v_tok[0:TS, i % 2].rearrange("p h v -> p (h v)")[:, 0:NS * DV].rearrange("p (b v) -> p b v", b=NS)

        ps = ctx.enter_context(nc.psum_tensor("ps", [P, 8, 512], F32))

        def pair(i):
            return ps[:, 2 * i:2 * i + 2, 0:HALF]

        def halves(ap):
            return ap.rearrange("p (a t) -> p a t", a=2)

        def c(name, parts=P):
            a, b = cc[name]
            return cst[0:parts, a:b]

        ident, ones, eps = c("ident"), c("ones"), c("eps")
        cos, sin = c("cos"), c("sin")

        def gain(l, n, k):
            return vecs[:, bass.ds(l * (NN * KD) + (n * KD + k), 1)]

        def post_gain(l, q, k):
            table = vecs if q == 1 else half_gain
            return table[:, bass.ds(l * (NN * KD) + ((2 * q + 1) * KD + k), 1)]

        loaded, vec_turned, vec_ready = sem("loaded"), sem("vec_turned"), sem("vec_ready")
        raw_ready = [sem(f"raw_ready{i}") for i in range(UNITS)]
        units_issued, mask_begun, sample_begun = sem("units_issued"), sem("mask_begun"), sem("sample_begun")
        hi_split = sem("hi_split")
        split_ready = [sem(f"split_ready{i}") for i in range(SPLIT_SLOTS)]
        split_used = [sem(f"split_used{i}") for i in range(SPLIT_SLOTS)]
        x_turned, x_copied = sem("x_turned"), sem("x_copied")
        w_a2_loaded = sem("w_a2_loaded")
        xh_ready, xs_ready = sig("xh_ready", 3 * KD), sig("xs_ready", 3 * KD)
        xsq_ready, xsq_used = sig("xsq_ready", 3 * KD), sig("xsq_used", 3 * KD)
        pre_log, pre_ready = sig("pre_log", 3), sig("pre_ready", 3)
        y_read = sig("y_read", 3 * KD)
        acc_step = sig("acc_step", 3 * (KD - 1))
        post_sum, post_log, post_ready = sig("post_sum", 3), sig("post_log", 3), sig("post_ready", 3)
        y_scaled, x_ready = sig("y_scaled", 3 * KD), sig("x_ready", 3 * KD)
        gate_scaled, up_scaled = sig("gate_scaled", 2 * KF), sig("up_scaled", 2 * KF)
        gate_silu, h_prod = sig("gate_silu", 2 * KF), sig("h_prod", 2 * KF)
        hh_ready, h_ready = sig("hh_ready", 2 * KF), sig("h_ready", 2 * KF)
        in_read = sig("in_read", NIN)
        z_ready, z_abs, z_min = sig("z_ready", 1), sig("z_abs", 1), sig("z_min", 1)
        z_exp, z_ln, log_gate, b_ready = sig("z_exp", 1), sig("z_ln", 1), sig("log_gate", 1), sig("b_ready", 1)
        swapped, rot_parts, rotated = sig("swapped", 2 * HR), sig("rot_parts", 2 * HR), sig("rotated", 2 * HR)
        silu_done, gates_ready = sig("silu_done", HA), sig("gates_ready", HA)
        diff_ready, exp_ready, prod_ready = sig("diff_ready", NL + 1), sig("exp_ready", NL + 2), sig("prod_ready", NL + 2)
        scores_ready, scores_taken, a_zeroed = sig("scores_ready", NL + 2), sig("scores_taken", NL + 2), sig("a_zeroed", 1)
        NSTEP = NCH + 1
        turned, v_tok_ready, k_tok_ready = sig("turned", NSTEP), sig("v_tok_ready", NSTEP), sig("k_tok_ready", NSTEP)
        qd_ready, q_zeroed, q_masked = sig("qd_ready", NCH - 1), sig("q_zeroed", 1), sig("q_masked", 1)
        ret_scores, a_ret_ready = sig("ret_scores", NSTEP), sig("a_ret_ready", NSTEP)
        state_delta, state_ready = sig("state_delta", NCH), sig("state_ready", NCH)
        o_ready, o_sq, o_ms = sig("o_ready", NSTEP), sig("o_sq", NSTEP), sig("o_ms", NSTEP)
        o_root, o_rms, o_normed = sig("o_root", NSTEP), sig("o_rms", NSTEP), sig("o_normed", NSTEP)
        o_turned, o_gated = sig("o_turned", NSTEP), sig("o_gated", NSTEP)
        v_masked, s_delta, s_updated = sig("v_masked", HA), sig("s_delta", HA), sig("s_updated", HA)
        states_stored, states_loaded = sem("states_stored"), sem("states_loaded")
        oh_ready, ol_ready = sig("oh_ready", HA), sig("ol_ready", HA)
        y_turned, y_copied, stored = sem("y_turned"), sem("y_copied"), sem("stored")

        block = ctx.enter_context(nc.Block())

        def out_slot(h):
            return (h % 2, h // 2) if h < HG else ((h - HG) // 2, 2 + (h - HG) % 2)

        def wait(eng, signal, l, i):
            eng.wait_ge(signal.sem, signal.at(l, i))

        def wait_unit(eng, g, u):
            eng.wait_ge(split_used[u % SPLIT_SLOTS], 2 * g + (u // SPLIT_SLOTS + 2))

        def wait_in_tile(eng, l, t):
            j, u = ((t - 1) // UNITS + 1, (t - 1) % UNITS) if t else (0, UNITS - 1)
            wait_unit(eng, l * GROUPS + (WIN + j), u)

        def ahead_of_wait(eng):
            eng.wait_ge(loaded, LOADS)

        X0 = KD + 1
        STATE_DMAS = (2 + QT + HR) * 16
        STATE_LOADS = (QT + HR) * 16
        LOADS = 8 * 16

        @block.sync
        def _(sp):
            sp.dma_start(cst[:, :], consts).then_inc(loaded, 16)
            sp.dma_start(mask_rows[:, :], masks).then_inc(loaded, 16)
            sp.dma_start(x_tok[:, 0:NCH, :], x_prompt[0].rearrange("(c p) d -> p c d", p=P)).then_inc(loaded, 16)
            sp.dma_start(x_tok[0:TS, NCH, :], x_sample.rearrange("b t d -> (b t) d")).then_inc(loaded, 16)
            for row, v in ((0, norm_g.rearrange("l n (k p) -> (l n k) p", p=P)),
                           (V_GLA, gn_gla.rearrange("l (k p) -> (l k) p", p=P)),
                           (V_RET, gn_ret.rearrange("l (k p) -> (l k) p", p=P)),
                           (V_BA, b_a.rearrange("l (k p) -> (l k) p", p=P))):
                sp.dma_start(vec_rows[row:row + v.shape[0], :], v).then_inc(loaded, 16)

            def unit(g, u, rows, kt):
                sp.wait_ge(split_ready[u % SPLIT_SLOTS], 2 * g + (u // SPLIT_SLOTS + 1))
                sp.sem_inc(units_issued, 1)
                sp.dma_start(raw[:, u, 0:kt, :], rows.rearrange("(k p) m -> p k m", p=P)).then_inc(raw_ready[u], 16)

            def k_parts(g, w, l, cols, kts):
                k0 = 0
                for u in range(UNITS):
                    unit(g, u, w[l, k0 * P:(k0 + kts[u]) * P, cols], kts[u])
                    k0 += kts[u]

            def ffn(l, f, w_gu, w_down):
                with sp.Fori(0, UP_GROUPS) as i:
                    for u in range(UNITS):
                        unit(l * GROUPS + UP[f] + i, u, w_gu[l, :, bass.ds(i * (2 * P) + (u // 2 * P + u % 2 * FF), P)], KD)
                with sp.Fori(0, DOWN_GROUPS) as m:
                    k_parts(l * GROUPS + DOWN[f] + m, w_down, l, bass.ds(m * P, P), DOWN_KT)

            with sp.Fori(0, DEPTH) as l:
                ffn(l, 0, w1_gu, w1_down)
                k_parts(l * GROUPS + WIN, w_in, l, slice(A_LO, A_LO + P), ALO_KT)
                for j, (_, col) in enumerate(IN_GROUPS):
                    for u in range(UNITS):
                        unit(l * GROUPS + (WIN + 1 + j), u, w_in[l, :, col + u * P:col + (u + 1) * P], KD)
                with sp.Fori(0, OUT_GROUPS) as j:
                    for u in range(UNITS):
                        unit(l * GROUPS + WOUT + j, u, w_out[l, :, bass.ds(j * (UNITS * P) + u * P, P)], KD)
                ffn(l, 1, w2_gu, w2_down)

        @block.gpsimd
        def _(pool):
            for s in range(SPLIT_SLOTS):
                pool.sem_inc(split_ready[s], 2)
            pool.wait_ge(loaded, LOADS)

            def group(g, kts):
                for u in range(UNITS):
                    s, kt = u % SPLIT_SLOTS, kts[u]
                    pool.wait_ge(raw_ready[u], g * 16 + 16)
                    pool.wait_ge(split_used[s], 2 * g + (u // SPLIT_SLOTS + 1))
                    pool.tensor_tensor(w_hi[:, s, 0:kt, :], raw[:, u, 0:kt, :],
                                       ones.rearrange("p (k m) -> p k m", k=1).broadcast_to([P, kt, P]),
                                       ALU.mult).then_inc(hi_split, 1)
                    pool.wait_ge(hi_split, g * UNITS + (u + 1))
                    pool.tensor_tensor(w_lo[:, s, 0:kt, :], raw[:, u, 0:kt, :], w_hi[:, s, 0:kt, :].bitcast(F32),
                                       ALU.subtract).then_inc(split_ready[s], 1)

            def mask_queries(l):
                wait(pool, o_ready, l, NCH - 2)
                pool.sem_inc(mask_begun, 1)
                pool.memset(acc[:, :], 0.0)
                pool.memset(v_tok[:, 0], 0.0).then_inc(q_zeroed.sem, 1)
                wait(pool, q_zeroed, l, 0)
                q_decay = c("q_decay").rearrange("p (h b t) -> p h b t", h=HR, b=1)[:, :, :, 0:DS]
                for n, src, dst in ((QT, q_dec, q_gla_s), (HR, q_r, q_ret_s)):
                    for b0, nb in ((0, NS - 1), (NS - 1, 1)):
                        t0, at, step_ = TP + b0 * DS, b0 * (TS + DS), (TS + DS if nb > 1 else DS)
                        scale = q_decay if n == HR else ones[:, 0:n * DS].rearrange("p (h b t) -> p h b t", h=n, b=1)
                        o = pool.tensor_tensor(
                            dst[:, :, at:at + nb * step_].rearrange("p h (b t) -> p h b t", b=nb)[:, :, :, 0:DS],
                            src[:, :, t0:t0 + nb * DS].rearrange("p h (b t) -> p h b t", b=nb),
                            scale.broadcast_to([P, n, nb, DS]), ALU.mult)
                o.then_inc(q_masked.sem, 1)

            with pool.Fori(0, DEPTH) as l:
                for f in range(2):
                    with pool.Fori(0, UP_GROUPS) as i:
                        group(l * GROUPS + UP[f] + i, FULL_KT)
                    with pool.Fori(0, DOWN_GROUPS) as i:
                        group(l * GROUPS + DOWN[f] + i, DOWN_KT)
                    if f == 0:
                        group(l * GROUPS + WIN, ALO_KT)
                        with pool.Fori(0, len(IN_GROUPS)) as i:
                            group(l * GROUPS + (WIN + 1) + i, FULL_KT)
                        mask_queries(l)
                        with pool.Fori(0, OUT_GROUPS) as i:
                            group(l * GROUPS + WOUT + i, FULL_KT)

        @block.tensor
        def _(pe):
            for s in range(SPLIT_SLOTS):
                pe.sem_inc(split_used[s], 1)

            def unit(g, u, kt, hi, lo, k0, bank, first, last, before_k=None, after_k=None):
                s = u % SPLIT_SLOTS
                pe.wait_ge(split_ready[s], 2 * g + (u // SPLIT_SLOTS + 3))
                for k in range(kt):
                    if before_k:
                        before_k(k0 + k)
                    for n, (w, v) in enumerate(((w_hi, hi), (w_hi, lo), (w_lo, hi))):
                        for a in range(2):
                            mm = pe.matmul(ps[:, bank + a, 0:HALF], w[:, s, k, :], v[:, k0 + k, a * HALF:(a + 1) * HALF],
                                           start=(first and k == 0 and n == 0), stop=(last and k == kt - 1 and n == 2))
                    if k == kt - 1:
                        mm.then_inc(split_used[s], 1)
                    if after_k:
                        after_k(k0 + k)

            def stats(l, q):
                def add(k):
                    wait(pe, xsq_ready, l, q * KD + k)
                    for a in range(2):
                        mm = pe.matmul(ps[:, 6 + a, 0:HALF], ones, tmp[:, k % 2, a * HALF:(a + 1) * HALF],
                                       start=(k == 0), stop=(k == KD - 1))
                    mm.then_inc(xsq_used.sem, 1)
                return add

            def x_split(l, q):
                return lambda k: wait(pe, xs_ready, l, q * KD + k)

            def up_chunk(l, f, g, par, first=False):
                for j in range(2):
                    peeled = first and j == 0
                    unit(g, 2 * par + j, KD, xs_hi, xs_lo, 0, 4 * par + 2 * j, True, True,
                         before_k=x_split(l, 2 * f) if peeled else None, after_k=stats(l, 2 * f) if peeled else None)

            def ffn(l, f):
                g0 = l * GROUPS + UP[f]
                up_chunk(l, f, g0, 0, first=True)
                wait(pe, pre_log, l, 2 * f)
                up_chunk(l, f, g0, 1)
                with pe.Fori(1, UP_GROUPS) as i:
                    for par in range(2):
                        pe.wait_ge(up_scaled.sem, l * up_scaled.per + i * 2 + (f * KF + par - 1))
                        up_chunk(l, f, g0 + i, par)
                wait(pe, up_scaled, l, f * KF + KF - 2)

                def down_tile(m, par, before_k=None):
                    k0 = 0
                    for u in range(UNITS):
                        unit(l * GROUPS + DOWN[f] + m, u, DOWN_KT[u], h_hi, h_lo, k0, 2 * par, u == 0, u == UNITS - 1,
                             before_k=before_k)
                        k0 += DOWN_KT[u]

                down_tile(0, 0, before_k=lambda k: wait(pe, h_ready, l, f * KF + k))
                down_tile(1, 1)
                with pe.Fori(1, DOWN_GROUPS // 2) as i:
                    for par in range(2):
                        pe.wait_ge(y_read.sem, l * y_read.per + i * 2 + (2 * f * KD + par - 1))
                        down_tile(i * 2 + par, par)
                post_stats(l, 2 * f)

            def post_stats(l, q):
                wait(pe, acc_step, l, q * (KD - 1) + KD - 2)
                for a in range(2):
                    mm = pe.matmul(ps[:, 4 + a, 0:HALF], ones, acc[:, a * HALF:(a + 1) * HALF], start=True, stop=True)
                mm.then_inc(post_sum.sem, 1)

            def in_tile(l, t):
                j, u = (t - 1) // UNITS, (t - 1) % UNITS
                if t >= 2:
                    wait(pe, in_read, l, t - 2)
                unit(l * GROUPS + (WIN + 1 + j), u, KD, xs_hi, xs_lo, 0, 2 * (t % 2), True, True)

            def gate_logits(l):
                wait(pe, in_read, l, 0)
                pe.wait_ge(w_a2_loaded, l * 16 + 16)
                wait(pe, pre_log, l, 1)
                for q in range(QT):
                    for a in range(2):
                        mm = pe.matmul(ps[:, 4 + 2 * q + a, 0:HALF], w_a2_sb[:, q * P:(q + 1) * P],
                                       tmp[0:GR, 0, a * HALF:(a + 1) * HALF], start=True, stop=True)
                mm.then_inc(z_ready.sem, 1)

            def level_scores(l, n):
                m = LEVELS[n]
                wait(pe, prod_ready, l, 2 + n)
                if n == 0:
                    wait(pe, z_min, l, 0)
                if n >= 2:
                    wait(pe, scores_taken, l, n - 1 if LEVELS[n - 1] < DS else n - 2)
                for p in range(2):
                    for c_ in range(NCH):
                        for hh in range(2):
                            at = (c_ * 2 + hh) * (CH // 2)
                            mm = pe.matmul(ps[:, 4 + 2 * (n % 2) + p, at:at + CH // 2],
                                           k_lvl[p * DKG:(p + 1) * DKG, hh, c_ * CH:(c_ + 1) * CH],
                                           q_lvl[p * DKG:(p + 1) * DKG, hh, c_ * CH // 2:(c_ + 1) * CH // 2],
                                           start=True, stop=True)
                if m < DS:
                    ahead_of_wait(pe)
                    wait(pe, scores_taken, l, n - 1)
                    for p in range(2):
                        for hh in range(2):
                            mm = pe.matmul(ps[0:TS, 4 + 2 * ((n + 1) % 2) + p, hh * TS:hh * TS + TS // 2],
                                           k_lvl[p * DKG:(p + 1) * DKG, hh, TP:T],
                                           q_lvl[p * DKG:(p + 1) * DKG, hh, TP // 2:HALF], start=True, stop=True)
                mm.then_inc(scores_ready.sem, 1)

            def diagonal_scores(l, sample):
                ahead_of_wait(pe)
                wait(pe, scores_taken, l, NL if sample else NL - 1)
                for p in range(2):
                    for c_ in ([NCH] if sample else range(NCH)):
                        n = TS if sample else CH
                        for hh in range(2):
                            at = (c_ % 2 * 2 + hh) * CH
                            mm = pe.matmul(ps[0:n, 4 + 2 * p + (0 if sample else c_ // 2), at:at + n],
                                           qk_a[p * DKG:(p + 1) * DKG, QT + hh, c_ * CH:c_ * CH + n],
                                           qk_a[p * DKG:(p + 1) * DKG, hh, c_ * CH:c_ * CH + n], start=True, stop=True)
                mm.then_inc(scores_ready.sem, 1)

            def turn(l, c_):
                t0, n, b0 = c_ * CH, (TS if c_ == S else CH), BANK0[c_]
                if c_ == 0:
                    wait(pe, in_read, l, V_LAST)
                    wait(pe, rotated, l, 2 * HR - 1)
                    wait(pe, scores_taken, l, NL + 1)
                elif c_ == 1:
                    wait(pe, o_normed, l, 0)
                elif c_ == 2:
                    wait(pe, in_read, l, NIN - 1)
                    wait(pe, o_gated, l, 0)
                else:
                    wait(pe, o_normed, l, c_ - 2)
                    wait(pe, o_gated, l, c_ - 2)
                for h in range(HA):
                    pe.transpose(ps[0:n, b0 + h // 4, h % 4 * P:(h % 4 + 1) * P], v_t[:, h, t0:t0 + n], ident)
                for h in range(HR):
                    pe.transpose(ps[0:n, b0 + 2, h * P:(h + 1) * P], k_r[:, h, t0:t0 + n], ident)
                for q in range(QT):
                    mm = pe.transpose(ps[0:n, b0 + 3, q * P:(q + 1) * P], k_dec[:, q, t0:t0 + n], ident)
                mm.then_inc(turned.sem, 1)

            def scores(l, c_):
                t0, n, b0 = c_ * CH, (TS if c_ == S else CH), BANK0[c_]
                wait(pe, v_tok_ready, l, c_)
                wait(pe, k_tok_ready, l, c_)
                for h in range(HR):
                    mm = pe.matmul(ps[0:n, b0, h * n:(h + 1) * n], k_r[:, h, t0:t0 + n], q_r[:, h, t0:t0 + n],
                                   start=True, stop=True)
                mm.then_inc(ret_scores.sem, 1)
                if c_ == S:
                    return
                for h in range(HR):
                    pe.matmul(ps[:, b0 + 1, h * DV:(h + 1) * DV], k_tok[:, h * P:(h + 1) * P], v_tok[:, c_ % 2, HG + h, :],
                              start=True, stop=True)
                for h in range(HG):
                    q, p = h // 2, h % 2
                    at = (HR + q) * P + p * DKG
                    mm = pe.matmul(ps[p * DKG:(p + 1) * DKG, b0 + 3, (QT + q) * DV:(QT + q + 1) * DV],
                                   k_tok[:, at:at + DKG], v_tok[:, c_ % 2, h, :], start=True, stop=True)
                mm.then_inc(state_delta.sem, 1)

            def out(l, c_):
                if c_ == S:
                    out_sample(l)
                    return
                t0, b0 = c_ * CH, BANK0[c_]
                wait(pe, a_ret_ready, l, c_)
                if c_:
                    wait(pe, state_ready, l, c_ - 1)
                    wait(pe, qd_ready, l, c_ - 1)
                for h in range(HG):
                    q, p = h // 2, h % 2
                    a, i = out_slot(h)
                    o = ps[:, b0 + 2 * a, i * DV:(i + 1) * DV]
                    pe.matmul(o, a_gla[:, p, c_, q, :], v_tok[:, c_ % 2, h, :], start=True, stop=(c_ == 0))
                    if c_:
                        pe.matmul(o, q_dec[p * DKG:(p + 1) * DKG, q, t0:t0 + CH],
                                  s_gla[p * DKG:(p + 1) * DKG, (c_ - 1) % 2, q, :], start=False, stop=True)
                for h in range(HR):
                    a, i = out_slot(HG + h)
                    o = ps[:, b0 + 2 * a, i * DV:(i + 1) * DV]
                    mm = pe.matmul(o, a_ret[:, h, :], v_tok[:, c_ % 2, HG + h, :], start=True, stop=(c_ == 0))
                    if c_:
                        mm = pe.matmul(o, q_r[:, h, t0:t0 + CH], s_ret[:, (c_ - 1) % 2, h, :], start=False, stop=True)
                mm.then_inc(o_ready.sem, 1)

            def back(l, c_):
                n = TS if c_ == S else CH
                ahead_of_wait(pe)
                wait(pe, o_normed, l, c_)
                if c_ == 0:
                    wait(pe, in_read, l, NIN - 1)
                elif c_ < S:
                    wait(pe, state_ready, l, c_)
                for h in range(HA):
                    a, i = out_slot(h)
                    mm = pe.transpose(ps[:, BACK_BANKS[c_][h // 4], h % 4 * n:(h % 4 + 1) * n],
                                      o_tok[0:n, 4 * a + i, :], ident[0:n, 0:n])
                mm.then_inc(o_turned.sem, 1)

            def out_sample(l):
                wait(pe, a_ret_ready, l, S)
                wait(pe, q_masked, l, 0)
                pe.wait_ge(states_loaded, l * STATE_LOADS + STATE_LOADS)
                pe.sem_inc(sample_begun, 1)
                for h in range(HA):
                    q, p = h // 2, h % 2
                    a, i = out_slot(h)
                    o = ps[0:TS, BANK0[S] + 2 * a, i * DV:(i + 1) * DV]
                    pe.matmul(o, a_gla_s[:, p, q, :] if h < HG else a_ret_s[:, h - HG, :], v_tok_s[:, h, :], start=True,
                              stop=False)
                    for b in range(NS):
                        if h < HG:
                            rows = slice(p * DKG, (p + 1) * DKG)
                            queries, state = q_gla_s[rows, q, b * TS:(b + 1) * TS], gla_state[rows, q, b, :]
                        else:
                            queries, state = q_ret_s[:, h - HG, b * TS:(b + 1) * TS], ret_state[:, h - HG, b, :]
                        mm = pe.matmul(o, queries, state, start=False, stop=(b == NS - 1))
                mm.then_inc(o_ready.sem, 1)

            def sample_delta(l, i):
                h = UPDATE_ORDER[i]
                wait(pe, v_masked, l, i)
                if i >= 2:
                    wait(pe, s_updated, l, i - 2)
                else:
                    wait(pe, o_gated, l, NCH - 1)
                if h < HG:
                    p = h % 2
                    keys, r0, r1 = k_tok_s[:, HR * P + h * DKG:HR * P + (h + 1) * DKG], p * DKG, (p + 1) * DKG
                else:
                    keys, r0, r1 = k_tok_s[:, (h - HG) * P:(h - HG + 1) * P], 0, P
                for a in range(2):
                    mm = pe.matmul(ps[r0:r1, 4 + 2 * (i % 2) + a, :], keys,
                                   v_by_batch(i)[:, a * NS // 2:(a + 1) * NS // 2, :], start=True, stop=True)
                mm.then_inc(s_delta.sem, 1)

            def step(l, kind, c_):
                {"turn": turn, "scores": scores, "out": out, "back": back}[kind](l, c_)

            def out_projection(l):
                for m in range(KD):
                    if m >= 2:
                        wait(pe, y_read, l, KD + m - 2)
                    unit(l * GROUPS + (WOUT + m // UNITS), m % UNITS, KD, o_hi, o_lo, 0, 2 * (m % 2), True, True,
                         before_k=(lambda k: wait(pe, ol_ready, l, k)) if m == 0 else None)
                    sample_delta(l, m)
                wait(pe, s_updated, l, HA - 1)
                post_stats(l, 1)

            pe.wait_ge(loaded, LOADS)
            pe.transpose(ps[:, 5, 0:NV], vec_rows[0:NV, :], ident[0:NV, 0:NV]).then_inc(vec_turned, 1)
            for d in range(KD):
                mm = pe.transpose(ps[:, 4, d * TS:(d + 1) * TS], x_tok[0:TS, NCH, d * P:(d + 1) * P], ident[0:TS, 0:TS])
            mm.then_inc(x_turned, 1)
            for d in range(KD):
                if d >= 4:
                    pe.wait_ge(x_copied, d - 2)
                for c_ in range(NCH):
                    mm = pe.transpose(ps[:, d % 4, c_ * P:(c_ + 1) * P], x_tok[:, c_, d * P:(d + 1) * P], ident)
                mm.then_inc(x_turned, 1)

            with pe.Fori(0, DEPTH) as l:
                ffn(l, 0)
                k0 = 0
                for u in range(UNITS):
                    unit(l * GROUPS + WIN, u, ALO_KT[u], xs_hi, xs_lo, k0, 0, u == 0, u == UNITS - 1,
                         before_k=x_split(l, 1), after_k=stats(l, 1))
                    k0 += ALO_KT[u]
                for t in range(1, NIN):
                    in_tile(l, t)
                    if t == UNITS:
                        gate_logits(l)
                    if t in SCORE_SLOT:
                        n = SCORE_SLOT[t]
                        if n < NL:
                            level_scores(l, n)
                        else:
                            diagonal_scores(l, sample=(n > NL))
                    if t in IN_SLOT_STEPS:
                        step(l, *IN_SLOT_STEPS[t])
                for kind, c_ in TAIL_STEPS:
                    step(l, kind, c_)
                out_projection(l)
                ffn(l, 1)

            for c_ in range(NCH + 1):
                n = P if c_ < NCH else TS
                for a in range(2):
                    i = 2 * c_ + a
                    if i == 0:
                        pe.wait_ge(x_ready.sem, X0 + DEPTH * x_ready.per)
                    if i >= 4:
                        pe.wait_ge(y_copied, i - 3)
                    for d in range(4):
                        mm = pe.transpose(ps[0:n, i % 4, d * P:(d + 1) * P], x[:, 4 * a + d, c_ * P:c_ * P + n], ident)
                    mm.then_inc(y_turned, 1)

        @block.scalar
        def _(act):
            def pre_tile(l, q, k, done):
                act.wait_ge(x_ready.sem, done)
                act.activation(xs_hi[:, k, :], x[:, k, :], ACT.Copy, scale=gain(l, 2 * q, k)).then_inc(xh_ready.sem, 1)
                if k >= 2:
                    wait(act, xsq_used, l, q * KD + k - 2)
                act.activation(tmp[:, k % 2, :], x[:, k, :], ACT.Square).then_inc(xsq_ready.sem, 1)

            def inverse_root(l, q, dst, bank_pair, log_sig, ready_sig):
                act.activation(halves(dst), pair(bank_pair), ACT.Ln, bias=eps, scale=1.0 / D).then_inc(log_sig.sem, 1)
                wait(act, log_sig, l, q)
                act.activation(dst, dst, ACT.Exp, scale=-0.5).then_inc(ready_sig.sem, 1)

            def pre_norm(l, q):
                for k in range(KD):
                    pre_tile(l, q, k, l * x_ready.per + (X0 if q == 0 else X0 + (q - 1) * KD + k + 1))
                wait(act, xsq_used, l, q * KD + KD - 1)
                inverse_root(l, q, rstd_pre[:, :], 3, pre_log, pre_ready)

            def up(l, f):
                with act.Fori(0, KF) as c_:
                    at = l * gate_scaled.per + c_ + (f * KF + 1)
                    act.wait_ge(gate_scaled.sem, at)
                    act.activation(tmp[:, 0, :], tmp[:, 0, :], ACT.Silu).then_inc(gate_silu.sem, 1)
                    act.wait_ge(h_prod.sem, at)
                    act.activation(h_hi[:, bass.ds(c_, 1), :], tmp[:, 0:1, :], ACT.Copy).then_inc(hh_ready.sem, 1)

            def post_norm(l, q, g0, last_unit, after_tile=None):
                for m in range(KD):
                    wait_unit(act, *last_unit(g0, m))
                    if m >= 2:
                        wait(act, acc_step, l, q * (KD - 1) + max(m - 2, 1) - 1)
                    act.activation(halves((y_out if q == 1 else y)[:, m, :]), pair(m % 2), ACT.Copy)
                    act.activation(halves(sq[:, m % 2, :]), pair(m % 2), ACT.Square).then_inc(y_read.sem, 1)
                    if after_tile and m:
                        after_tile(l, m - 1)
                if after_tile:
                    after_tile(l, KD - 1)
                wait(act, post_sum, l, q)
                inverse_root(l, q, acc[:, :], 2, post_log, post_ready)

            down_unit = lambda g0, m: (g0 + m, UNITS - 1)
            out_unit = lambda g0, m: (g0 + m // UNITS, m % UNITS)

            def swap_halves(l, t):
                n = t - ROT0
                src, hd = (q_r if n < HR else k_r)[:, n % HR, :], DKR // 2
                wait(act, in_read, l, t)
                if n:
                    wait(act, rotated, l, n - 1)
                act.activation(tmp[0:hd, 1, :], src[hd:2 * hd, :], ACT.Copy)
                act.activation(tmp[hd:2 * hd, 1, :], src[0:hd, :], ACT.Copy).then_inc(swapped.sem, 1)

            def act_step(l, kind, c_):
                n, b0 = TS if c_ == S else CH, BANK0[c_]
                if kind == "turn":
                    wait(act, turned, l, c_)
                    if 0 < c_ < S:
                        wait(act, state_delta, l, c_ - 1)
                    if 2 <= c_ < S:
                        wait(act, o_ready, l, c_ - 2)
                    vt, kt = (v_tok_s, k_tok_s) if c_ == S else (v_tok[:, c_ % 2], k_tok)
                    for i in range(2):
                        act.activation(vt[0:n, 4 * i:4 * i + 4, :],
                                       ps[0:n, b0 + i, :].rearrange("p (h v) -> p h v", v=DV), ACT.Copy)
                    act.activation(kt[0:n, HR * P:(HR + QT) * P], ps[0:n, b0 + 3, 0:QT * P], ACT.Copy)\
                        .then_inc(v_tok_ready.sem, 1)
                elif kind == "scores" and c_ == NCH - 1:
                    wait(act, state_ready, l, c_)
                    act.dma_start(gla_p[l, 0].rearrange("(q p) k v -> (p k) q v", p=2), s_gla[:, c_ % 2, :, :])\
                        .then_inc(states_stored, 16)
                    act.dma_start(ret_p[l, 0].rearrange("h k v -> k h v"), s_ret[:, c_ % 2, :, :])\
                        .then_inc(states_stored, 16)
                elif kind == "out":
                    wait(act, o_ready, l, c_)
                    for a in range(2):
                        o = act.activation(sq[0:n, a, 0:4 * DV], ps[0:n, b0 + 2 * a, :], ACT.Square)
                    o.then_inc(o_sq.sem, 1)
                    wait(act, o_ms, l, c_)
                    act.activation(rms[0:n, 1, :], rms[0:n, 0, :], ACT.Sqrt, bias=eps[0:n], scale=1.0 / DV)\
                        .then_inc(o_root.sem, 1)

            def store_sample_state(l, i):
                h = UPDATE_ORDER[i]
                if h >= HG:
                    wait(act, s_updated, l, i)
                    act.dma_start(ret_s[l, :, h - HG].rearrange("b k v -> k b v"), ret_state[:, h - HG, :, :])\
                        .then_inc(states_stored, 16)
                elif h % 2:
                    wait(act, s_updated, l, i)
                    act.dma_start(gla_s[l, :, h - 1:h + 1].rearrange("b p k v -> (p k) b v"),
                                  gla_state[:, h // 2, :, :]).then_inc(states_stored, 16)

            act.wait_ge(vec_turned, 1)
            act.activation(vecs[:, :], ps[:, 5, 0:NV], ACT.Copy).then_inc(vec_ready, 1)
            act.wait_ge(vec_ready, 1)
            act.activation(half_gain[:, :], vecs[:, 0:DEPTH * NN * KD], ACT.Copy, scale=0.5).then_inc(vec_ready, 1)
            with act.Fori(0, DEPTH) as l:
                pre_norm(l, 0)
                up(l, 0)
                post_norm(l, 0, l * GROUPS + DOWN[0], down_unit)
                act.dma_start(w_a2_sb[:, :], w_a2[l]).then_inc(w_a2_loaded, 16)
                pre_norm(l, 1)
                wait(act, z_ready, l, 0)
                for q in range(QT):
                    o = act.activation(halves(e_buf[:, q, :]), pair(2 + q), ACT.Abs,
                                       bias=vecs[:, bass.ds(l * QT + (V_BA + q), 1)])
                o.then_inc(z_abs.sem, 1)
                wait(act, z_abs, l, 0)
                act.activation(e_buf[:, :, :], e_buf[:, :, :], ACT.Exp, scale=-1.0).then_inc(z_exp.sem, 1)
                wait(act, z_exp, l, 0)
                act.activation(e_buf[:, :, :], e_buf[:, :, :], ACT.Ln, bias=ones[:, 0:1]).then_inc(z_ln.sem, 1)
                for t in range(SCAN_SLOT, NIN):
                    if ROT0 <= t < ROT0 + 2 * HR:
                        swap_halves(l, t)
                    if t in DIFF_SLOT:
                        s = DIFF_SLOT[t]
                        if s == "q":
                            wait(act, b_ready, l, 0)
                            act.activation(e_buf[:, :, :], b_cum[:, :, :], ACT.Exp, scale=1.0 / GATE_TEMP)\
                                .then_inc(exp_ready.sem, 1)
                        else:
                            n = 0 if s == "k" else 1 + s
                            wait(act, diff_ready, l, n)
                            act.activation(e_buf[:, :, :], e_buf[:, :, :], ACT.Exp, scale=1.0 / GATE_TEMP)\
                                .then_inc(exp_ready.sem, 1)
                    if t >= G0:
                        wait(act, in_read, l, t)
                        act.activation(g_t[:, t - G0, :], g_t[:, t - G0, :], ACT.Silu).then_inc(silu_done.sem, 1)
                    if t in IN_SLOT_STEPS:
                        act_step(l, *IN_SLOT_STEPS[t])
                wait(act, in_read, l, NIN - 1)
                for h in range(HR):
                    act.dma_start(ret_state[:, h, :, :], state_ret[l, :, h].rearrange("b k v -> k b v"))\
                        .then_inc(states_loaded, 16)
                for q in range(QT):
                    act.dma_start(gla_state[:, q, :, :], state_gla[l, :, 2 * q:2 * q + 2]
                                  .rearrange("b p k v -> (p k) b v")).then_inc(states_loaded, 16)
                for kind, c_ in TAIL_STEPS:
                    act_step(l, kind, c_)
                wait(act, o_gated, l, S)
                for h in range(HA):
                    act.activation(o_hi[:, h, :], v_t[:, h, :], ACT.Copy).then_inc(oh_ready.sem, 1)
                post_norm(l, 1, l * GROUPS + WOUT, out_unit, after_tile=store_sample_state)
                act.wait_ge(states_stored, l * STATE_DMAS + STATE_DMAS)
                pre_norm(l, 2)
                up(l, 1)
                post_norm(l, 2, l * GROUPS + DOWN[1], down_unit)

            for i in range(2 * (NCH + 1)):
                c_, a = i // 2, i % 2
                n = P if c_ < NCH else TS
                act.wait_ge(y_turned, i + 1)
                act.activation(y_tok[0:n, c_, a * 512:(a + 1) * 512], ps[0:n, i % 4, :], ACT.Copy).then_inc(y_copied, 1)
                if a:
                    act.wait_ge(y_copied, i + 1)
                    act.dma_start(y_prompt[0, c_ * P:(c_ + 1) * P, :] if c_ < NCH else
                                  y_sample.rearrange("b t d -> (b t) d"), y_tok[0:n, c_, :]).then_inc(stored, 16)
            act.wait_ge(stored, 16 * (NCH + 1))
            act.wait_ge(states_stored, DEPTH * STATE_DMAS)

        @block.vector
        def _(dve):
            def pre_low(l, q, k):
                wait(dve, xh_ready, l, q * KD + k)
                dve.scalar_tensor_tensor(out=xs_lo[:, k, :], in0=x[:, k, :], scalar=gain(l, 2 * q, k),
                                         in1=xs_hi[:, k, :].bitcast(F32), op0=ALU.mult, op1=ALU.subtract)\
                   .then_inc(xs_ready.sem, 1)

            def up(l, f):
                with dve.Fori(0, UP_GROUPS) as i:
                    for par in range(2):
                        at = l * gate_scaled.per + i * 2 + (f * KF + par + 1)
                        wait(dve, pre_ready, l, 2 * f)
                        wait_unit(dve, l * GROUPS + UP[f] + i, 2 * par + 1)
                        dve.tensor_tensor(halves(tmp[:, 0, :]), pair(2 * par), halves(rstd_pre[:, :]), ALU.mult)\
                           .then_inc(gate_scaled.sem, 1)
                        dve.tensor_tensor(halves(tmp[:, 1, :]), pair(2 * par + 1), halves(rstd_pre[:, :]), ALU.mult)\
                           .then_inc(up_scaled.sem, 1)
                        dve.wait_ge(gate_silu.sem, at)
                        dve.wait_ge(up_scaled.sem, at)
                        dve.tensor_tensor(tmp[:, 0, :], tmp[:, 0, :], tmp[:, 1, :], ALU.mult).then_inc(h_prod.sem, 1)
                        dve.wait_ge(hh_ready.sem, at)
                        tile = bass.ds(i * 2 + par, 1)
                        dve.tensor_tensor(h_lo[:, tile, :], tmp[:, 0:1, :], h_hi[:, tile, :].bitcast(F32), ALU.subtract)\
                           .then_inc(h_ready.sem, 1)
                        dve.wait_ge(h_ready.sem, at)

            def add_squares(l, q, m):
                if m == 0:
                    return
                wait(dve, y_read, l, q * KD + m)
                if m > 1:
                    wait(dve, acc_step, l, q * (KD - 1) + m - 2)
                dve.tensor_tensor(acc[:, :], sq[:, 0, :] if m == 1 else acc[:, :], sq[:, m % 2, :], ALU.add)\
                   .then_inc(acc_step.sem, 1)

            def residual(l, q, pre=None):
                wait(dve, post_ready, l, q)
                for k in range(KD):
                    yk = (y_out if q == 1 else y)[:, k, :]
                    dve.tensor_tensor(yk, yk, acc[:, :], ALU.mult).then_inc(y_scaled.sem, 1)
                    if pre is not None and k:
                        pre_low(l, pre, k - 1)
                    wait(dve, y_scaled, l, q * KD + k)
                    dve.scalar_tensor_tensor(out=x[:, k, :], in0=yk, scalar=post_gain(l, q, k), in1=x[:, k, :],
                                             op0=ALU.mult, op1=ALU.add).then_inc(x_ready.sem, 1)
                if pre is not None:
                    pre_low(l, pre, KD - 1)

            def take_tile(l, t):
                wait_in_tile(dve, l, t)
                out, src, r, scale = None, pair(t % 2), halves(rstd_pre[:, :]), None
                if t == 0:
                    dve.tensor_tensor(halves(tmp[0:GR, 0, :]), src[0:GR], r[0:GR], ALU.mult).then_inc(in_read.sem, 1)
                    return
                kind, i = IN_GROUPS[(t - 1) // UNITS][0], (t - 1) % UNITS
                out = {"qk_a": qk_a, "v_a": v_t, "q_r": q_r, "k_r": k_r, "v_r": v_t, "g_a": g_t, "g_r": g_t}[kind]
                i += {"v_r": HG, "g_r": HG}.get(kind, 0)
                scale = DKG ** -0.5 if kind == "qk_a" and i < QT else 1.0
                dve.scalar_tensor_tensor(out=halves(out[:, i, :]), in0=src, scalar=scale, in1=r, op0=ALU.mult,
                                         op1=ALU.mult).then_inc(in_read.sem, 1)

            def rotate(l, n):
                buf, scale = (q_r, 1.0) if n < HR else (k_r, DKR ** -0.5)
                wait(dve, swapped, l, n)
                dve.scalar_tensor_tensor(out=tmp[:, 1, :], in0=tmp[:, 1, :], scalar=scale, in1=sin, op0=ALU.mult,
                                         op1=ALU.mult)
                dve.scalar_tensor_tensor(out=buf[:, n % HR, :], in0=buf[:, n % HR, :], scalar=scale, in1=cos,
                                         op0=ALU.mult, op1=ALU.mult).then_inc(rot_parts.sem, 1)
                wait(dve, rot_parts, l, n)
                dve.tensor_tensor(buf[:, n % HR, :], buf[:, n % HR, :], tmp[:, 1, :], ALU.add).then_inc(rotated.sem, 1)

            def by_block(buf, w, m):
                return buf[:, :, 0:w].rearrange("p q (n h m) -> p q n h m", h=2, m=m)

            def exponents(l, s):
                if s == "q":
                    return
                wait(dve, prod_ready, l, STEPS.index(s) - 1)
                if s == "k":
                    for t0, w, m in ((0, TP, CH), (TP, TS, DS)):
                        b = b_cum[:, :, t0:t0 + w].rearrange("p q (n m) -> p q n m", m=m)
                        e = e_buf[:, :, t0:t0 + w].rearrange("p q (n m) -> p q n m", m=m)
                        o = dve.tensor_tensor(e, b[:, :, :, m - 1:m].broadcast_to([P, QT, w // m, m]), b, ALU.subtract)
                    o.then_inc(diff_ready.sem, 1)
                    return
                m = LEVELS[s]
                w = T if m < DS else TP
                b, e = by_block(b_cum, w, m), by_block(e_buf, w, m)
                ref = b[:, :, :, 0, m - 1:m].broadcast_to([P, QT, w // (2 * m), m])
                dve.tensor_tensor(e[:, :, :, 0, :], ref, b[:, :, :, 0, :], ALU.subtract)
                dve.tensor_tensor(e[:, :, :, 1, :], b[:, :, :, 1, :], ref, ALU.subtract).then_inc(diff_ready.sem, 1)

            def products(l, s):
                queries, keys = qk_a[:, 0:QT, :], qk_a[:, QT:2 * QT, :]
                j = STEPS.index(s)
                wait(dve, exp_ready, l, j)
                if s == "q":
                    dve.tensor_copy(chunk_decay[:, :, 0:NCH], e_buf[:, :, CH - 1:TP:CH])
                    dve.tensor_copy(chunk_decay[:, :, NCH:NCH + NS], e_buf[:, :, TP + DS - 1:T:DS])
                    dve.tensor_tensor(q_dec[:, :, :], queries, e_buf[:, :, :], ALU.mult).then_inc(prod_ready.sem, 1)
                elif s == "k":
                    dve.tensor_tensor(k_dec[:, :, :], keys, e_buf[:, :, :], ALU.mult).then_inc(prod_ready.sem, 1)
                else:
                    m = LEVELS[s]
                    w = T if m < DS else TP
                    if s:
                        wait(dve, scores_ready, l, s - 1)
                    dve.tensor_tensor(k_lvl[:, :, 0:w], keys[:, :, 0:w], e_buf[:, :, 0:w], ALU.mult)
                    dve.tensor_tensor(q_lvl[:, :, 0:w // 2].rearrange("p q (n m) -> p q n m", m=m),
                                      by_block(queries, w, m)[:, :, :, 1, :], by_block(e_buf, w, m)[:, :, :, 1, :],
                                      ALU.mult).then_inc(prod_ready.sem, 1)

            def take_scores(l, n):
                ahead_of_wait(dve)
                wait(dve, scores_ready, l, n)
                if n == 0:
                    wait(dve, a_zeroed, l, 0)
                for p in range(2):
                    if n < NL:
                        m = LEVELS[n]
                        mask = msk[:, n * (CH // 2):(n + 1) * (CH // 2)]
                        nb = CH // (2 * m)
                        o = dve.copy_predicated(
                            a_gla[:, p].rearrange("p c x (n h m) -> p (c x) n h m", h=2, m=m)[:, :, :, 1, :],
                            mask.rearrange("p (x n m) -> p x n m", x=1, m=m).broadcast_to([P, 2 * NCH, nb, m]),
                            ps[:, 4 + 2 * (n % 2) + p, :].rearrange("p (x n m) -> p x n m", x=2 * NCH, m=m))
                        if m < DS:
                            nb = TS // (2 * m)
                            o = dve.copy_predicated(
                                a_gla_s[:, p].rearrange("p x (n h m) -> p x n h m", h=2, m=m)[:, :, :, 1, :],
                                mask[0:TS, 0:TS // 2].rearrange("p (x n m) -> p x n m", x=1, m=m)
                                .broadcast_to([TS, 2, nb, m]),
                                ps[0:TS, 4 + 2 * ((n + 1) % 2) + p, 0:2 * TS]
                                .rearrange("p (x t) -> p x t", x=2)[:, :, 0:TS // 2]
                                .rearrange("p x (n m) -> p x n m", m=m))
                    elif n == NL:
                        mask = msk[:, NL * (CH // 2):NL * (CH // 2) + CH].rearrange("p (x t) -> p x t", x=1)
                        o = dve.copy_predicated(a_gla[:, p].rearrange("p c x t -> p (c x) t"),
                                                mask.broadcast_to([P, 2 * NCH, CH]),
                                                ps[:, 4 + 2 * p:6 + 2 * p, :].rearrange("p a (x t) -> p (a x) t", t=CH))
                    else:
                        mask = msk[0:TS, NL * (CH // 2):NL * (CH // 2) + TS].rearrange("p (x t) -> p x t", x=1)
                        o = dve.copy_predicated(a_gla_s[:, p], mask.broadcast_to([TS, 2, TS]),
                                                ps[0:TS, 4 + 2 * p, 0:2 * CH].rearrange("p (x t) -> p x t", t=CH)[:, :, 0:TS])
                o.then_inc(scores_taken.sem, 1)

            def turn_keys(l, c_):
                wait(dve, turned, l, c_)
                if 0 < c_ < S:
                    wait(dve, state_delta, l, c_ - 1)
                if c_ == S:
                    wait(dve, v_tok_ready, l, c_)
                n, b0 = TS if c_ == S else CH, BANK0[c_]
                kt, decay = (k_tok_s, c("k_decay_s", TS)) if c_ == S else (k_tok, c("k_decay"))
                o = dve.tensor_tensor(kt[0:n, 0:HR * P].rearrange("p (h k) -> p h k", h=HR),
                                      ps[0:n, b0 + 2, :].rearrange("p (h k) -> p h k", h=HR),
                                      decay.rearrange("p (h k) -> p h k", k=1).broadcast_to([n, HR, P]), ALU.mult)
                o.then_inc(k_tok_ready.sem, 1)

            def decay_scores(l, c_):
                t0 = c_ * CH
                wait(dve, ret_scores, l, c_)
                if c_ == S:
                    dve.tensor_tensor(a_ret_s.rearrange("p h t -> p (h t)"), ps[0:TS, 0, 0:HR * TS],
                                      c("decay_mask_s", TS), ALU.mult).then_inc(a_ret_ready.sem, 1)
                else:
                    if c_:
                        wait(dve, o_ready, l, c_ - 1)
                    dve.tensor_tensor(a_ret.rearrange("p h t -> p (h t)"), ps[:, BANK0[c_], :], c("decay_mask"),
                                      ALU.mult).then_inc(a_ret_ready.sem, 1)
                if 0 < c_ < S:
                    q = q_r[:, :, t0:t0 + CH]
                    dve.tensor_tensor(q, q, c("q_decay").rearrange("p (h t) -> p h t", h=HR), ALU.mult)\
                       .then_inc(qd_ready.sem, 1)

            def update_states(l, c_):
                wait(dve, state_delta, l, c_)
                new, old = c_ % 2, (c_ - 1) % 2
                if c_ >= 1:
                    wait(dve, o_ready, l, c_ - 1)
                    wait(dve, state_ready, l, c_ - 1)
                b0 = BANK0[c_]
                for q in range(QT):
                    delta = ps[:, b0 + 3, (QT + q) * DV:(QT + q + 1) * DV]
                    if c_ == 0:
                        dve.tensor_copy(s_gla[:, new, q, :], delta)
                    else:
                        dve.scalar_tensor_tensor(out=s_gla[:, new, q, :], in0=s_gla[:, old, q, :],
                                                 scalar=chunk_decay[:, q, c_:c_ + 1], in1=delta, op0=ALU.mult, op1=ALU.add)
                for h in range(HR):
                    delta = ps[:, b0 + 1, h * DV:(h + 1) * DV]
                    if c_ == 0:
                        o = dve.tensor_copy(s_ret[:, new, h, :], delta)
                    else:
                        o = dve.scalar_tensor_tensor(out=s_ret[:, new, h, :], in0=s_ret[:, old, h, :],
                                                     scalar=gammas[h] ** CH, in1=delta, op0=ALU.mult, op1=ALU.add)
                o.then_inc(state_ready.sem, 1)

            def norm_outputs(l, c_):
                n = TS if c_ == S else CH
                wait(dve, o_sq, l, c_)
                if c_:
                    wait(dve, o_normed, l, c_ - 1)
                dve.tensor_reduce(rms[0:n, 0, :], sq[0:n, :, 0:4 * DV].rearrange("p a (h v) -> p a h v", v=DV), AX.X,
                                  ALU.add).then_inc(o_ms.sem, 1)
                wait(dve, o_root, l, c_)
                dve.reciprocal(rms[0:n, 0, :], rms[0:n, 1, :]).then_inc(o_rms.sem, 1)
                wait(dve, o_rms, l, c_)
                if c_:
                    wait(dve, o_turned, l, c_ - 1)
                for a in range(2):
                    o = dve.tensor_tensor(o_tok[0:n, 4 * a:4 * a + 4, :],
                                          ps[0:n, BANK0[c_] + 2 * a, :].rearrange("p (h v) -> p h v", v=DV),
                                          rms[0:n, 0, 4 * a:4 * a + 4].rearrange("p (h v) -> p h v", v=1)
                                          .broadcast_to([n, 4, DV]), ALU.mult)
                o.then_inc(o_normed.sem, 1)

            def gate_outputs(l, c_):
                t0, n = c_ * CH, TS if c_ == S else CH
                wait(dve, o_turned, l, c_)
                wait(dve, gates_ready, l, HA - 1)
                for a in range(2):
                    o = dve.tensor_tensor(v_t[:, 4 * a:4 * a + 4, t0:t0 + n],
                                          ps[:, BACK_BANKS[c_][a], 0:4 * n].rearrange("p (h t) -> p h t", t=n),
                                          g_t[:, 4 * a:4 * a + 4, t0:t0 + n], ALU.mult)
                o.then_inc(o_gated.sem, 1)

            def head_gain(l, h):
                wait(dve, silu_done, l, h)
                v = bass.ds(l * HG + ((V_GLA if h < HG else V_RET - HG) + h), 1)
                dve.tensor_scalar(g_t[:, h, :], g_t[:, h, :], vecs[:, v], None, ALU.mult).then_inc(gates_ready.sem, 1)

            def mask_values(l, i):
                h = UPDATE_ORDER[i]
                if i >= 2:
                    wait(dve, s_delta, l, i - 2)
                dve.tensor_tensor(v_by_batch(i), v_tok_s[:, h:h + 1, :].broadcast_to([TS, NS, DV]),
                                  c("batch_mask", TS).rearrange("p (b x) -> p b x", x=1).broadcast_to([TS, NS, DV]),
                                  ALU.mult).then_inc(v_masked.sem, 1)

            def update_sample_state(l, i):
                h = UPDATE_ORDER[i]
                wait(dve, s_delta, l, i)
                delta = ps[:, 4 + 2 * (i % 2):6 + 2 * (i % 2), :]
                if h < HG:
                    rows, q = slice(h % 2 * DKG, (h % 2 + 1) * DKG), h // 2
                    for b in range(NS):
                        o = dve.scalar_tensor_tensor(out=gla_state[rows, q, b, :], in0=gla_state[rows, q, b, :],
                                                     scalar=chunk_decay[rows, q, NCH + b:NCH + b + 1],
                                                     in1=delta[rows, b // 4, b % 4 * DV:(b % 4 + 1) * DV],
                                                     op0=ALU.mult, op1=ALU.add)
                else:
                    s = ret_state[:, h - HG, :, :].rearrange("p (a b) v -> p a (b v)", a=2)
                    o = dve.scalar_tensor_tensor(out=s, in0=s, scalar=gammas[h - HG] ** DS, in1=delta, op0=ALU.mult,
                                                 op1=ALU.add)
                o.then_inc(s_updated.sem, 1)

            def dve_step(l, kind, c_):
                if kind == "turn":
                    turn_keys(l, c_)
                elif kind == "scores":
                    decay_scores(l, c_)
                    if c_ < S:
                        update_states(l, c_)
                elif kind == "out":
                    norm_outputs(l, c_)
                elif kind == "back":
                    gate_outputs(l, c_)

            dve.wait_ge(loaded, LOADS)
            dve.tensor_copy(msk[:, :], mask_rows[:, :])
            dve.wait_ge(x_turned, 1)
            dve.tensor_copy(x[:, :, TP:T], ps[:, 4, 0:KD * TS].rearrange("p (d t) -> p d t", t=TS)).then_inc(x_copied, 1)
            for d in range(KD):
                dve.wait_ge(x_turned, d + 2)
                dve.tensor_copy(x[:, d, 0:TP], ps[:, d % 4, :]).then_inc(x_copied, 1)
            dve.wait_ge(x_copied, X0)
            dve.sem_inc(x_ready.sem, X0)
            with dve.Fori(0, DEPTH) as l:
                for k in range(KD):
                    pre_low(l, 0, k)
                up(l, 0)
                for m in range(KD):
                    add_squares(l, 0, m)
                residual(l, 0, pre=1)
                for t in range(NIN):
                    if t == 0:
                        wait(dve, pre_ready, l, 1)
                    take_tile(l, t)
                    if t == UNITS:
                        wait(dve, z_abs, l, 0)
                        for q in range(QT):
                            o = dve.tensor_scalar(halves(k_lvl[:, q, :]), pair(2 + q), vecs[:, bass.ds(l * QT + (V_BA + q), 1)], 0.0,
                                                  ALU.add, ALU.min)
                        o.then_inc(z_min.sem, 1)
                        dve.memset(a_gla.rearrange("p a c x t -> p (a c x t)"), 0.0)
                        dve.memset(a_gla_s.rearrange("p a x t -> p (a x t)"), 0.0).then_inc(a_zeroed.sem, 1)
                    if t == SCAN_SLOT:
                        wait(dve, z_ln, l, 0)
                        wait(dve, z_min, l, 0)
                        dve.tensor_tensor(k_lvl[:, :, :], k_lvl[:, :, :], e_buf[:, :, :], ALU.subtract)\
                           .then_inc(log_gate.sem, 1)
                        wait(dve, log_gate, l, 0)
                        for q in range(QT):
                            o = dve.tensor_tensor_scan(b_cum[:, q, :], c("scan_keep"), k_lvl[:, q, :], 0.0, ALU.mult, ALU.add)
                        o.then_inc(b_ready.sem, 1)
                    if ROT0 < t <= ROT0 + 2 * HR:
                        rotate(l, t - 1 - ROT0)
                    if t in TAKE_SLOT:
                        take_scores(l, TAKE_SLOT[t])
                    if t in PROD_SLOT:
                        products(l, PROD_SLOT[t])
                    if t in DIFF_SLOT:
                        exponents(l, DIFF_SLOT[t])
                    if G0 < t:
                        head_gain(l, t - 1 - G0)
                    if t in IN_SLOT_STEPS:
                        dve_step(l, *IN_SLOT_STEPS[t])
                head_gain(l, HA - 1)
                for kind, c_ in TAIL_STEPS:
                    dve_step(l, kind, c_)
                for h in range(HA):
                    wait(dve, oh_ready, l, h)
                    dve.tensor_tensor(o_lo[:, h, :], v_t[:, h, :], o_hi[:, h, :].bitcast(F32), ALU.subtract)\
                       .then_inc(ol_ready.sem, 1)
                mask_values(l, 0)
                mask_values(l, 1)
                for m in range(KD):
                    add_squares(l, 1, m)
                    update_sample_state(l, m)
                    if m + 2 < HA:
                        mask_values(l, m + 2)
                residual(l, 1, pre=2)
                up(l, 1)
                for m in range(KD):
                    add_squares(l, 2, m)
                residual(l, 2)


_INS = ["x_prompt", "x_sample", "state_gla", "state_ret", "norm_g", "w1_gu", "w1_down", "w2_gu", "w2_down",
        "w_in", "w_a2", "b_a", "gn_gla", "gn_ret", "w_out"]
PAST_LEN = 4096
ROPE_BASE = 10000.0


def _tables(np, HR, DKR, TP, NS, DS):
    TS = NS * DS
    T = TP + TS
    cols, n = const_layout(HR, T, TS, NS, 0)
    tab = np.zeros((P, n), np.float32)

    def put(name, a):
        lo, hi = cols[name]
        tab[0:a.shape[0], lo:hi] = a.reshape(a.shape[0], hi - lo)

    put("ident", np.eye(P))
    put("ones", np.ones((P, P)))
    half = DKR // 2
    freq = np.float32(ROPE_BASE) ** (-np.arange(half, dtype=np.float32) / np.float32(half))
    pos = np.concatenate([np.arange(TP), np.tile(PAST_LEN + np.arange(DS), NS)]).astype(np.float32)
    ang = (freq[:, None] * pos[None, :]).astype(np.float32).astype(np.float64)
    put("cos", np.concatenate([np.cos(ang), np.cos(ang)]))
    put("sin", np.concatenate([-np.sin(ang), np.sin(ang)]))
    gam = 1.0 - 2.0 ** (-5.0 - np.arange(HR))
    i = np.arange(CH)
    d = i[None, :] - i[:, None]
    put("decay_mask", np.stack([np.where(d >= 0, g ** np.maximum(d, 0), 0.0) for g in gam], 1))
    put("q_decay", np.broadcast_to(np.stack([g ** (i + 1) for g in gam])[None], (P, HR, CH)))
    put("k_decay", np.stack([g ** (CH - 1 - i) for g in gam], 1))
    j = np.arange(TS)
    put("k_decay_s", np.stack([g ** (DS - 1 - j % DS) for g in gam], 1))
    d = j[None, :] - j[:, None]
    same = j[None, :] // DS == j[:, None] // DS
    put("decay_mask_s", np.stack([np.where(same & (d >= 0), g ** np.maximum(d, 0), 0.0) for g in gam], 1))
    keep = np.ones((P, T))
    keep[:, 0:TP:CH] = 0.0
    keep[:, TP::DS] = 0.0
    put("scan_keep", keep)
    put("batch_mask", (j[:, None] // DS == np.arange(NS)[None, :]).astype(np.float32))
    put("eps", np.full((P, 1), EPS))
    parts = []
    t = np.arange(CH // 2)
    for m in LEVELS:
        parts.append((i[:, None] // (2 * m) == t[None, :] // m) & (i[:, None] % (2 * m) < m))
    parts.append(np.eye(CH, dtype=bool))
    return tab, np.concatenate(parts, 1).astype(np.float32), [float(g) for g in gam]


def kernel(**inputs):
    import numpy as _np
    import concourse.bacc as _bacc
    from concourse import mybir as _mybir
    from concourse.bass_utils import run_bass_kernel_spmd as _run

    nc = _bacc.Bacc("TRN2", target_bir_lowering=False, num_devices=1)
    arrays, args = {}, []
    given = {name: _np.ascontiguousarray(inputs[name]) for name in _INS}
    DEPTH, NS, HG, DKG, DV = given["state_gla"].shape
    HR, DKR = given["state_ret"].shape[2:4]
    B, TP, D = given["x_prompt"].shape
    DS = given["x_sample"].shape[1]
    given["consts"], given["masks"], gammas = _tables(_np, HR, DKR, TP, NS, DS)
    for name, a in given.items():
        arrays[f"in_{name}_dram"] = a
        args.append(nc.dram_tensor(f"in_{name}_dram", a.shape, _mybir.dt.from_np(a.dtype), kind="ExternalInput").ap())
    outs = [(B, TP, D), (NS, DS, D), (DEPTH, B, HG, DKG, DV), (DEPTH, B, HR, DKR, DV),
            (DEPTH, NS, HG, DKG, DV), (DEPTH, NS, HR, DKR, DV)]
    for i, shape in enumerate(outs):
        args.append(nc.dram_tensor(f"out_{i}_dram", shape, F32, kind="ExternalOutput").ap())
    trunk_kernel(nc, *args, gammas)
    r = _run(nc, [arrays], core_ids=[0])
    return tuple(r.results[0][f"out_{i}_dram"] for i in range(len(outs)))
```

```python
from contextlib import ExitStack

import concourse.bass as bass
from concourse import mybir

F32 = mybir.dt.float32
F32R = mybir.dt.float32r
U8 = mybir.dt.uint8
ALU = mybir.AluOpType
ACT = mybir.ActivationFunctionType
AX = mybir.AxisListType

P = 128
EPS = 1e-6
GATE_TEMP = 16.0
SPLIT_SLOTS = 4
UNITS = 4
UNIT_KT = 8
CH = 128
LEVELS = (64, 32, 16, 8, 4, 2, 1)
X_PARTS = 4


class Signal:

    def __init__(self, sem, per_layer):
        self.sem, self.per = sem, per_layer

    def at(self, l, i):
        return l * self.per + (i + 1)


def const_layout(HR, T, TS, NS):
    cols, at = {}, 0
    for name, n in (("ident", P), ("ones", P), ("eps", 1), ("cos", T), ("sin", T), ("decay_mask", HR * CH),
                    ("q_decay", HR * CH), ("k_decay", HR), ("k_decay_s", HR), ("decay_mask_s", HR * TS),
                    ("scan_keep", T), ("batch_mask", NS)):
        cols[name] = (at, at + n)
        at += n
    return cols, at


def trunk_kernel(nc, x_prompt, x_sample, state_gla, state_ret, norm_g, w1_gu, w1_down, w2_gu, w2_down,
                 w_in, w_a2, b_a, gn_gla, gn_ret, w_out, consts, masks,
                 y_prompt, y_sample, gla_p, ret_p, gla_s, ret_s, gammas):
    DEPTH, NS, HG, DKG, DV = state_gla.shape
    HR, DKR = state_ret.shape[2:4]
    TP, D = x_prompt.shape[1:]
    DS = x_sample.shape[1]
    TS = NS * DS
    T = TP + TS
    HALF = T // 2
    KD = D // P
    FF = w1_down.shape[1]
    KF = FF // P
    GR = w_a2.shape[1]
    NCH = TP // CH
    HA = HG + HR
    QT = HG * DKG // P
    NN = norm_g.shape[1]
    DOWN_KT = [(KF + UNITS - 1 - u) // UNITS for u in range(UNITS)]
    ALO_KT = [KD // UNITS] * UNITS
    FULL_KT = [KD] * UNITS
    cc, _ = const_layout(HR, T, TS, NS)
    V_GLA = DEPTH * NN * KD
    V_RET = V_GLA + DEPTH * HG
    V_BA = V_RET + DEPTH * HR
    NV = V_BA + DEPTH * QT

    GLA_V = 2 * HG * DKG
    GLA_G = GLA_V + HG * DV
    A_LO = GLA_G + HG * DV
    RET_Q = A_LO + GR
    RET_K = RET_Q + HR * DKR
    RET_V = RET_K + HR * DKR
    RET_G = RET_V + HR * DV
    IN_GROUPS = (("qk_a", 0), ("q_r", RET_Q), ("k_r", RET_K), ("v_a", GLA_V), ("v_r", RET_V),
                 ("g_a", GLA_G), ("g_r", RET_G))
    NIN = 1 + UNITS * len(IN_GROUPS)
    UP_GROUPS, DOWN_GROUPS, OUT_GROUPS = KF // 2, KD, KD // UNITS
    UP = (0, UP_GROUPS + DOWN_GROUPS + 1 + len(IN_GROUPS) + OUT_GROUPS)
    DOWN = (UP[0] + UP_GROUPS, UP[1] + UP_GROUPS)
    WIN = DOWN[0] + DOWN_GROUPS
    WOUT = WIN + 1 + len(IN_GROUPS)
    GROUPS = DOWN[1] + DOWN_GROUPS
    NL = len(LEVELS)
    SCAN_SLOT = 5
    STEPS = ["q", "k"] + list(range(NL))
    STEP_SLOTS = [6, 8, 10, 12, 14, 15, 16, 17, 18, 19]
    DIFF_SLOT = dict(zip(STEP_SLOTS, STEPS))
    PROD_SLOT = dict(zip(STEP_SLOTS[1:], STEPS))
    SCORE_SLOT = {t + 1: s for t, s in PROD_SLOT.items() if s not in ("q", "k")}
    SCORE_SLOT.update({21: NL, 22: NL + 1})
    TAKE_SLOT = {t + 1: n for t, n in SCORE_SLOT.items()}
    DIAG_SLOT = STEP_SLOTS[-1] + 1
    ROT0 = 1 + UNITS
    V_LAST = 5 * UNITS
    G0 = V_LAST + 1
    S = NCH
    IN_BANK = [0, 2, 4] + [2 * ((t + 1) % 2) for t in range(3, NIN)]
    DVE_SCALES = ((0, KD // 2), (0, KD // 2), (0, 1, 3, 5, 7))
    POOL_SCALES = tuple(tuple(k for k in range(KD) if k not in own) for own in DVE_SCALES)
    IN_SLOT_STEPS = {23: ("turn", 0), 24: ("scores", 0), 25: ("out", 0), 27: ("turn", 1), 28: ("scores", 1)}
    TAIL_STEPS = (("back", 0), ("out", 1), ("turn", 2), ("scores", 2), ("back", 1), ("turn", 3), ("out", 2),
                  ("scores", 3), ("back", 2), ("turn", S), ("out", 3), ("scores", S), ("out", S), ("back", 3),
                  ("rest of out", S), ("back", S))
    HALF_STEPS = {"out": ("squares", "root"), "scores": ("scores", "state")}
    TAIL_HALF_STEPS = (("back", 0), ("squares", 1), ("turn", 2), ("root", 1), ("scores", 2), ("back", 1), ("state", 2),
                       ("turn", 3), ("squares", 2), ("root", 2), ("scores", 3), ("back", 2), ("state", 3), ("turn", S),
                       ("scores", S), ("squares", 3), ("root", 3), ("back", 3), ("squares", S), ("root", S),
                       ("back", S))
    WARM_UP, WARM_POST, WARM_NORM, WARM_STEP = 7, (7, 0, 6), 2, 1
    assert NCH == 4
    BANK0 = (4, 4, 0, 4, 0)
    BACK_BANKS = ((2, 3), (5, 7), (1, 3), (5, 7), (1, 3))
    UPDATE_ORDER = tuple(range(HG, HA)) + tuple(range(HG))

    with ExitStack() as ctx:
        def sb(name, shape, dt=F32):
            return ctx.enter_context(nc.sbuf_tensor(name, shape, dt))

        def sem(name):
            return ctx.enter_context(nc.semaphore(name))

        def sig(name, per_layer):
            return Signal(sem(name), per_layer)

        def overlay(*tensors):
            out = []
            with ExitStack() as place:
                for name, shape, dt in tensors:
                    out.append(place.enter_context(nc.sbuf_tensor(name, shape, dt)))
            return out

        x = sb("x", [P, KD, T])
        raw = sb("raw", [P, UNITS, UNIT_KT, P])
        w_hi = sb("w_hi", [P, SPLIT_SLOTS, UNIT_KT // 2, P], F32R)
        w_lo = sb("w_lo", [P, SPLIT_SLOTS, UNIT_KT // 2, P], F32R)
        cst = sb("cst", [P, consts.shape[1]])
        msk = sb("msk", [P, masks.shape[1]], U8)
        rstd_pre = sb("rstd_pre", [P, T])
        acc = sb("acc", [P, T])
        sq = sb("sq", [P, 2, T])
        tmp = sb("tmp", [P, 2, T])
        vecs = sb("vecs", [P, NV])
        half_gain = sb("half_gain", [P, DEPTH * NN * KD])
        chunk_decay = sb("chunk_decay", [P, QT, NCH + NS])
        rms = sb("rms", [P, 2, HA])

        xs_hi, xs_lo = overlay(("xs_hi", [P, KD, T], F32R), ("xs_lo", [P, KD, T], F32R))
        y, = overlay(("y", [P, KD, T], F32))
        ret_state, gla_state, v_tok_s, k_tok_s = overlay(
            ("ret_state", [P, HR, NS, DV], F32), ("gla_state", [P, QT, NS, DV], F32),
            ("v_tok_s", [TS, HA, P], F32), ("k_tok_s", [TS, HR * P + QT * P], F32))
        sb("xs_place", [P, 2 * KD * T])

        h_hi, h_lo = overlay(("h_hi", [P, KF, T], F32R), ("h_lo", [P, KF, T], F32R))
        x_tok, vec_rows, mask_rows = overlay(("x_tok", [P, NCH + 1, D], F32), ("vec_rows", [P, P], F32),
                                             ("mask_rows", [P, masks.shape[1]], F32))
        y_tok, = overlay(("y_tok", [P, NCH + 1, D], F32))
        (qk_a, b_cum, e_buf, k_lvl, _, q_dec, k_dec, v_t, g_t, q_r, k_r, a_gla, a_gla_s, a_ret_s,
         w_a2_sb) = overlay(
            ("qk_a", [P, 2 * QT, T], F32), ("b_cum", [P, QT, T], F32), ("e_buf", [P, QT, T], F32),
            ("k_lvl", [P, QT, T], F32), ("spare", [P, QT, HALF], F32),
            ("q_dec", [P, QT, T], F32),
            ("k_dec", [P, QT, T], F32),
            ("v_t", [P, HA, T], F32),
            ("g_t", [P, HA, T], F32),
            ("q_r", [P, HR, T], F32), ("k_r", [P, HR, T], F32),
            ("a_gla", [P, 2, NCH, 2, CH], F32),
            ("a_gla_s", [TS, 2, 2, TS], F32), ("a_ret_s", [TS, HR, TS], F32),
            ("w_a2_sb", [GR, QT * P], F32))
        v_tok, k_tok, a_ret, s_gla, s_ret, o_tok = overlay(
            ("v_tok", [P, 2, HA, P], F32),
            ("k_tok", [P, HR * P + QT * P], F32),
            ("a_ret", [P, HR, CH], F32),
            ("s_gla", [P, 2, QT, DV], F32), ("s_ret", [P, 2, HR, DV], F32),
            ("o_tok", [P, HA, P], F32))
        _, y_out, o_lo, o_hi = overlay(("ahead_of_v_t", [P, 7 * QT * T + QT * HALF], F32), ("y_out", [P, KD, T], F32),
                                       ("o_lo", [P, HA, T], F32R), ("o_hi", [P, HA, T], F32R))
        assert KD == HA == 2 * HR
        _, x_sq = overlay(("ahead_of_g_t", [P, (7 * QT + HA) * T + QT * HALF], F32), ("x_sq", [P, KD, T], F32))
        _, q_lvl = overlay(("ahead_of_g_t2", [P, (7 * QT + HA) * T + QT * HALF], F32), ("q_lvl", [P, QT, 2, HALF], F32))
        sb("h_place", [P, 2 * KF * T])
        QW = NS * TS
        q_gla_s = acc[:, 0:QT * QW].rearrange("p (q t) -> p q t", t=QW)
        q_ret_s = v_tok[:, 0].rearrange("p h v -> p (h v)")[:, 0:HR * QW].rearrange("p (h t) -> p h t", t=QW)

        def v_by_batch(i):
            return v_tok[0:TS, (i + 1) % 2].rearrange("p h v -> p (h v)")[:, 0:NS * DV].rearrange("p (b v) -> p b v", b=NS)

        ps = ctx.enter_context(nc.psum_tensor("ps", [P, 8, 512], F32))

        def pair(i):
            return ps[:, 2 * i:2 * i + 2, 0:HALF]

        def halves(ap):
            return ap.rearrange("p (a t) -> p a t", a=2)

        def c(name, parts=P):
            a, b = cc[name]
            return cst[0:parts, a:b]

        ident, ones, eps = c("ident"), c("ones"), c("eps")
        cos, sin = c("cos"), c("sin")

        def gain(l, n, k):
            return vecs[:, bass.ds(l * (NN * KD) + (n * KD + k), 1)]

        def post_gain(l, q, k):
            table = vecs if q == 1 else half_gain
            return table[:, bass.ds(l * (NN * KD) + ((2 * q + 1) * KD + k), 1)]

        tables_loaded, x_loaded = sem("tables_loaded"), [sem(f"x_loaded{i}") for i in range(X_PARTS)]
        loaded, vec_turned, vec_ready = sem("loaded"), sem("vec_turned"), sem("vec_ready")
        raw_ready = [sem(f"raw_ready{i}") for i in range(UNITS)]
        units_issued, mask_begun, sample_begun = sem("units_issued"), sem("mask_begun"), sem("sample_begun")
        hi_split = sem("hi_split")
        split_ready = [sem(f"split_ready{i}") for i in range(SPLIT_SLOTS)]
        split_used = [sem(f"split_used{i}") for i in range(SPLIT_SLOTS)]
        x_turned = sem("x_turned")
        w_a2_loaded = sem("w_a2_loaded")
        xh_ready, xs_ready = sig("xh_ready", 3 * KD), sig("xs_ready", 3 * KD)
        xsq_ready, xsq_step, pre_sum = sig("xsq_ready", 3 * KD), sig("xsq_step", 3 * (KD - 1)), sig("pre_sum", 3)
        pre_log, pre_ready = sig("pre_log", 3), sig("pre_ready", 3)
        y_sq, y_read = sig("y_sq", 3 * KD), sig("y_read", 3 * KD)
        acc_step = sig("acc_step", 3 * (KD - 2))
        post_sum, post_log, post_ready = sig("post_sum", 3), sig("post_log", 3), sig("post_ready", 3)
        x_ready = sig("x_ready", 3 * KD)
        y_scaled = sig("y_scaled", sum(len(own) for own in DVE_SCALES))
        y_scaled_pool = sig("y_scaled_pool", sum(len(own) for own in POOL_SCALES))
        gate_scaled, up_scaled = sig("gate_scaled", 2 * KF), sig("up_scaled", 2 * KF)
        gate_silu, h_prod = sig("gate_silu", 2 * KF), sig("h_prod", 2 * KF)
        hh_ready, h_ready = sig("hh_ready", 2 * KF), sig("h_ready", 2 * KF)
        in_read = sig("in_read", NIN)
        z_ready, z_abs, z_min = sig("z_ready", 1), sig("z_abs", 1), sig("z_min", 1)
        z_exp, z_ln, log_gate, b_ready = sig("z_exp", 1), sig("z_ln", 1), sig("log_gate", 1), sig("b_ready", 1)
        swapped, rot_parts, rotated = sig("swapped", 2 * HR), sig("rot_parts", 2 * HR), sig("rotated", 2 * HR)
        silu_done, gates_ready = sig("silu_done", HA), sig("gates_ready", HA)
        diff_ready, exp_ready, prod_ready = sig("diff_ready", NL + 1), sig("exp_ready", NL + 2), sig("prod_ready", NL + 2)
        diag_prod = sig("diag_prod", 1)
        scores_ready, scores_taken, a_zeroed = sig("scores_ready", NL + 2), sig("scores_taken", NL + 2), sig("a_zeroed", 1)
        NSTEP = NCH + 1
        turned, v_tok_ready, k_tok_ready = sig("turned", NSTEP), sig("v_tok_ready", NSTEP), sig("k_tok_ready", NSTEP)
        qd_ready, q_zeroed, q_masked = sig("qd_ready", NCH - 1), sig("q_zeroed", 1), sig("q_masked", 1)
        ret_scores, a_ret_ready = sig("ret_scores", NSTEP), sig("a_ret_ready", NSTEP)
        state_delta, state_ready = sig("state_delta", NCH), sig("state_ready", NCH)
        o_ready, o_sq, o_ms = sig("o_ready", NSTEP), sig("o_sq", NSTEP), sig("o_ms", NSTEP)
        o_root, o_rms, o_normed = sig("o_root", NSTEP), sig("o_rms", NSTEP), sig("o_normed", NSTEP)
        o_turned, o_gated = sig("o_turned", NSTEP), sig("o_gated", NSTEP)
        v_masked, s_delta, s_updated = sig("v_masked", HA), sig("s_delta", HA), sig("s_updated", HA)
        states_stored, states_loaded = sem("states_stored"), sem("states_loaded")
        oh_ready, ol_ready = sig("oh_ready", HA), sig("ol_ready", HA)
        y_turned, y_copied, y_copied_dve = sem("y_turned"), sem("y_copied"), sem("y_copied_dve")
        stored = sem("stored")

        block = ctx.enter_context(nc.Block())

        def out_slot(h):
            return (h % 2, h // 2) if h < HG else ((h - HG) // 2, 2 + (h - HG) % 2)

        def wait(eng, signal, l, i):
            eng.wait_ge(signal.sem, signal.at(l, i))

        def split_slot(u, half):
            return 2 * (u % 2) + half

        def half_units(kt):
            return (0, 0, (kt + 1) // 2), (1, (kt + 1) // 2, kt // 2)

        def wait_unit(eng, g, u):
            eng.wait_ge(split_used[split_slot(u, 1)], 2 * g + (u // 2 + 2))

        def wait_in_tile(eng, l, t):
            j, u = ((t - 1) // UNITS + 1, (t - 1) % UNITS) if t else (0, UNITS - 1)
            wait_unit(eng, l * GROUPS + (WIN + j), u)

        def y_tile(q, k):
            return (y_out if q == 1 else y)[:, k, :]

        def nth_scale(table, q, k):
            return sum(len(own) for own in table[:q]) + table[q].index(k)

        def ahead_of_wait(eng):
            eng.wait_ge(loaded, LOADS)

        YD = KD // 2
        W = YD * P
        X0 = KD + 1
        STATE_DMAS = (2 + QT + HR) * 16
        STATE_LOADS = (QT + HR) * 16
        LOADS = 7 * 16

        @block.sync
        def _(sp):
            sp.dma_start(cst[:, 0:cc["cos"][0]], consts[:, 0:cc["cos"][0]]).then_inc(loaded, 16)
            sp.dma_start(mask_rows[:, :], masks).then_inc(loaded, 16)
            sp.dma_start(x_tok[0:TS, NCH, :], x_sample.rearrange("b t d -> (b t) d")).then_inc(loaded, 16)
            for row, v in ((0, norm_g.rearrange("l n (k p) -> (l n k) p", p=P)),
                           (V_GLA, gn_gla.rearrange("l (k p) -> (l k) p", p=P)),
                           (V_RET, gn_ret.rearrange("l (k p) -> (l k) p", p=P)),
                           (V_BA, b_a.rearrange("l (k p) -> (l k) p", p=P))):
                sp.dma_start(vec_rows[row:row + v.shape[0], :], v).then_inc(loaded, 16)
            for i in range(X_PARTS):
                cols = slice(i * D // X_PARTS, (i + 1) * D // X_PARTS)
                sp.dma_start(x_tok[:, 0:NCH, cols], x_prompt[0, :, cols].rearrange("(c p) d -> p c d", p=P))\
                    .then_inc(x_loaded[i], 16)

            def unit(g, u, rows, kt):
                sp.wait_ge(split_ready[split_slot(u, 1)], 2 * g + (u // 2 + 1))
                sp.sem_inc(units_issued, 1)
                sp.dma_start(raw[:, u, 0:kt, :], rows.rearrange("(k p) m -> p k m", p=P)).then_inc(raw_ready[u], 16)

            def k_parts(g, w, l, cols, kts):
                k0 = 0
                for u in range(UNITS):
                    unit(g, u, w[l, k0 * P:(k0 + kts[u]) * P, cols], kts[u])
                    k0 += kts[u]

            def ffn(l, f, w_gu, w_down):
                with sp.Fori(0, UP_GROUPS) as i:
                    for u in range(UNITS):
                        unit(l * GROUPS + UP[f] + i, u, w_gu[l, :, bass.ds(i * (2 * P) + (u // 2 * P + u % 2 * FF), P)], KD)
                with sp.Fori(0, DOWN_GROUPS) as m:
                    k_parts(l * GROUPS + DOWN[f] + m, w_down, l, bass.ds(m * P, P), DOWN_KT)

            with sp.Fori(0, DEPTH) as l:
                ffn(l, 0, w1_gu, w1_down)
                k_parts(l * GROUPS + WIN, w_in, l, slice(A_LO, A_LO + P), ALO_KT)
                for j, (_, col) in enumerate(IN_GROUPS):
                    for u in range(UNITS):
                        unit(l * GROUPS + (WIN + 1 + j), u, w_in[l, :, col + u * P:col + (u + 1) * P], KD)
                with sp.Fori(0, OUT_GROUPS) as j:
                    for u in range(UNITS):
                        unit(l * GROUPS + WOUT + j, u, w_out[l, :, bass.ds(j * (UNITS * P) + u * P, P)], KD)
                ffn(l, 1, w2_gu, w2_down)

            y_rows, y_parts = y_prompt[0].rearrange("(c p) d -> p c d", p=P), NCH // 2
            for sem_, n, dst, src in ((y_copied, NCH, y_rows[:, :, 0:W], y_tok[:, 0:NCH, 0:W]),
                                      (y_copied, NCH + y_parts, y_rows[:, 0:y_parts, W:2 * W], y_tok[:, 0:y_parts, W:2 * W]),
                                      (y_copied_dve, y_parts, y_rows[:, y_parts:NCH, W:2 * W],
                                       y_tok[:, y_parts:NCH, W:2 * W])):
                sp.wait_ge(sem_, n)
                sp.dma_start(dst, src).then_inc(stored, 16)
            sp.wait_ge(y_copied, NCH + y_parts + 1)
            sp.wait_ge(y_copied_dve, y_parts + 1)
            sp.dma_start(y_sample.rearrange("b t d -> (b t) d"), y_tok[0:TS, NCH, :]).then_inc(stored, 16)
            sp.wait_ge(stored, 4 * 16)

        @block.gpsimd
        def _(pool):
            for s in range(SPLIT_SLOTS):
                pool.sem_inc(split_ready[s], 2)
            pool.wait_ge(loaded, LOADS)

            def scale_y(l, q, ks):
                wait(pool, post_ready, l, q)
                for k in ks:
                    if k in POOL_SCALES[q]:
                        pool.tensor_tensor(y_tile(q, k), y_tile(q, k), acc[:, :], ALU.mult).then_inc(y_scaled_pool.sem, 1)

            UNIT_ORDER = tuple((u, half) for u in range(UNITS) for half in range(2))
            PAIR_ORDER = ((0, 0), (1, 0), (0, 1), (1, 1)) + UNIT_ORDER[4:]

            def group(g, kts, order=UNIT_ORDER, before_unit={}):
                for i, (u, half) in enumerate(order):
                    if half == 0:
                        if u in before_unit:
                            before_unit[u]()
                        pool.wait_ge(raw_ready[u], g * 16 + 16)
                    _, k0, n = half_units(kts[u])[half]
                    s = split_slot(u, half)
                    pool.wait_ge(split_used[s], 2 * g + (u // 2 + 1))
                    pool.tensor_tensor(w_hi[:, s, 0:n, :], raw[:, u, k0:k0 + n, :],
                                       ones.rearrange("p (k m) -> p k m", k=1).broadcast_to([P, n, P]),
                                       ALU.mult).then_inc(hi_split, 1)
                    pool.wait_ge(hi_split, g * (2 * UNITS) + (i + 1))
                    pool.tensor_tensor(w_lo[:, s, 0:n, :], raw[:, u, k0:k0 + n, :], w_hi[:, s, 0:n, :].bitcast(F32),
                                       ALU.subtract).then_inc(split_ready[s], 1)

            def mask_queries(l):
                pool.wait_ge(tables_loaded, 16)
                wait(pool, o_ready, l, NCH - 2)
                pool.sem_inc(mask_begun, 1)
                pool.memset(acc[:, :], 0.0)
                pool.memset(v_tok[:, 0], 0.0).then_inc(q_zeroed.sem, 1)
                wait(pool, q_zeroed, l, 0)
                q_decay = c("q_decay").rearrange("p (h b t) -> p h b t", h=HR, b=1)[:, :, :, 0:DS]
                for n, src, dst in ((QT, q_dec, q_gla_s), (HR, q_r, q_ret_s)):
                    for b0, nb in ((0, NS - 1), (NS - 1, 1)):
                        t0, at, step_ = TP + b0 * DS, b0 * (TS + DS), (TS + DS if nb > 1 else DS)
                        scale = q_decay if n == HR else ones[:, 0:n * DS].rearrange("p (h b t) -> p h b t", h=n, b=1)
                        o = pool.tensor_tensor(
                            dst[:, :, at:at + nb * step_].rearrange("p h (b t) -> p h b t", b=nb)[:, :, :, 0:DS],
                            src[:, :, t0:t0 + nb * DS].rearrange("p h (b t) -> p h b t", b=nb),
                            scale.broadcast_to([P, n, nb, DS]), ALU.mult)
                o.then_inc(q_masked.sem, 1)

            with pool.Fori(0, DEPTH) as l:
                for f in range(2):
                    group(l * GROUPS + UP[f], FULL_KT, PAIR_ORDER,
                          before_unit={2: lambda: scale_y(l, 1, range(KD))} if f == 1 else {})
                    with pool.Fori(1, UP_GROUPS) as i:
                        group(l * GROUPS + UP[f] + i, FULL_KT)
                    with pool.Fori(0, DOWN_GROUPS) as i:
                        group(l * GROUPS + DOWN[f] + i, DOWN_KT)
                    if f == 1:
                        scale_y(l, 2, range(KD))
                    if f == 0:
                        group(l * GROUPS + WIN, ALO_KT, before_unit={2: lambda: scale_y(l, 0, range(KD // 2)),
                                                                     3: lambda: scale_y(l, 0, range(KD // 2, KD))})
                        with pool.Fori(0, len(IN_GROUPS)) as i:
                            group(l * GROUPS + (WIN + 1) + i, FULL_KT)
                        mask_queries(l)
                        with pool.Fori(0, OUT_GROUPS) as i:
                            group(l * GROUPS + WOUT + i, FULL_KT)

        @block.tensor
        def _(pe):
            for s in range(SPLIT_SLOTS):
                pe.sem_inc(split_used[s], 1)

            def wait_split(g, u, half):
                pe.wait_ge(split_ready[split_slot(u, half)], 2 * g + (u // 2 + 3))

            def products(s, k, hi, lo, kx, bank, start, stop):
                for n, (w, v) in enumerate(((w_hi, hi), (w_hi, lo), (w_lo, hi))):
                    for a in range(2):
                        mm = pe.matmul(ps[:, bank + a, 0:HALF], w[:, s, k, :], v[:, kx, a * HALF:(a + 1) * HALF],
                                       start=(start and n == 0), stop=(stop and n == 2))
                return mm

            def unit(g, u, kt, hi, lo, k0, bank, first, last, before_k=None):
                for half, h0, n in half_units(kt):
                    s = split_slot(u, half)
                    wait_split(g, u, half)
                    for k in range(n):
                        if before_k:
                            before_k(k0 + h0 + k)
                        mm = products(s, k, hi, lo, k0 + h0 + k, bank, first and h0 + k == 0, last and h0 + k == kt - 1)
                    mm.then_inc(split_used[s], 1)

            def keep_clock_up(n):
                for _ in range(n):
                    pe.matmul(ps[:, 6, 0:2 * P], ones, cst[:, 0:2 * P], start=True, stop=True)

            def pre_stats(l, q):
                wait(pe, xsq_step, l, q * (KD - 1) + KD - 2)
                for a in range(2):
                    mm = pe.matmul(ps[:, 6 + a, 0:HALF], ones, x_sq[:, 0, a * HALF:(a + 1) * HALF], start=True, stop=True)
                mm.then_inc(pre_sum.sem, 1)

            def x_split(l, q):
                return lambda k: wait(pe, xs_ready, l, q * KD + k)

            def up_chunk(g, par):
                for j in range(2):
                    unit(g, 2 * par + j, KD, xs_hi, xs_lo, 0, 4 * par + 2 * j, True, True)

            def ffn(l, f):
                g0 = l * GROUPS + UP[f]
                keep_clock_up(WARM_UP)
                for half, k0, n in half_units(KD):
                    for j in range(2):
                        wait_split(g0, j, half)
                    for k in range(n):
                        wait(pe, xs_ready, l, 2 * f * KD + k0 + k)
                        for j in range(2):
                            mm = products(split_slot(j, half), k, xs_hi, xs_lo, k0 + k, 2 * j, k0 + k == 0,
                                          k0 + k == KD - 1)
                            if k == n - 1:
                                mm.then_inc(split_used[split_slot(j, half)], 1)
                unit(g0, 2, KD, xs_hi, xs_lo, 0, 4, True, True)
                pre_stats(l, 2 * f)
                wait(pe, pre_log, l, 2 * f)
                unit(g0, 3, KD, xs_hi, xs_lo, 0, 6, True, True)
                with pe.Fori(1, UP_GROUPS) as i:
                    for par in range(2):
                        pe.wait_ge(up_scaled.sem, l * up_scaled.per + i * 2 + (f * KF + par - 1))
                        up_chunk(g0 + i, par)
                wait(pe, up_scaled, l, f * KF + KF - 2)

                def down_tile(m, par, before_k=None):
                    k0 = 0
                    for u in range(UNITS):
                        unit(l * GROUPS + DOWN[f] + m, u, DOWN_KT[u], h_hi, h_lo, k0, 2 * par, u == 0, u == UNITS - 1,
                             before_k=before_k)
                        k0 += DOWN_KT[u]

                down_tile(0, 0, before_k=lambda k: wait(pe, h_ready, l, f * KF + k))
                down_tile(1, 1)
                with pe.Fori(1, DOWN_GROUPS // 2) as i:
                    for par in range(2):
                        pe.wait_ge(y_read.sem, l * y_read.per + i * 2 + (2 * f * KD + par - 1))
                        down_tile(i * 2 + par, par)
                post_stats(l, 2 * f)

            def post_stats(l, q):
                wait(pe, acc_step, l, q * (KD - 2) + KD - 3)
                for a in range(2):
                    pe.matmul(ps[:, 4 + a, 0:HALF], ones, acc[:, a * HALF:(a + 1) * HALF], start=True, stop=False)
                wait(pe, y_sq, l, q * KD + KD - 1)
                for a in range(2):
                    mm = pe.matmul(ps[:, 4 + a, 0:HALF], ones, sq[:, (KD - 1) % 2, a * HALF:(a + 1) * HALF], start=False,
                                   stop=True)
                mm.then_inc(post_sum.sem, 1)
                keep_clock_up(WARM_POST[q])

            def in_tile(l, t):
                j, u = (t - 1) // UNITS, (t - 1) % UNITS
                if t >= 3:
                    wait(pe, in_read, l, t - 2 if t >= 5 else t - 3)
                unit(l * GROUPS + (WIN + 1 + j), u, KD, xs_hi, xs_lo, 0, IN_BANK[t], True, True)

            def gate_logits(l):
                wait(pe, in_read, l, 2)
                pe.wait_ge(w_a2_loaded, l * 16 + 16)
                wait(pe, pre_log, l, 1)
                for q in range(QT):
                    for a in range(2):
                        mm = pe.matmul(ps[:, 4 + 2 * q + a, 0:HALF], w_a2_sb[:, q * P:(q + 1) * P],
                                       tmp[0:GR, 0, a * HALF:(a + 1) * HALF], start=True, stop=True)
                mm.then_inc(z_ready.sem, 1)

            def level_scores(l, n):
                m = LEVELS[n]
                wait(pe, prod_ready, l, 2 + n)
                if n == 0:
                    wait(pe, z_min, l, 0)
                if n >= 2:
                    wait(pe, scores_taken, l, n - 1 if LEVELS[n - 1] < DS else n - 2)
                for c_ in range(NCH):
                    for hh in range(QT):
                        at = (c_ % 2 * QT + hh) * CH
                        mm = pe.matmul(ps[:, 4 + 2 * (n % 2) + c_ // 2, at:at + CH].rearrange("p (a t) -> p a t", a=2),
                                       k_lvl[:, hh, c_ * CH:(c_ + 1) * CH],
                                       q_lvl[:, hh, :, c_ * CH // 2:(c_ + 1) * CH // 2], start=True, stop=True)
                if m < DS:
                    wait(pe, scores_taken, l, n - 1)
                    pe.sem_inc(sample_begun, 1)
                    for hh in range(QT):
                        mm = pe.matmul(ps[0:TS, 4 + 2 * ((n + 1) % 2), hh * TS:(hh + 1) * TS].rearrange("p (a t) -> p a t", a=2),
                                       k_lvl[:, hh, TP:T], q_lvl[:, hh, :, TP // 2:HALF], start=True, stop=True)
                mm.then_inc(scores_ready.sem, 1)

            def diagonal_scores(l, sample):
                wait(pe, diag_prod, l, 0)
                wait(pe, scores_taken, l, NL if sample else NL - 1)
                pe.sem_inc(sample_begun, 1)
                t0, t1, n = (TP, T, TS) if sample else (0, TP, P)
                for p in range(2):
                    for hh in range(QT):
                        mm = pe.matmul(ps[0:n, 4 + 2 * p + hh, 0:t1 - t0], ones[p * DKG:(p + 1) * DKG, 0:n],
                                       e_buf[p * DKG:(p + 1) * DKG, hh, t0:t1], start=True, stop=True)
                mm.then_inc(scores_ready.sem, 1)

            def turn(l, c_):
                t0, n, b0 = c_ * CH, (TS if c_ == S else CH), BANK0[c_]
                if c_ == 0:
                    wait(pe, in_read, l, V_LAST)
                    wait(pe, rotated, l, 2 * HR - 1)
                    wait(pe, scores_taken, l, NL + 1)
                elif c_ == 1:
                    wait(pe, o_normed, l, 0)
                elif c_ == 2:
                    wait(pe, in_read, l, NIN - 1)
                    wait(pe, o_gated, l, 0)
                else:
                    wait(pe, o_normed, l, c_ - 2)
                    wait(pe, o_gated, l, c_ - 2)
                for h in range(HA):
                    pe.transpose(ps[0:n, b0 + h // 4, h % 4 * P:(h % 4 + 1) * P], v_t[:, h, t0:t0 + n], ident)
                for h in range(HR):
                    pe.transpose(ps[0:n, b0 + 2, h * P:(h + 1) * P], k_r[:, h, t0:t0 + n], ident)
                for q in range(QT):
                    mm = pe.transpose(ps[0:n, b0 + 3, q * P:(q + 1) * P], k_dec[:, q, t0:t0 + n], ident)
                mm.then_inc(turned.sem, 1)

            def scores(l, c_):
                t0, n, b0 = c_ * CH, (TS if c_ == S else CH), BANK0[c_]
                wait(pe, v_tok_ready, l, c_)
                wait(pe, k_tok_ready, l, c_)
                for h in range(HR):
                    mm = pe.matmul(ps[0:n, b0, h * n:(h + 1) * n], k_r[:, h, t0:t0 + n], q_r[:, h, t0:t0 + n],
                                   start=True, stop=True)
                mm.then_inc(ret_scores.sem, 1)
                if c_ == S:
                    return
                for h in range(HR):
                    pe.matmul(ps[:, b0 + 1, h * DV:(h + 1) * DV], k_tok[:, h * P:(h + 1) * P], v_tok[:, c_ % 2, HG + h, :],
                              start=True, stop=True)
                for h in range(HG):
                    q, p = h // 2, h % 2
                    at = (HR + q) * P + p * DKG
                    mm = pe.matmul(ps[p * DKG:(p + 1) * DKG, b0 + 3, (QT + q) * DV:(QT + q + 1) * DV],
                                   k_tok[:, at:at + DKG], v_tok[:, c_ % 2, h, :], start=True, stop=True)
                mm.then_inc(state_delta.sem, 1)

            def out(l, c_):
                if c_ == S:
                    out_sample(l, 0)
                    return
                t0, b0 = c_ * CH, BANK0[c_]
                wait(pe, a_ret_ready, l, c_)
                if c_:
                    wait(pe, state_ready, l, c_ - 1)
                    wait(pe, qd_ready, l, c_ - 1)
                for h in range(HG):
                    q, p = h // 2, h % 2
                    a, i = out_slot(h)
                    o = ps[:, b0 + 2 * a, i * DV:(i + 1) * DV]
                    pe.matmul(o, a_gla[:, p, c_, q, :], v_tok[:, c_ % 2, h, :], start=True, stop=(c_ == 0))
                    if c_:
                        pe.matmul(o, q_dec[p * DKG:(p + 1) * DKG, q, t0:t0 + CH],
                                  s_gla[p * DKG:(p + 1) * DKG, (c_ - 1) % 2, q, :], start=False, stop=True)
                for h in range(HR):
                    a, i = out_slot(HG + h)
                    o = ps[:, b0 + 2 * a, i * DV:(i + 1) * DV]
                    mm = pe.matmul(o, a_ret[:, h, :], v_tok[:, c_ % 2, HG + h, :], start=True, stop=(c_ == 0))
                    if c_:
                        mm = pe.matmul(o, q_r[:, h, t0:t0 + CH], s_ret[:, (c_ - 1) % 2, h, :], start=False, stop=True)
                mm.then_inc(o_ready.sem, 1)

            def back(l, c_):
                n = TS if c_ == S else CH
                ahead_of_wait(pe)
                wait(pe, o_normed, l, c_)
                if c_ == 0:
                    wait(pe, in_read, l, NIN - 1)
                elif c_ < S:
                    wait(pe, state_ready, l, c_)
                for h in range(HA):
                    a, i = out_slot(h)
                    mm = pe.transpose(ps[:, BACK_BANKS[c_][h // 4], h % 4 * n:(h % 4 + 1) * n],
                                      o_tok[0:n, 4 * a + i, :], ident[0:n, 0:n])
                mm.then_inc(o_turned.sem, 1)

            def out_sample(l, part):
                if part == 0:
                    wait_for_sample(l)
                for h in range(part * HA // 2, (part + 1) * HA // 2):
                    q, p = h // 2, h % 2
                    a, i = out_slot(h)
                    o = ps[0:TS, BANK0[S] + 2 * a, i * DV:(i + 1) * DV]
                    pe.matmul(o, a_gla_s[:, p, q, :] if h < HG else a_ret_s[:, h - HG, :], v_tok_s[:, h, :], start=True,
                              stop=False)
                    for b in range(NS):
                        if h < HG:
                            rows = slice(p * DKG, (p + 1) * DKG)
                            queries, state = q_gla_s[rows, q, b * TS:(b + 1) * TS], gla_state[rows, q, b, :]
                        else:
                            queries, state = q_ret_s[:, h - HG, b * TS:(b + 1) * TS], ret_state[:, h - HG, b, :]
                        mm = pe.matmul(o, queries, state, start=False, stop=(b == NS - 1))
                if part:
                    mm.then_inc(o_ready.sem, 1)

            def wait_for_sample(l):
                wait(pe, a_ret_ready, l, S)
                wait(pe, q_masked, l, 0)
                pe.wait_ge(states_loaded, l * STATE_LOADS + STATE_LOADS)
                pe.sem_inc(sample_begun, 1)

            def sample_delta(l, i):
                h = UPDATE_ORDER[i]
                wait(pe, v_masked, l, i)
                if i >= 2:
                    wait(pe, s_updated, l, i - 2)
                else:
                    wait(pe, o_gated, l, NCH - 1)
                if h < HG:
                    p = h % 2
                    keys, r0, r1 = k_tok_s[:, HR * P + h * DKG:HR * P + (h + 1) * DKG], p * DKG, (p + 1) * DKG
                else:
                    keys, r0, r1 = k_tok_s[:, (h - HG) * P:(h - HG + 1) * P], 0, P
                for a in range(2):
                    mm = pe.matmul(ps[r0:r1, 4 + 2 * (i % 2) + a, :], keys,
                                   v_by_batch(i)[:, a * NS // 2:(a + 1) * NS // 2, :], start=True, stop=True)
                mm.then_inc(s_delta.sem, 1)

            def step(l, kind, c_):
                if kind == "turn":
                    turn(l, c_)
                elif kind == "scores":
                    scores(l, c_)
                elif kind == "out":
                    out(l, c_)
                elif kind == "back":
                    back(l, c_)
                else:
                    out_sample(l, 1)
                    sample_delta(l, 0)
                    keep_clock_up(WARM_NORM)

            def out_projection(l):
                for m in range(KD):
                    if m >= 2:
                        wait(pe, y_read, l, KD + m - 2)
                    unit(l * GROUPS + (WOUT + m // UNITS), m % UNITS, KD, o_hi, o_lo, 0, 2 * (m % 2), True, True,
                         before_k=(lambda k: wait(pe, ol_ready, l, k)) if m == 0 else None)
                    if m:
                        sample_delta(l, m)
                wait(pe, s_updated, l, HA - 1)
                post_stats(l, 1)

            pe.wait_ge(loaded, LOADS)
            pe.transpose(ps[:, 5, 0:NV], vec_rows[0:NV, :], ident[0:NV, 0:NV]).then_inc(vec_turned, 1)
            for d in range(KD):
                mm = pe.transpose(ps[:, 4, d * TS:(d + 1) * TS], x_tok[0:TS, NCH, d * P:(d + 1) * P], ident[0:TS, 0:TS])
            mm.then_inc(x_turned, 1)
            for d in range(KD):
                if d % (KD // X_PARTS) == 0:
                    pe.wait_ge(x_loaded[d // (KD // X_PARTS)], 16)
                if d >= 4:
                    pe.wait_ge(x_ready.sem, d - 2)
                for c_ in range(NCH):
                    mm = pe.transpose(ps[:, d % 4, c_ * P:(c_ + 1) * P], x_tok[:, c_, d * P:(d + 1) * P], ident)
                mm.then_inc(x_turned, 1)

            with pe.Fori(0, DEPTH) as l:
                ffn(l, 0)
                k0 = 0
                for u in range(UNITS):
                    unit(l * GROUPS + WIN, u, ALO_KT[u], xs_hi, xs_lo, k0, 0, u == 0, u == UNITS - 1,
                         before_k=x_split(l, 1))
                    k0 += ALO_KT[u]
                for t in range(1, NIN):
                    in_tile(l, t)
                    if t == 1:
                        pre_stats(l, 1)
                    if t == UNITS:
                        gate_logits(l)
                    if t in SCORE_SLOT:
                        n = SCORE_SLOT[t]
                        if n < NL:
                            level_scores(l, n)
                        else:
                            diagonal_scores(l, sample=(n > NL))
                    if t in IN_SLOT_STEPS:
                        step(l, *IN_SLOT_STEPS[t])
                for kind, c_ in TAIL_STEPS:
                    if (kind, c_) in (("back", 2), ("turn", S)):
                        keep_clock_up(WARM_STEP)
                    step(l, kind, c_)
                out_projection(l)
                ffn(l, 1)

            for d in range(KD):
                pe.wait_ge(x_ready.sem, DEPTH * x_ready.per + (X0 - KD + d + 1))
                for c_ in range(NCH):
                    mm = pe.transpose(ps[:, 2 * c_ + d // YD, d % YD * P:(d % YD + 1) * P],
                                      x[:, d, c_ * P:(c_ + 1) * P], ident)
                if d % YD == YD - 1:
                    mm.then_inc(y_turned, 1)
            pe.wait_ge(y_copied, 2)
            for d in range(KD):
                mm = pe.transpose(ps[0:TS, 2 * (d // YD), d % YD * P:(d % YD + 1) * P], x[:, d, TP:T], ident)
            mm.then_inc(y_turned, 1)

        @block.scalar
        def _(act):
            def pre_tile(l, q, k, done):
                act.wait_ge(x_ready.sem, done)
                act.activation(xs_hi[:, k, :], x[:, k, :], ACT.Copy, scale=gain(l, 2 * q, k)).then_inc(xh_ready.sem, 1)
                act.activation(x_sq[:, k, :], x[:, k, :], ACT.Square).then_inc(xsq_ready.sem, 1)

            def inverse_root(l, q, dst, bank_pair, log_sig, ready_sig):
                act.activation(halves(dst), pair(bank_pair), ACT.Ln, bias=eps, scale=1.0 / D).then_inc(log_sig.sem, 1)
                wait(act, log_sig, l, q)
                act.activation(dst, dst, ACT.Exp, scale=-0.5).then_inc(ready_sig.sem, 1)

            def pre_norm(l, q):
                for k in range(KD):
                    pre_tile(l, q, k, l * x_ready.per + (X0 + (q - 1) * KD + k + 1))
                wait(act, pre_sum, l, q)
                inverse_root(l, q, rstd_pre[:, :], 3, pre_log, pre_ready)

            def up(l, f):
                with act.Fori(0, KF) as c_:
                    at = l * gate_scaled.per + c_ + (f * KF + 1)
                    act.wait_ge(gate_scaled.sem, at)
                    act.activation(tmp[:, 0, :], tmp[:, 0, :], ACT.Silu).then_inc(gate_silu.sem, 1)
                    act.wait_ge(h_prod.sem, at)
                    act.activation(h_hi[:, bass.ds(c_, 1), :], tmp[:, 0:1, :], ACT.Copy).then_inc(hh_ready.sem, 1)

            def post_norm(l, q, g0, last_unit, after_tile=None):
                for m in range(KD):
                    wait_unit(act, *last_unit(g0, m))
                    if m >= 2:
                        wait(act, acc_step, l, q * (KD - 2) + max(m - 2, 1) - 1)
                    act.activation(halves(sq[:, m % 2, :]), pair(m % 2), ACT.Square).then_inc(y_sq.sem, 1)
                    act.activation(halves(y_tile(q, m)), pair(m % 2), ACT.Copy).then_inc(y_read.sem, 1)
                    if after_tile and m:
                        after_tile(l, m - 1)
                if after_tile:
                    after_tile(l, KD - 1)
                wait(act, post_sum, l, q)
                inverse_root(l, q, acc[:, :], 2, post_log, post_ready)

            down_unit = lambda g0, m: (g0 + m, UNITS - 1)
            out_unit = lambda g0, m: (g0 + m // UNITS, m % UNITS)

            def swap_halves(l, t):
                n = t - ROT0
                src, hd = (q_r if n < HR else k_r)[:, n % HR, :], DKR // 2
                wait(act, in_read, l, t)
                if n:
                    wait(act, rotated, l, n - 1)
                act.activation(tmp[0:hd, 1, :], src[hd:2 * hd, :], ACT.Copy)
                act.activation(tmp[hd:2 * hd, 1, :], src[0:hd, :], ACT.Copy).then_inc(swapped.sem, 1)

            def act_step(l, kind, c_):
                n, b0 = TS if c_ == S else CH, BANK0[c_]
                if kind == "turn":
                    wait(act, turned, l, c_)
                    if 0 < c_ < S:
                        wait(act, state_delta, l, c_ - 1)
                    if 2 <= c_ < S:
                        wait(act, o_ready, l, c_ - 2)
                    vt, kt = (v_tok_s, k_tok_s) if c_ == S else (v_tok[:, c_ % 2], k_tok)
                    for i in range(2):
                        act.activation(vt[0:n, 4 * i:4 * i + 4, :],
                                       ps[0:n, b0 + i, :].rearrange("p (h v) -> p h v", v=DV), ACT.Copy)
                    act.activation(kt[0:n, HR * P:(HR + QT) * P], ps[0:n, b0 + 3, 0:QT * P], ACT.Copy)\
                        .then_inc(v_tok_ready.sem, 1)
                elif kind == "squares":
                    wait(act, o_ready, l, c_)
                    for a in range(2):
                        o = act.activation(sq[0:n, a, 0:4 * DV], ps[0:n, b0 + 2 * a, :], ACT.Square)
                    o.then_inc(o_sq.sem, 1)
                elif kind == "root":
                    wait(act, o_ms, l, c_)
                    act.activation(rms[0:n, 1, :], rms[0:n, 0, :], ACT.Sqrt, bias=eps[0:n], scale=1.0 / DV)\
                        .then_inc(o_root.sem, 1)
                if kind == "root" and c_ == NCH - 1:
                    wait(act, state_ready, l, c_)
                    act.dma_start(gla_p[l, 0].rearrange("(q p) k v -> (p k) q v", p=2), s_gla[:, c_ % 2, :, :])\
                        .then_inc(states_stored, 16)
                    act.dma_start(ret_p[l, 0].rearrange("h k v -> k h v"), s_ret[:, c_ % 2, :, :])\
                        .then_inc(states_stored, 16)

            def store_sample_state(l, i):
                h = UPDATE_ORDER[i]
                if h >= HG:
                    wait(act, s_updated, l, i)
                    act.dma_start(ret_s[l, :, h - HG].rearrange("b k v -> k b v"), ret_state[:, h - HG, :, :])\
                        .then_inc(states_stored, 16)
                elif h % 2:
                    wait(act, s_updated, l, i)
                    act.dma_start(gla_s[l, :, h - 1:h + 1].rearrange("b p k v -> (p k) b v"),
                                  gla_state[:, h // 2, :, :]).then_inc(states_stored, 16)

            act.wait_ge(vec_turned, 1)
            act.activation(vecs[:, :], ps[:, 5, 0:NV], ACT.Copy).then_inc(vec_ready, 1)
            act.wait_ge(vec_ready, 1)
            act.activation(half_gain[:, :], vecs[:, 0:DEPTH * NN * KD], ACT.Copy, scale=0.5).then_inc(vec_ready, 1)
            act.wait_ge(raw_ready[1], 16)
            act.dma_start(cst[:, cc["cos"][0]:], consts[:, cc["cos"][0]:]).then_inc(tables_loaded, 16)
            with act.Fori(0, DEPTH) as l:
                pre_norm(l, 0)
                up(l, 0)
                post_norm(l, 0, l * GROUPS + DOWN[0], down_unit)
                act.dma_start(w_a2_sb[:, :], w_a2[l]).then_inc(w_a2_loaded, 16)
                pre_norm(l, 1)
                wait(act, z_ready, l, 0)
                for q in range(QT):
                    o = act.activation(halves(e_buf[:, q, :]), pair(2 + q), ACT.Abs,
                                       bias=vecs[:, bass.ds(l * QT + (V_BA + q), 1)])
                o.then_inc(z_abs.sem, 1)
                wait(act, z_abs, l, 0)
                act.activation(e_buf[:, :, :], e_buf[:, :, :], ACT.Exp, scale=-1.0).then_inc(z_exp.sem, 1)
                wait(act, z_exp, l, 0)
                act.activation(e_buf[:, :, :], e_buf[:, :, :], ACT.Ln, bias=ones[:, 0:1]).then_inc(z_ln.sem, 1)
                for t in range(SCAN_SLOT, NIN):
                    if ROT0 <= t < ROT0 + 2 * HR:
                        swap_halves(l, t)
                    if t in DIFF_SLOT:
                        s = DIFF_SLOT[t]
                        if s == "q":
                            wait(act, b_ready, l, 0)
                            act.activation(e_buf[:, :, :], b_cum[:, :, :], ACT.Exp, scale=1.0 / GATE_TEMP)\
                                .then_inc(exp_ready.sem, 1)
                        else:
                            n = 0 if s == "k" else 1 + s
                            wait(act, diff_ready, l, n)
                            act.activation(e_buf[:, :, :], e_buf[:, :, :], ACT.Exp, scale=1.0 / GATE_TEMP)\
                                .then_inc(exp_ready.sem, 1)
                    if t >= G0:
                        wait(act, in_read, l, t)
                        act.activation(g_t[:, t - G0, :], g_t[:, t - G0, :], ACT.Silu).then_inc(silu_done.sem, 1)
                    if t in IN_SLOT_STEPS:
                        kind, c_ = IN_SLOT_STEPS[t]
                        for part in HALF_STEPS.get(kind, (kind,)):
                            act_step(l, part, c_)
                wait(act, in_read, l, NIN - 1)
                for h in range(HR):
                    act.dma_start(ret_state[:, h, :, :], state_ret[l, :, h].rearrange("b k v -> k b v"))\
                        .then_inc(states_loaded, 16)
                for q in range(QT):
                    act.dma_start(gla_state[:, q, :, :], state_gla[l, :, 2 * q:2 * q + 2]
                                  .rearrange("b p k v -> (p k) b v")).then_inc(states_loaded, 16)
                for kind, c_ in TAIL_HALF_STEPS:
                    act_step(l, kind, c_)
                wait(act, o_gated, l, S)
                for h in range(HA):
                    act.activation(o_hi[:, h, :], v_t[:, h, :], ACT.Copy).then_inc(oh_ready.sem, 1)
                post_norm(l, 1, l * GROUPS + WOUT, out_unit, after_tile=store_sample_state)
                act.wait_ge(states_stored, l * STATE_DMAS + STATE_DMAS)
                pre_norm(l, 2)
                up(l, 1)
                post_norm(l, 2, l * GROUPS + DOWN[1], down_unit)

            act.wait_ge(y_turned, 1)
            for c_ in range(NCH):
                act.activation(y_tok[:, c_, 0:W], ps[:, 2 * c_, :], ACT.Copy).then_inc(y_copied, 1)
            act.wait_ge(y_turned, 2)
            for c_ in range(NCH // 2):
                act.activation(y_tok[:, c_, W:2 * W], ps[:, 2 * c_ + 1, :], ACT.Copy).then_inc(y_copied, 1)
            act.wait_ge(y_turned, 3)
            act.activation(y_tok[0:TS, NCH, 0:W], ps[0:TS, 0, :], ACT.Copy).then_inc(y_copied, 1)
            act.wait_ge(states_stored, DEPTH * STATE_DMAS)

        @block.vector
        def _(dve):
            def pre_low(l, q, k):
                wait(dve, xh_ready, l, q * KD + k)
                dve.scalar_tensor_tensor(out=xs_lo[:, k, :], in0=x[:, k, :], scalar=gain(l, 2 * q, k),
                                         in1=xs_hi[:, k, :].bitcast(F32), op0=ALU.mult, op1=ALU.subtract)\
                   .then_inc(xs_ready.sem, 1)

            def add_x_squares(l, q):
                for k in range(1, KD):
                    wait(dve, xsq_ready, l, q * KD + k)
                    if k > 1:
                        wait(dve, xsq_step, l, q * (KD - 1) + k - 2)
                    dve.tensor_tensor(x_sq[:, 0, :], x_sq[:, 0, :], x_sq[:, k, :], ALU.add).then_inc(xsq_step.sem, 1)

            def up(l, f):
                with dve.Fori(0, UP_GROUPS) as i:
                    for par in range(2):
                        at = l * gate_scaled.per + i * 2 + (f * KF + par + 1)
                        wait(dve, pre_ready, l, 2 * f)
                        wait_unit(dve, l * GROUPS + UP[f] + i, 2 * par + 1)
                        dve.tensor_tensor(halves(tmp[:, 0, :]), pair(2 * par), halves(rstd_pre[:, :]), ALU.mult)\
                           .then_inc(gate_scaled.sem, 1)
                        dve.tensor_tensor(halves(tmp[:, 1, :]), pair(2 * par + 1), halves(rstd_pre[:, :]), ALU.mult)\
                           .then_inc(up_scaled.sem, 1)
                        dve.wait_ge(gate_silu.sem, at)
                        dve.wait_ge(up_scaled.sem, at)
                        dve.tensor_tensor(tmp[:, 0, :], tmp[:, 0, :], tmp[:, 1, :], ALU.mult).then_inc(h_prod.sem, 1)
                        dve.wait_ge(hh_ready.sem, at)
                        tile = bass.ds(i * 2 + par, 1)
                        dve.tensor_tensor(h_lo[:, tile, :], tmp[:, 0:1, :], h_hi[:, tile, :].bitcast(F32), ALU.subtract)\
                           .then_inc(h_ready.sem, 1)
                        dve.wait_ge(h_ready.sem, at)

            def add_squares(l, q, m):
                if m == 0 or m == KD - 1:
                    return
                wait(dve, y_sq, l, q * KD + m)
                if m > 1:
                    wait(dve, acc_step, l, q * (KD - 2) + m - 2)
                dve.tensor_tensor(acc[:, :], sq[:, 0, :] if m == 1 else acc[:, :], sq[:, m % 2, :], ALU.add)\
                   .then_inc(acc_step.sem, 1)

            def residual(l, q, pre=None):
                wait(dve, post_ready, l, q)
                for k in range(KD):
                    yk, own = y_tile(q, k), k in DVE_SCALES[q]
                    for n in ((0, 1) if k == 0 else (k + 1,)):
                        if n in DVE_SCALES[q]:
                            dve.tensor_tensor(y_tile(q, n), y_tile(q, n), acc[:, :], ALU.mult).then_inc(y_scaled.sem, 1)
                    if pre is not None and k >= 2:
                        pre_low(l, pre, k - 2)
                    if own:
                        wait(dve, y_scaled, l, nth_scale(DVE_SCALES, q, k))
                    else:
                        wait(dve, y_scaled_pool, l, nth_scale(POOL_SCALES, q, k))
                    dve.scalar_tensor_tensor(out=x[:, k, :], in0=yk, scalar=post_gain(l, q, k), in1=x[:, k, :],
                                             op0=ALU.mult, op1=ALU.add).then_inc(x_ready.sem, 1)
                if pre is not None:
                    pre_low(l, pre, KD - 2)
                    pre_low(l, pre, KD - 1)
                    add_x_squares(l, pre)

            def take_tile(l, t):
                wait_in_tile(dve, l, t)
                src, r = pair(IN_BANK[t] // 2), halves(rstd_pre[:, :])
                if t == 0:
                    dve.tensor_tensor(halves(tmp[0:GR, 0, :]), src[0:GR], r[0:GR], ALU.mult).then_inc(in_read.sem, 1)
                    return
                kind, i = IN_GROUPS[(t - 1) // UNITS][0], (t - 1) % UNITS
                out = {"qk_a": qk_a, "v_a": v_t, "q_r": q_r, "k_r": k_r, "v_r": v_t, "g_a": g_t, "g_r": g_t}[kind]
                i += {"v_r": HG, "g_r": HG}.get(kind, 0)
                scale = DKG ** -0.5 if kind == "qk_a" and i < QT else 1.0
                dve.scalar_tensor_tensor(out=halves(out[:, i, :]), in0=src, scalar=scale, in1=r, op0=ALU.mult,
                                         op1=ALU.mult).then_inc(in_read.sem, 1)

            def rotate(l, n):
                buf, scale = (q_r, 1.0) if n < HR else (k_r, DKR ** -0.5)
                wait(dve, swapped, l, n)
                dve.scalar_tensor_tensor(out=tmp[:, 1, :], in0=tmp[:, 1, :], scalar=scale, in1=sin, op0=ALU.mult,
                                         op1=ALU.mult)
                dve.scalar_tensor_tensor(out=buf[:, n % HR, :], in0=buf[:, n % HR, :], scalar=scale, in1=cos,
                                         op0=ALU.mult, op1=ALU.mult).then_inc(rot_parts.sem, 1)
                wait(dve, rot_parts, l, n)
                dve.tensor_tensor(buf[:, n % HR, :], buf[:, n % HR, :], tmp[:, 1, :], ALU.add).then_inc(rotated.sem, 1)

            def by_block(buf, w, m):
                return buf[:, :, 0:w].rearrange("p q (n h m) -> p q n h m", h=2, m=m)

            def exponents(l, s):
                if s == "q":
                    return
                wait(dve, prod_ready, l, STEPS.index(s) - 1)
                if s == "k":
                    for t0, w, m in ((0, TP, CH), (TP, TS, DS)):
                        b = b_cum[:, :, t0:t0 + w].rearrange("p q (n m) -> p q n m", m=m)
                        e = e_buf[:, :, t0:t0 + w].rearrange("p q (n m) -> p q n m", m=m)
                        o = dve.tensor_tensor(e, b[:, :, :, m - 1:m].broadcast_to([P, QT, w // m, m]), b, ALU.subtract)
                    o.then_inc(diff_ready.sem, 1)
                    return
                m = LEVELS[s]
                w = T if m < DS else TP
                b, e = by_block(b_cum, w, m), by_block(e_buf, w, m)
                ref = b[:, :, :, 0, m - 1:m].broadcast_to([P, QT, w // (2 * m), m])
                dve.tensor_tensor(e[:, :, :, 0, :], ref, b[:, :, :, 0, :], ALU.subtract)
                dve.tensor_tensor(e[:, :, :, 1, :], b[:, :, :, 1, :], ref, ALU.subtract).then_inc(diff_ready.sem, 1)

            def products(l, s):
                queries, keys = qk_a[:, 0:QT, :], qk_a[:, QT:2 * QT, :]
                j = STEPS.index(s)
                wait(dve, exp_ready, l, j)
                if s == "q":
                    dve.tensor_copy(chunk_decay[:, :, 0:NCH], e_buf[:, :, CH - 1:TP:CH])
                    dve.tensor_copy(chunk_decay[:, :, NCH:NCH + NS], e_buf[:, :, TP + DS - 1:T:DS])
                    dve.tensor_tensor(q_dec[:, :, :], queries, e_buf[:, :, :], ALU.mult).then_inc(prod_ready.sem, 1)
                elif s == "k":
                    dve.tensor_tensor(k_dec[:, :, :], keys, e_buf[:, :, :], ALU.mult).then_inc(prod_ready.sem, 1)
                else:
                    m = LEVELS[s]
                    w = T if m < DS else TP
                    if s:
                        wait(dve, scores_ready, l, s - 1)
                    else:
                        wait(dve, a_zeroed, l, 0)
                    dve.tensor_tensor(k_lvl[:, :, 0:w], keys[:, :, 0:w], e_buf[:, :, 0:w], ALU.mult)
                    for p in range(2):
                        rows = slice(p * DKG, (p + 1) * DKG)
                        o = dve.tensor_tensor(q_lvl[rows, :, p, 0:w // 2].rearrange("p q (n m) -> p q n m", m=m),
                                              by_block(queries, w, m)[rows, :, :, 1, :],
                                              by_block(e_buf, w, m)[rows, :, :, 1, :], ALU.mult)
                    o.then_inc(prod_ready.sem, 1)

            def take_scores(l, n):
                ahead_of_wait(dve)
                wait(dve, scores_ready, l, n)
                if n == 0:
                    wait(dve, a_zeroed, l, 0)
                for p in range(2):
                    if n < NL:
                        m = LEVELS[n]
                        mask = msk[:, n * (CH // 2):(n + 1) * (CH // 2)]
                        nb = CH // (2 * m)
                        o = dve.copy_predicated(
                            a_gla[:, p].rearrange("p c x (n h m) -> p (c x) n h m", h=2, m=m)[:, :, :, 1, :],
                            mask.rearrange("p (x n m) -> p x n m", x=1, m=m).broadcast_to([P, 2 * NCH, nb, m]),
                            ps[:, 4 + 2 * (n % 2):6 + 2 * (n % 2), :]
                            .rearrange("p a (x h t) -> p (a x) h t", h=2, t=CH // 2)[:, :, p, :]
                            .rearrange("p x (n m) -> p x n m", m=m))
                        if m < DS:
                            nb = TS // (2 * m)
                            o = dve.copy_predicated(
                                a_gla_s[:, p].rearrange("p x (n h m) -> p x n h m", h=2, m=m)[:, :, :, 1, :],
                                mask[0:TS, 0:TS // 2].rearrange("p (x n m) -> p x n m", x=1, m=m)
                                .broadcast_to([TS, 2, nb, m]),
                                ps[0:TS, 4 + 2 * ((n + 1) % 2), 0:QT * TS]
                                .rearrange("p (x h t) -> p x h t", h=2, t=TS // 2)[:, :, p, :]
                                .rearrange("p x (n m) -> p x n m", m=m))
                    elif n == NL:
                        mask = msk[:, NL * (CH // 2):NL * (CH // 2) + CH].rearrange("p (x t) -> p x t", x=1)
                        for hh in range(QT):
                            o = dve.copy_predicated(a_gla[:, p, :, hh, :], mask.broadcast_to([P, NCH, CH]),
                                                    ps[:, 4 + 2 * p + hh, :].rearrange("p (c t) -> p c t", t=CH))
                    else:
                        mask = msk[0:TS, NL * (CH // 2):NL * (CH // 2) + TS].rearrange("p (x t) -> p x t", x=1)
                        o = dve.copy_predicated(a_gla_s[:, p], mask.broadcast_to([TS, 2, TS]),
                                                ps[0:TS, 4 + 2 * p:6 + 2 * p, 0:TS])
                o.then_inc(scores_taken.sem, 1)

            def turn_keys(l, c_):
                wait(dve, turned, l, c_)
                if 0 < c_ < S:
                    wait(dve, state_delta, l, c_ - 1)
                if c_ == S:
                    wait(dve, v_tok_ready, l, c_)
                n, b0 = TS if c_ == S else CH, BANK0[c_]
                kt, decay = (k_tok_s, c("k_decay_s", TS)) if c_ == S else (k_tok, c("k_decay"))
                o = dve.tensor_tensor(kt[0:n, 0:HR * P].rearrange("p (h k) -> p h k", h=HR),
                                      ps[0:n, b0 + 2, :].rearrange("p (h k) -> p h k", h=HR),
                                      decay.rearrange("p (h k) -> p h k", k=1).broadcast_to([n, HR, P]), ALU.mult)
                o.then_inc(k_tok_ready.sem, 1)

            def decay_scores(l, c_):
                t0 = c_ * CH
                wait(dve, ret_scores, l, c_)
                if c_ == S:
                    dve.tensor_tensor(a_ret_s.rearrange("p h t -> p (h t)"), ps[0:TS, 0, 0:HR * TS],
                                      c("decay_mask_s", TS), ALU.mult).then_inc(a_ret_ready.sem, 1)
                else:
                    if c_:
                        wait(dve, o_ready, l, c_ - 1)
                    dve.tensor_tensor(a_ret.rearrange("p h t -> p (h t)"), ps[:, BANK0[c_], :], c("decay_mask"),
                                      ALU.mult).then_inc(a_ret_ready.sem, 1)
                if 0 < c_ < S:
                    q = q_r[:, :, t0:t0 + CH]
                    dve.tensor_tensor(q, q, c("q_decay").rearrange("p (h t) -> p h t", h=HR), ALU.mult)\
                       .then_inc(qd_ready.sem, 1)

            def update_states(l, c_):
                wait(dve, state_delta, l, c_)
                new, old = c_ % 2, (c_ - 1) % 2
                if c_ >= 1:
                    wait(dve, o_ready, l, c_ - 1)
                    wait(dve, state_ready, l, c_ - 1)
                b0 = BANK0[c_]
                for q in range(QT):
                    delta = ps[:, b0 + 3, (QT + q) * DV:(QT + q + 1) * DV]
                    if c_ == 0:
                        dve.tensor_copy(s_gla[:, new, q, :], delta)
                    else:
                        dve.scalar_tensor_tensor(out=s_gla[:, new, q, :], in0=s_gla[:, old, q, :],
                                                 scalar=chunk_decay[:, q, c_:c_ + 1], in1=delta, op0=ALU.mult, op1=ALU.add)
                for h in range(HR):
                    delta = ps[:, b0 + 1, h * DV:(h + 1) * DV]
                    if c_ == 0:
                        o = dve.tensor_copy(s_ret[:, new, h, :], delta)
                    else:
                        o = dve.scalar_tensor_tensor(out=s_ret[:, new, h, :], in0=s_ret[:, old, h, :],
                                                     scalar=gammas[h] ** CH, in1=delta, op0=ALU.mult, op1=ALU.add)
                o.then_inc(state_ready.sem, 1)

            def sum_squares(l, c_):
                n = TS if c_ == S else CH
                wait(dve, o_sq, l, c_)
                if c_:
                    wait(dve, o_normed, l, c_ - 1)
                dve.tensor_reduce(rms[0:n, 0, :], sq[0:n, :, 0:4 * DV].rearrange("p a (h v) -> p a h v", v=DV), AX.X,
                                  ALU.add).then_inc(o_ms.sem, 1)

            def norm_outputs(l, c_):
                n = TS if c_ == S else CH
                wait(dve, o_root, l, c_)
                dve.reciprocal(rms[0:n, 0, :], rms[0:n, 1, :]).then_inc(o_rms.sem, 1)
                wait(dve, o_rms, l, c_)
                if c_:
                    wait(dve, o_turned, l, c_ - 1)
                for a in range(2):
                    o = dve.tensor_tensor(o_tok[0:n, 4 * a:4 * a + 4, :],
                                          ps[0:n, BANK0[c_] + 2 * a, :].rearrange("p (h v) -> p h v", v=DV),
                                          rms[0:n, 0, 4 * a:4 * a + 4].rearrange("p (h v) -> p h v", v=1)
                                          .broadcast_to([n, 4, DV]), ALU.mult)
                o.then_inc(o_normed.sem, 1)

            def gate_outputs(l, c_):
                t0, n = c_ * CH, TS if c_ == S else CH
                wait(dve, o_turned, l, c_)
                wait(dve, gates_ready, l, HA - 1)
                for a in range(2):
                    o = dve.tensor_tensor(v_t[:, 4 * a:4 * a + 4, t0:t0 + n],
                                          ps[:, BACK_BANKS[c_][a], 0:4 * n].rearrange("p (h t) -> p h t", t=n),
                                          g_t[:, 4 * a:4 * a + 4, t0:t0 + n], ALU.mult)
                o.then_inc(o_gated.sem, 1)

            def head_gain(l, h):
                wait(dve, silu_done, l, h)
                v = bass.ds(l * HG + ((V_GLA if h < HG else V_RET - HG) + h), 1)
                dve.tensor_scalar(g_t[:, h, :], g_t[:, h, :], vecs[:, v], None, ALU.mult).then_inc(gates_ready.sem, 1)

            def mask_values(l, i):
                h = UPDATE_ORDER[i]
                if i >= 2:
                    wait(dve, s_delta, l, i - 2)
                dve.tensor_tensor(v_by_batch(i), v_tok_s[:, h:h + 1, :].broadcast_to([TS, NS, DV]),
                                  c("batch_mask", TS).rearrange("p (b x) -> p b x", x=1).broadcast_to([TS, NS, DV]),
                                  ALU.mult).then_inc(v_masked.sem, 1)

            def update_sample_state(l, i):
                h = UPDATE_ORDER[i]
                wait(dve, s_delta, l, i)
                delta = ps[:, 4 + 2 * (i % 2):6 + 2 * (i % 2), :]
                if h < HG:
                    rows, q = slice(h % 2 * DKG, (h % 2 + 1) * DKG), h // 2
                    for b in range(NS):
                        o = dve.scalar_tensor_tensor(out=gla_state[rows, q, b, :], in0=gla_state[rows, q, b, :],
                                                     scalar=chunk_decay[rows, q, NCH + b:NCH + b + 1],
                                                     in1=delta[rows, b // 4, b % 4 * DV:(b % 4 + 1) * DV],
                                                     op0=ALU.mult, op1=ALU.add)
                else:
                    s = ret_state[:, h - HG, :, :].rearrange("p (a b) v -> p a (b v)", a=2)
                    o = dve.scalar_tensor_tensor(out=s, in0=s, scalar=gammas[h - HG] ** DS, in1=delta, op0=ALU.mult,
                                                 op1=ALU.add)
                o.then_inc(s_updated.sem, 1)

            def dve_step(l, kind, c_):
                if kind == "turn":
                    turn_keys(l, c_)
                elif kind == "scores":
                    decay_scores(l, c_)
                elif kind == "state":
                    update_states(l, c_)
                elif kind == "squares":
                    sum_squares(l, c_)
                elif kind == "root":
                    norm_outputs(l, c_)
                else:
                    gate_outputs(l, c_)

            dve.wait_ge(loaded, LOADS)
            dve.wait_ge(x_turned, 1)
            dve.tensor_copy(x[:, :, TP:T], ps[:, 4, 0:KD * TS].rearrange("p (d t) -> p d t", t=TS)).then_inc(x_ready.sem, 1)
            for d in range(KD):
                dve.wait_ge(x_turned, d + 2)
                dve.tensor_copy(x[:, d, 0:TP], ps[:, d % 4, :]).then_inc(x_ready.sem, 1)
            dve.tensor_copy(msk[:, :], mask_rows[:, :])
            with dve.Fori(0, DEPTH) as l:
                for k in range(KD):
                    pre_low(l, 0, k)
                add_x_squares(l, 0)
                up(l, 0)
                for m in range(KD):
                    add_squares(l, 0, m)
                residual(l, 0, pre=1)
                for t in range(NIN):
                    if t == 0:
                        wait(dve, pre_ready, l, 1)
                        dve.wait_ge(tables_loaded, 16)
                    if t in TAKE_SLOT:
                        take_scores(l, TAKE_SLOT[t])
                    take_tile(l, t)
                    if t == UNITS:
                        wait(dve, z_abs, l, 0)
                        for q in range(QT):
                            o = dve.tensor_scalar(halves(k_lvl[:, q, :]), pair(2 + q), vecs[:, bass.ds(l * QT + (V_BA + q), 1)], 0.0,
                                                  ALU.add, ALU.min)
                        o.then_inc(z_min.sem, 1)
                        dve.memset(a_gla.rearrange("p a c x t -> p (a c x t)"), 0.0)
                        dve.memset(q_lvl.rearrange("p q a t -> p (q a t)"), 0.0)
                        dve.memset(a_gla_s.rearrange("p a x t -> p (a x t)"), 0.0).then_inc(a_zeroed.sem, 1)
                    if t == SCAN_SLOT:
                        wait(dve, z_ln, l, 0)
                        wait(dve, z_min, l, 0)
                        dve.tensor_tensor(k_lvl[:, :, :], k_lvl[:, :, :], e_buf[:, :, :], ALU.subtract)\
                           .then_inc(log_gate.sem, 1)
                        wait(dve, log_gate, l, 0)
                        for q in range(QT):
                            o = dve.tensor_tensor_scan(b_cum[:, q, :], c("scan_keep"), k_lvl[:, q, :], 0.0, ALU.mult, ALU.add)
                        o.then_inc(b_ready.sem, 1)
                    if ROT0 < t <= ROT0 + 2 * HR:
                        rotate(l, t - 1 - ROT0)
                    if t in PROD_SLOT:
                        products(l, PROD_SLOT[t])
                    if t in DIFF_SLOT:
                        exponents(l, DIFF_SLOT[t])
                    if t == DIAG_SLOT:
                        wait(dve, prod_ready, l, NL + 1)
                        dve.tensor_tensor(e_buf[:, :, :], qk_a[:, 0:QT, :], qk_a[:, QT:2 * QT, :], ALU.mult)\
                           .then_inc(diag_prod.sem, 1)
                    if G0 < t:
                        head_gain(l, t - 1 - G0)
                    if t in IN_SLOT_STEPS:
                        kind, c_ = IN_SLOT_STEPS[t]
                        for part in HALF_STEPS.get(kind, (kind,)):
                            dve_step(l, part, c_)
                head_gain(l, HA - 1)
                for kind, c_ in TAIL_HALF_STEPS:
                    if (kind, c_) == ("squares", S):
                        mask_values(l, 0)
                    dve_step(l, kind, c_)
                for h in range(HA):
                    wait(dve, oh_ready, l, h)
                    dve.tensor_tensor(o_lo[:, h, :], v_t[:, h, :], o_hi[:, h, :].bitcast(F32), ALU.subtract)\
                       .then_inc(ol_ready.sem, 1)
                mask_values(l, 1)
                for m in range(KD):
                    add_squares(l, 1, m)
                    update_sample_state(l, m)
                    if m + 2 < HA:
                        mask_values(l, m + 2)
                residual(l, 1, pre=2)
                up(l, 1)
                for m in range(KD):
                    add_squares(l, 2, m)
                residual(l, 2)

            dve.wait_ge(y_turned, 2)
            for c_ in range(NCH // 2, NCH):
                dve.tensor_copy(y_tok[:, c_, W:2 * W], ps[:, 2 * c_ + 1, :]).then_inc(y_copied_dve, 1)
            dve.wait_ge(y_turned, 3)
            dve.tensor_copy(y_tok[0:TS, NCH, W:2 * W], ps[0:TS, 2, :]).then_inc(y_copied_dve, 1)


_INS = ["x_prompt", "x_sample", "state_gla", "state_ret", "norm_g", "w1_gu", "w1_down", "w2_gu", "w2_down",
        "w_in", "w_a2", "b_a", "gn_gla", "gn_ret", "w_out"]
PAST_LEN = 4096
ROPE_BASE = 10000.0


def _tables(np, HR, DKR, TP, NS, DS):
    TS = NS * DS
    T = TP + TS
    cols, n = const_layout(HR, T, TS, NS)
    tab = np.zeros((P, n), np.float32)

    def put(name, a):
        lo, hi = cols[name]
        tab[0:a.shape[0], lo:hi] = a.reshape(a.shape[0], hi - lo)

    put("ident", np.eye(P))
    put("ones", np.ones((P, P)))
    half = DKR // 2
    freq = np.float32(ROPE_BASE) ** (-np.arange(half, dtype=np.float32) / np.float32(half))
    pos = np.concatenate([np.arange(TP), np.tile(PAST_LEN + np.arange(DS), NS)]).astype(np.float32)
    ang = (freq[:, None] * pos[None, :]).astype(np.float32).astype(np.float64)
    put("cos", np.concatenate([np.cos(ang), np.cos(ang)]))
    put("sin", np.concatenate([-np.sin(ang), np.sin(ang)]))
    gam = 1.0 - 2.0 ** (-5.0 - np.arange(HR))
    i = np.arange(CH)
    d = i[None, :] - i[:, None]
    put("decay_mask", np.stack([np.where(d >= 0, g ** np.maximum(d, 0), 0.0) for g in gam], 1))
    put("q_decay", np.broadcast_to(np.stack([g ** (i + 1) for g in gam])[None], (P, HR, CH)))
    put("k_decay", np.stack([g ** (CH - 1 - i) for g in gam], 1))
    j = np.arange(TS)
    put("k_decay_s", np.stack([g ** (DS - 1 - j % DS) for g in gam], 1))
    d = j[None, :] - j[:, None]
    same = j[None, :] // DS == j[:, None] // DS
    put("decay_mask_s", np.stack([np.where(same & (d >= 0), g ** np.maximum(d, 0), 0.0) for g in gam], 1))
    keep = np.ones((P, T))
    keep[:, 0:TP:CH] = 0.0
    keep[:, TP::DS] = 0.0
    put("scan_keep", keep)
    put("batch_mask", (j[:, None] // DS == np.arange(NS)[None, :]).astype(np.float32))
    put("eps", np.full((P, 1), EPS))
    parts = []
    t = np.arange(CH // 2)
    for m in LEVELS:
        parts.append((i[:, None] // (2 * m) == t[None, :] // m) & (i[:, None] % (2 * m) < m))
    parts.append(np.eye(CH, dtype=bool))
    return tab, np.concatenate(parts, 1).astype(np.float32), [float(g) for g in gam]


def kernel(**inputs):
    import numpy as _np
    import concourse.bacc as _bacc
    from concourse import mybir as _mybir
    from concourse.bass_utils import run_bass_kernel_spmd as _run

    nc = _bacc.Bacc("TRN2", target_bir_lowering=False, num_devices=1)
    arrays, args = {}, []
    given = {name: _np.ascontiguousarray(inputs[name]) for name in _INS}
    DEPTH, NS, HG, DKG, DV = given["state_gla"].shape
    HR, DKR = given["state_ret"].shape[2:4]
    B, TP, D = given["x_prompt"].shape
    DS = given["x_sample"].shape[1]
    given["consts"], given["masks"], gammas = _tables(_np, HR, DKR, TP, NS, DS)
    for name, a in given.items():
        arrays[f"in_{name}_dram"] = a
        args.append(nc.dram_tensor(f"in_{name}_dram", a.shape, _mybir.dt.from_np(a.dtype), kind="ExternalInput").ap())
    outs = [(B, TP, D), (NS, DS, D), (DEPTH, B, HG, DKG, DV), (DEPTH, B, HR, DKR, DV),
            (DEPTH, NS, HG, DKG, DV), (DEPTH, NS, HR, DKR, DV)]
    for i, shape in enumerate(outs):
        args.append(nc.dram_tensor(f"out_{i}_dram", shape, F32, kind="ExternalOutput").ap())
    trunk_kernel(nc, *args, gammas)
    r = _run(nc, [arrays], core_ids=[0])
    return tuple(r.results[0][f"out_{i}_dram"] for i in range(len(outs)))
```
